# Optimizing a Trainium2 kernel written in Bass

```python
import math
import jax, jax.numpy as jnp
from jax import lax
import numpy as np

'''One inference step of a hybrid decoder trunk (DEPTH layers).

Per layer (post-norm, DeepNorm residual scaling, adaLN conditioning):
  h   = x * (1 + scale1(c)) + shift1(c)
  one combined projection h @ w_in -> [q | k | v | u | gate_att | gate_ssm]
  branch A: stick-breaking attention (8 heads x 128, strictly causal, no softmax, no positions),
            beta = sigmoid(q.k / sqrt(d) + b_head)
  branch B: S5 diagonal complex SSM (64 groups x 16 channels, 64-dim complex state per group), D skip, GELU, GLU
  merged = sigmoid(gate_att) * (A @ w_att_br) + sigmoid(gate_ssm) * (B @ w_ssm_br)
  x = LN(alpha * x + (1 + gate1(c)) * (merged @ w_out))
  h2 = x * (1 + scale2(c)) + shift2(c)
  ConvFFN: up-projection -> causal depthwise conv (width 3) -> GELU-gated product -> down-projection
  x = LN(alpha * x + (1 + gate2(c)) * ffn)

Inputs: x_prompt (BATCH, SEQ, D_MODEL); x_sample (DEC_BATCH, DEC_SEQ, D_MODEL);
  cache_k, cache_v (DEPTH, N_PHYS, PAGE_SIZE, ATT_HEADS, HEAD_DIM) paged K/V pool;
  state_ssm_re, state_ssm_im (DEPTH, DEC_BATCH, SSM_GROUPS, SSM_STATE);
  state_conv (DEPTH, DEC_BATCH, CONV_W - 1, 2 * D_FF); page_table (DEC_BATCH, N_PAGES) int32;
  c_prompt (BATCH, D_MODEL); c_sample (DEC_BATCH, D_MODEL); weights with a leading DEPTH axis.

Returns (y_prompt, y_sample, k_prompt, v_prompt, ssm_re_prompt, ssm_im_prompt, conv_prompt,
         k_sample, v_sample, ssm_re_sample, ssm_im_sample, conv_sample):
  y_prompt (BATCH, SEQ, D_MODEL); y_sample (DEC_BATCH, DEC_SEQ, D_MODEL)
  k_prompt, v_prompt (DEPTH, BATCH, SEQ, ATT_HEADS, HEAD_DIM)   new K/V rows
  ssm_re_prompt, ssm_im_prompt (DEPTH, BATCH, SSM_GROUPS, SSM_STATE)   final SSM state
  conv_prompt (DEPTH, BATCH, CONV_W - 1, 2 * D_FF)   last up-projected rows
  k_sample, v_sample (DEPTH, DEC_BATCH, DEC_SEQ, ATT_HEADS, HEAD_DIM)
  ssm_re_sample, ssm_im_sample (DEPTH, DEC_BATCH, SSM_GROUPS, SSM_STATE)
  conv_sample (DEPTH, DEC_BATCH, CONV_W - 1, 2 * D_FF)
'''

D_MODEL = 2048
BATCH = 1
SEQ = 256
DEPTH = 1
DEC_BATCH = 8
DEC_SEQ = 8
PAST_LEN = 1024
PAGE_SIZE = 128

ATT_HEADS = 8
HEAD_DIM = 128
ATT_W = ATT_HEADS * HEAD_DIM
SSM_W = D_MODEL - ATT_W
SSM_GROUP = 16
SSM_GROUPS = SSM_W // SSM_GROUP
SSM_STATE = 64
D_FF = 5632
CONV_W = 3
Q_BLOCK = 128
N_MOD = 6
IN_COLS = 3 * ATT_W + SSM_W + 2 * D_MODEL
DN_ALPHA = (2.0 * DEPTH) ** 0.25
DN_BETA = (8.0 * DEPTH) ** -0.25
LN_EPS = 1e-5
SB_BIAS_LO = -7.0
SB_BIAS_HI = -5.0

kernel_name = 'stick_breaking_s5_hybrid_step'

def _layernorm(x, g, b):
    xf = x.astype(jnp.float32)
    mu = jnp.mean(xf, axis=-1, keepdims=True)
    var = jnp.mean(jnp.square(xf - mu), axis=-1, keepdims=True)
    y = (xf - mu) * lax.rsqrt(var + LN_EPS) * g.astype(jnp.float32) + b.astype(jnp.float32)
    return y.astype(x.dtype)

def _stick_breaking(q, k, v, bias, n_ctx):
    tq = q.shape[1]
    scale = HEAD_DIM ** -0.5
    b_h = bias.astype(jnp.float32)[None, :, None, None]
    outs = []
    for start in range(0, tq, Q_BLOCK):
        end = min(start + Q_BLOCK, tq)
        nk = n_ctx + end
        z = jnp.einsum('bqhd,bkhd->bhqk', q[:, start:end], k[:, :nk]).astype(jnp.float32) * scale + b_h
        q_pos = n_ctx + jnp.arange(start, end)
        k_pos = jnp.arange(nk)
        causal = k_pos[None, :] < q_pos[:, None]
        log_1m = jnp.where(causal, jax.nn.log_sigmoid(-z), 0.0)
        later = lax.cumsum(log_1m, axis=3, reverse=True) - log_1m
        w = jnp.where(causal, jnp.exp(jax.nn.log_sigmoid(z) + later), 0.0)
        outs.append(jnp.einsum('bhqk,bkhd->bqhd', w.astype(v.dtype), v[:, :nk]))
    return jnp.concatenate(outs, axis=1)

def _s5(u, h0, a_re, a_im, log_dt, b_re, b_im, c_re, c_im, d_skip):
    bsz, t, _ = u.shape
    uf = u.astype(jnp.float32).reshape(bsz, t, SSM_GROUPS, SSM_GROUP)
    lam = lax.complex(a_re.astype(jnp.float32), a_im.astype(jnp.float32))
    dt = jnp.exp(log_dt.astype(jnp.float32))[:, None]
    lam_bar = jnp.exp(lam * dt)
    b_c = lax.complex(b_re.astype(jnp.float32), b_im.astype(jnp.float32))
    b_bar = ((lam_bar - 1.0) / lam)[..., None] * b_c
    c_c = lax.complex(c_re.astype(jnp.float32), c_im.astype(jnp.float32))
    bu = jnp.einsum('btgn,gpn->btgp', uf, b_bar)
    a = jnp.broadcast_to(lam_bar, bu.shape)

    def combine(e1, e2):
        a1, x1 = e1
        a2, x2 = e2
        return a1 * a2, a2 * x1 + x2

    a_cum, h = lax.associative_scan(combine, (a, bu), axis=1)
    h = h + a_cum * h0[:, None]
    y = jnp.einsum('btgp,gnp->btgn', h, c_c).real
    y = y + d_skip.astype(jnp.float32).reshape(SSM_GROUPS, SSM_GROUP) * uf
    return y.reshape(bsz, t, SSM_W).astype(u.dtype), h[:, -1]

def _block(x, c, past_k, past_v, ssm_h0, conv_buf, lp):
    bsz, t, _ = x.shape
    mod = jax.nn.silu(c) @ lp['w_ada'] + lp['b_ada']
    sh1, sc1, g1, sh2, sc2, g2 = jnp.split(mod[:, None, :], N_MOD, axis=-1)

    h = x * (1.0 + sc1) + sh1
    cuts = [ATT_W, 2 * ATT_W, 3 * ATT_W, 3 * ATT_W + SSM_W, 3 * ATT_W + SSM_W + D_MODEL]
    q, k, v, u, ga, gb = jnp.split(h @ lp['w_in'], cuts, axis=-1)
    q = q.reshape(bsz, t, ATT_HEADS, HEAD_DIM)
    k = k.reshape(bsz, t, ATT_HEADS, HEAD_DIM)
    v = v.reshape(bsz, t, ATT_HEADS, HEAD_DIM)
    if past_k is None:
        n_ctx, k_all, v_all = 0, k, v
    else:
        n_ctx = past_k.shape[1]
        k_all = jnp.concatenate([past_k.astype(k.dtype), k], axis=1)
        v_all = jnp.concatenate([past_v.astype(v.dtype), v], axis=1)
    att = _stick_breaking(q, k_all, v_all, lp['sb_bias'], n_ctx).reshape(bsz, t, ATT_W)

    y_s, h_last = _s5(u, ssm_h0, lp['ssm_a_re'], lp['ssm_a_im'], lp['ssm_log_dt'],
                      lp['ssm_b_re'], lp['ssm_b_im'], lp['ssm_c_re'], lp['ssm_c_im'], lp['ssm_d'])
    y_s = jax.nn.gelu(y_s)
    y_s = y_s * jax.nn.sigmoid(y_s @ lp['w_glu'] + lp['b_glu'])

    merged = jax.nn.sigmoid(ga) * (att @ lp['w_att_br']) + jax.nn.sigmoid(gb) * (y_s @ lp['w_ssm_br'])
    x = _layernorm(DN_ALPHA * x + (1.0 + g1) * (merged @ lp['w_out']), lp['ln1_g'], lp['ln1_b'])

    h2 = x * (1.0 + sc2) + sh2
    up = h2 @ lp['w_up']
    ext = jnp.concatenate([conv_buf.astype(up.dtype), up], axis=1)
    conv = lp['conv_b']
    for i in range(CONV_W):
        conv = conv + lp['conv_w'][i] * ext[:, i:i + t]
    val, gate = jnp.split(conv, 2, axis=-1)
    f = (jax.nn.gelu(gate) * val) @ lp['w_down']
    x = _layernorm(DN_ALPHA * x + (1.0 + g2) * f, lp['ln2_g'], lp['ln2_b'])
    return x, k, v, h_last.real, h_last.imag, ext[:, t:]

def setup_inputs(seed: int = 0) -> dict:
    key = jax.random.key(seed)
    ks = jax.random.split(key, 40)
    f32 = jnp.float32
    n_pages = PAST_LEN // PAGE_SIZE
    n_phys = (DEC_BATCH * n_pages * 5) // 4
    L, D, F = DEPTH, D_MODEL, D_FF

    def nrm(k, shape, s):
        return jax.random.normal(k, shape, f32) * s

    page_table = jax.random.permutation(ks[7], n_phys)[:DEC_BATCH * n_pages]
    page_table = page_table.reshape(DEC_BATCH, n_pages).astype(jnp.int32)
    a_im0 = jnp.pi * jnp.arange(SSM_STATE, dtype=f32)
    return {
        'x_prompt': nrm(ks[0], (BATCH, SEQ, D), 1.0),
        'x_sample': nrm(ks[1], (DEC_BATCH, DEC_SEQ, D), 1.0),
        'cache_k': nrm(ks[2], (L, n_phys, PAGE_SIZE, ATT_HEADS, HEAD_DIM), 1.0),
        'cache_v': nrm(ks[3], (L, n_phys, PAGE_SIZE, ATT_HEADS, HEAD_DIM), 1.0),
        'state_ssm_re': nrm(ks[4], (L, DEC_BATCH, SSM_GROUPS, SSM_STATE), 0.1),
        'state_ssm_im': nrm(ks[5], (L, DEC_BATCH, SSM_GROUPS, SSM_STATE), 0.1),
        'state_conv': nrm(ks[6], (L, DEC_BATCH, CONV_W - 1, 2 * F), 1.0),
        'page_table': page_table,
        'c_prompt': nrm(ks[8], (BATCH, D), 1.0),
        'c_sample': nrm(ks[9], (DEC_BATCH, D), 1.0),
        'w_ada': nrm(ks[10], (L, D, N_MOD * D), 0.2 * D ** -0.5),
        'b_ada': nrm(ks[11], (L, N_MOD * D), 0.02),
        'w_in': nrm(ks[12], (L, D, IN_COLS), D ** -0.5),
        'w_att_br': nrm(ks[13], (L, ATT_W, D), ATT_W ** -0.5),
        'w_ssm_br': nrm(ks[14], (L, SSM_W, D), SSM_W ** -0.5),
        'w_out': nrm(ks[15], (L, D, D), DN_BETA * D ** -0.5),
        'sb_bias': jax.random.uniform(ks[34], (L, ATT_HEADS), f32, SB_BIAS_LO, SB_BIAS_HI),
        'ssm_a_re': -0.5 + nrm(ks[16], (L, SSM_GROUPS, SSM_STATE), 0.01),
        'ssm_a_im': a_im0 + nrm(ks[17], (L, SSM_GROUPS, SSM_STATE), 0.01),
        'ssm_log_dt': jax.random.uniform(ks[18], (L, SSM_GROUPS), f32, math.log(1e-3), math.log(1e-1)),
        'ssm_b_re': nrm(ks[19], (L, SSM_GROUPS, SSM_STATE, SSM_GROUP), (2.0 * SSM_GROUP) ** -0.5),
        'ssm_b_im': nrm(ks[20], (L, SSM_GROUPS, SSM_STATE, SSM_GROUP), (2.0 * SSM_GROUP) ** -0.5),
        'ssm_c_re': nrm(ks[21], (L, SSM_GROUPS, SSM_GROUP, SSM_STATE), SSM_STATE ** -0.5),
        'ssm_c_im': nrm(ks[22], (L, SSM_GROUPS, SSM_GROUP, SSM_STATE), SSM_STATE ** -0.5),
        'ssm_d': nrm(ks[23], (L, SSM_W), 1.0),
        'w_glu': nrm(ks[24], (L, SSM_W, SSM_W), SSM_W ** -0.5),
        'b_glu': nrm(ks[25], (L, SSM_W), 0.02),
        'ln1_g': 1.0 + nrm(ks[26], (L, D), 0.02),
        'ln1_b': nrm(ks[27], (L, D), 0.02),
        'w_up': nrm(ks[28], (L, D, 2 * F), D ** -0.5),
        'conv_w': nrm(ks[29], (L, CONV_W, 2 * F), CONV_W ** -0.5),
        'conv_b': nrm(ks[30], (L, 2 * F), 0.02),
        'w_down': nrm(ks[31], (L, F, D), DN_BETA * F ** -0.5),
        'ln2_g': 1.0 + nrm(ks[32], (L, D), 0.02),
        'ln2_b': nrm(ks[33], (L, D), 0.02),
    }

def reference(x_prompt, x_sample, cache_k, cache_v, state_ssm_re, state_ssm_im, state_conv, page_table,
              c_prompt, c_sample, w_ada, b_ada, w_in, w_att_br, w_ssm_br, w_out, sb_bias,
              ssm_a_re, ssm_a_im, ssm_log_dt, ssm_b_re, ssm_b_im, ssm_c_re, ssm_c_im, ssm_d,
              w_glu, b_glu, ln1_g, ln1_b, w_up, conv_w, conv_b, w_down, ln2_g, ln2_b):
    dec_b, n_pages = page_table.shape
    past_len = n_pages * cache_k.shape[2]
    xp, xs = x_prompt, x_sample
    kp_l, vp_l, srp_l, sip_l, cvp_l = [], [], [], [], []
    ks_l, vs_l, srs_l, sis_l, cvs_l = [], [], [], [], []
    for l in range(DEPTH):
        lp = dict(w_ada=w_ada[l], b_ada=b_ada[l], w_in=w_in[l], w_att_br=w_att_br[l],
                  w_ssm_br=w_ssm_br[l], w_out=w_out[l], sb_bias=sb_bias[l],
                  ssm_a_re=ssm_a_re[l], ssm_a_im=ssm_a_im[l],
                  ssm_log_dt=ssm_log_dt[l], ssm_b_re=ssm_b_re[l], ssm_b_im=ssm_b_im[l],
                  ssm_c_re=ssm_c_re[l], ssm_c_im=ssm_c_im[l], ssm_d=ssm_d[l], w_glu=w_glu[l],
                  b_glu=b_glu[l], ln1_g=ln1_g[l], ln1_b=ln1_b[l], w_up=w_up[l], conv_w=conv_w[l],
                  conv_b=conv_b[l], w_down=w_down[l], ln2_g=ln2_g[l], ln2_b=ln2_b[l])
        bp = xp.shape[0]
        h0_p = jnp.zeros((bp, SSM_GROUPS, SSM_STATE), jnp.complex64)
        buf_p = jnp.zeros((bp, CONV_W - 1, 2 * D_FF), xp.dtype)
        xp, kp, vp, srp, sip, cvp = _block(xp, c_prompt, None, None, h0_p, buf_p, lp)
        past_k = cache_k[l][page_table].reshape(dec_b, past_len, ATT_HEADS, HEAD_DIM)
        past_v = cache_v[l][page_table].reshape(dec_b, past_len, ATT_HEADS, HEAD_DIM)
        h0_s = lax.complex(state_ssm_re[l].astype(jnp.float32), state_ssm_im[l].astype(jnp.float32))
        xs, kss, vss, srs, sis, cvs = _block(xs, c_sample, past_k, past_v, h0_s, state_conv[l], lp)
        kp_l.append(kp); vp_l.append(vp); srp_l.append(srp.astype(xp.dtype))
        sip_l.append(sip.astype(xp.dtype)); cvp_l.append(cvp)
        ks_l.append(kss); vs_l.append(vss); srs_l.append(srs.astype(state_ssm_re.dtype))
        sis_l.append(sis.astype(state_ssm_im.dtype)); cvs_l.append(cvs.astype(state_conv.dtype))
    return (xp, xs, jnp.stack(kp_l), jnp.stack(vp_l), jnp.stack(srp_l), jnp.stack(sip_l), jnp.stack(cvp_l),
            jnp.stack(ks_l), jnp.stack(vs_l), jnp.stack(srs_l), jnp.stack(sis_l), jnp.stack(cvs_l))


_drawn_inputs = setup_inputs


def setup_inputs(seed=0):
    import zlib

    import numpy as np

    out = dict(_drawn_inputs(seed))
    spreads = {}
    factors = {'cache_k': 3.576,
     'cache_v': 2.867,
     'sb_bias': 7.78,
     'ssm_a_re': 16.889,
     'ssm_c_re': 5.821,
     'ssm_c_im': 5.844,
     'b_glu': 46.908,
     'ln1_g': 2.759,
     'ln1_b': 2.682,
     'conv_b': 6.283,
     'ln2_g': 7.522,
     'ln2_b': 7.802}
    for name, (base, spread) in spreads.items():
        noise = np.random.default_rng([zlib.crc32(name.encode()), seed]).standard_normal(out[name].shape)
        drawn = base * np.exp(spread * noise) if base else spread * noise
        out[name] = __import__('jax').numpy.asarray(drawn.astype(out[name].dtype))
    for name, factor in factors.items():
        out[name] = (out[name] * factor).astype(out[name].dtype)
    return out
```

```python
import math

import concourse.bass as bass
from concourse import mybir

P = 128
F32 = mybir.dt.float32
F32R = mybir.dt.float32r
I32 = mybir.dt.int32
ALU = mybir.AluOpType
ACT = mybir.ActivationFunctionType
ds = bass.ds

D = 2048
NP = 256
SB, ST = 8, 8
T = NP + SB * ST
HEADS, HD = 8, 128
AW = HEADS * HD
SW = D - AW
GROUPS, GC, GS = 64, 16, 64
FF = 5632
PAGE, PAGES = 128, 8
KD = D // P
KA = AW // P
JF = FF // P
MODS = 6
NC = 1 + SB
CHUNK = 8
CP = NP // CHUNK
CT = CP + SB
GB = P // GC
BATCHES = GROUPS // GB
ALPHA = 2.0 ** 0.25
EPS = 1e-5
SCALE = HD ** -0.5
EXT = 2 + NP + SB * (2 + ST)
QUARTERS = [12, 12, 10, 10]

TWO_PI = (6.28125, 0.0019350051879882812, 2.0 * math.pi - 6.28125 - 0.0019350051879882812)
ROUND = 1.5 * 2.0 ** 23
PI_IN = 3.1415925
LOG_2 = (0.693359375, math.log(2.0) - 0.693359375)

RING = 4
ADA_RING = 4


class Own:

    def __init__(self, eng, sem):
        self.eng, self.sem, self.count, self.index = eng, sem, 0, None

    def begin(self, index, per_pass):
        self.index, self.per_pass, self.k = index, per_pass, 0

    def end(self, passes):
        assert self.k == self.per_pass, (self.k, self.per_pass)
        self.count, self.index = self.count + passes * self.per_pass, None

    def mark(self, instruction):
        instruction.then_inc(self.sem, 1)
        if self.index is None:
            self.count += 1
        else:
            self.k += 1

    def settle(self):
        at = self.count if self.index is None else self.index * self.per_pass + (self.count + self.k)
        self.eng.wait_ge(self.sem, at)

    def step(self, instruction):
        self.mark(instruction)
        self.settle()


def hybrid_step(nc, x_prompt, x_sample, cache_k, cache_v, state_ssm_re, state_ssm_im, state_conv, page_table,
                c_prompt, c_sample, w_ada, b_ada, w_in, w_att_br, w_ssm_br, w_out, sb_bias,
                ssm_a_re, ssm_a_im, ssm_log_dt, ssm_b_re, ssm_b_im, ssm_c_re, ssm_c_im, ssm_d,
                w_glu, b_glu, ln1_g, ln1_b, w_up, conv_w, conv_b, w_down, ln2_g, ln2_b,
                y_prompt, y_sample, k_prompt, v_prompt, ssm_re_prompt, ssm_im_prompt, conv_prompt,
                k_sample, v_sample, ssm_re_sample, ssm_im_sample, conv_sample):
    n_phys = cache_k.shape[1]
    S = {}

    def sem(name):
        S[name] = nc.alloc_semaphore(name)
        return S[name]

    base = (nc.sbuf_base + 127) // 128 * 128

    def at(name, shape, offset, dtype=F32):
        return nc.alloc_sbuf_tensor_at(name, shape, dtype, offset=base + offset)

    CH = T * 4
    small, r_x, r_h = 0, 16384, 16384 + KD * CH
    r_ring = r_h + 2 * KD * CH
    r_split = r_ring + RING * KD * P * 4
    r_u = r_split + 4 * KD * P * 4
    r_q, r_k, r_v = r_u + KA * CH, r_u + 2 * KA * CH, r_u + 3 * KA * CH
    r_vtok = r_v + KA * CH
    r_attl = r_vtok + 3 * AW * 4
    r_tail = r_attl + KA * CH

    mod = at("mod", [P, MODS * KD, NC], small)
    par = at("par", [P, 256], small + 3456)
    cw = at("cw", [P, 3 * 2 * JF + KA], small + 4480)
    ident = at("ident", [P, P], small + 5568)
    mean_of = at("mean_of", [P, P], small + 6080)
    later = at("later", [P, P], small + 6592)
    ones = at("ones", [P, P], small + 7104)
    r_small2 = small + 7616
    masks = at("masks", [P, 384], small + 13312)
    lam8 = at("lam8", [P, 3, GROUPS], small + 14848)
    bias_h = at("bias_h", [P, HEADS], small + 15616)
    sign = at("sign", [P, 2], small + 15648)
    pages = at("pages", [1, SB * PAGES], small + 15680, I32)
    mask_new = at("mask_new", [ST, HEADS * ST], small + 15936)

    xT = at("xT", [P, KD, T], r_x)
    hH, hL = (at(n, [P, KD, T], r_h + i * KD * CH, F32R) for i, n in enumerate(("hH", "hL")))
    ring = [at(f"ring{i}", [P, KD, P], r_ring + i * KD * P * 4) for i in range(RING)]
    wH = [at(f"wH{i}", [P, KD, P], r_split + 2 * i * KD * P * 4, F32R) for i in range(2)]
    wL = [at(f"wL{i}", [P, KD, P], r_split + (2 * i + 1) * KD * P * 4, F32R) for i in range(2)]
    projT = at("projT", [P, 4 * KA, T], r_u)
    ada_ring = [at(f"ada_ring{i}", [P, KD // 2, P], r_vtok + i * KD // 2 * P * 4) for i in range(ADA_RING)]

    xrows = at("xrows", [P, 3, D], r_h)
    crows = at("crows", [NC, D], r_h + 24576)
    csil = at("csil", [NC, D], r_h + 32768)
    b_raw = at("b_raw", [GROUPS, 3, GS * GC], r_ring)
    c_raw = at("c_raw", [GROUPS, GC, 3, GS], r_ring + 12288)
    zeros = at("zeros", [112, AW], r_ring + 24576)
    r_tail2 = r_vtok + 16384
    pr = at("pr", [P, 2, P], r_tail2)
    prw = at("prw", [2 * JF, 3, P], r_tail2 + 1024)
    prd = at("prd", [KA, P], r_tail2 + 2560)
    a_raw = at("a_raw", [GROUPS, 2, P], r_tail2 + 3072)
    log_dt = at("log_dt", [P, GROUPS], r_tail2 + 4096)
    small64 = at("small64", [P, 20, GROUPS], r_tail2 + 4352)
    two_n = at("two_n", [P, GROUPS], r_tail2 + 4352 + 5120 + 576, I32)
    cT = at("cT", [P, KD, NC], r_tail2 + 4352 + 5120)
    pows = [at(f"pow{n}", [P, GROUPS, CHUNK + 1], r_u + i * 2304) for i, n in enumerate(("R", "I"))]
    revs = [at(f"rev{n}", [P, GROUPS, CHUNK], r_u + 4608 + i * 2048) for i, n in enumerate(("R", "I"))]
    b1, b2, c1, c2 = (at(n, [P, GROUPS, GC], r_split + i * 4096) for i, n in enumerate(("b1", "b2", "c1", "c2")))
    bb1, bb2, bt = (at(n, [P, GROUPS, GC], r_split + (4 + i) * 4096) for i, n in enumerate(("bb1", "bb2", "bt")))
    V, VT, PT, PX, P_, w1s = (at(n, [P, GB, P], r_u + 8704 + i * 4096)
                              for i, n in enumerate(("V", "VT", "PT", "PX", "Pm", "w1s")))
    o_s = at("o_s", [P, P], r_u + 8704 + 6 * 4096)

    vtok = at("vtok", [P, 3, AW], r_vtok)
    stage = at("stage", [P, 3, AW], r_attl)

    vpage = [at(f"vpage{i}", [P, AW], r_ring + i * 4096) for i in range(PAGES)]
    kpage = [at(f"kpage{i}", [P, AW], r_split + i * 4096) for i in range(2)]
    kTp = [at(f"kTp{i}", [P, HEADS, PAGE], r_split + 8192 + i * 4096) for i in range(2)]
    HQ = HEADS * ST
    sz, se, sS, sR = (at(n, [P, PAGES + 1, HQ], r_split + 16384 + i * 2304) for i, n in enumerate(("sz", "se", "sS", "sR")))
    pz, pe_, pS = (at(n, [P, 384], r_split + 25600 + i * 1536) for i, n in enumerate(("pz", "pe_", "pS")))
    kh = at("kh", [P, NP], r_split + 30208)
    vh = at("vh", [P, 2, HD], r_split + 31232)
    knew = at("knew", [P, HEADS, ST], r_split + 32256)
    bias_q = at("bias_q", [P, HQ], r_split + 32512)
    vnew = at("vnew", [ST, AW], r_small2)
    attH, attL = at("attH", [P, KA, T], r_v, F32R), at("attL", [P, KA, T], r_attl, F32R)

    U = at("U", [P, GROUPS, CT], r_q)
    G = at("G", [P, 2, GROUPS, CT], r_ring)
    Z = at("Z", [P, 2, GROUPS, CT + 1], r_ring + 20480)
    r_ssm = r_ring + 20480 + 20992
    W1 = at("W1", [P, GB, P], r_ssm)
    W2 = at("W2", [P, GB, P], r_ssm + 4096)
    Uraw = at("Uraw", [CT, CHUNK, P], r_ssm + 8192)
    Ug = at("Ug", [CT, GB, P], r_ssm + 12288)
    Kt = at("Kt", [P, CHUNK, P], r_ssm)
    Pt = at("Pt", [P, GB, P], r_ssm + 4096)
    Yt = at("Yt", [CT, CHUNK, GB, GC], r_ssm + 8192)
    Us = at("Us", [P, GB, CT], r_ssm + 12288)
    Hs = at("Hs", [P, GB, CT], r_ssm + 12288 + 1280)
    h0raw = at("h0raw", [GROUPS, SB, 3, GS], r_k)
    h0 = at("h0", [P, 2, GROUPS, SB], r_vtok)
    t1 = at("t1", [P, 2, GROUPS], r_vtok + 4096)
    t2 = at("t2", [P, 2, GROUPS], r_vtok + 4096 + 512)
    u1 = at("u1", [P, GROUPS, SB], r_vtok + 5120)
    zf = at("zf", [P, GROUPS, SB], r_vtok + 7168)
    fin = at("fin", [GROUPS, NC, P], r_small2)
    ytk = at("ytk", [P, 3, SW], r_ring)
    ypre = [at(f"ypre{i}", [P, T], r_vtok + i * CH) for i in range(2)]
    ygl = [at(f"ygl{i}", [P, T], r_vtok + (2 + i) * CH) for i in range(2)]

    ygH, ygL = at("ygH", [P, KA, T], r_q, F32R), at("ygL", [P, KA, T], r_k, F32R)
    sH, sL = at("sH", [P, KA, T], r_u, F32R), at("sL", [P, KA, T], r_vtok, F32R)
    merged = at("merged", [P, KD, T], r_q)
    gate = [at(f"gate{i}", [P, T], r_tail + i * CH) for i in range(2)]
    part = [at(f"part{i}", [P, T], r_tail + (2 + i) * CH) for i in range(2)]
    mH, mL = (at(n, [P, KD, T], r_h + i * KD * CH, F32R) for i, n in enumerate(("mH", "mL")))

    centred_sq = at("centred_sq", [P, KD, T], r_u)
    mu, var, sd, rstd, newton = (at(n, [P, T], r_u + (KD + i) * CH) for i, n in enumerate(("mu", "var", "sd", "rstd", "newton")))
    res = [at(f"res{i}", [P, T], r_u + (KD + 5 + i) * CH) for i in range(2)]

    conv_raw = at("conv_raw", [2 * JF, SB * 2, P], r_u + (KD + 7) * CH)
    conv_st = at("conv_st", [P, SB * 2, 2 * JF], r_small2)
    fH, fL = (at(n, [P, QUARTERS[0], T], r_u + i * QUARTERS[0] * CH, F32R) for i, n in enumerate(("fH", "fL")))
    yacc = at("yacc", [P, KD, T], r_u + 24 * CH)
    r_f, EB = r_u + 40 * CH, (EXT * 4 + 31) // 32 * 32
    ext = [at(f"ext{i}", [P, EXT], r_f + i * EB) for i in range(4)]
    cvV, cvG = (at(n, [P, EXT], r_f + (4 + i) * EB) for i, n in enumerate(("cvV", "cvG")))
    prod = at("prod", [P, T], r_f + 6 * EB)
    rows_out = at("rows_out", [P, NC * 2, 2 * JF], r_f + 6 * EB + CH)
    rows_t = at("rows_t", [2 * JF, NC * 2, P], r_h)
    ytok = at("ytok", [P, 3, D], r_ring)

    bank = [nc.alloc_psum_tensor(f"bank{i}", [P, 512], F32) for i in range(8)]

    u_tok = nc.dram_tensor("u_tok", (T, SW), F32).ap()
    y_tok = nc.dram_tensor("y_tok", (T, SW), F32).ap()
    w1_d = nc.dram_tensor("w1_d", (BATCHES, P, GB * P), F32).ap()
    p_d = nc.dram_tensor("p_d", (BATCHES, P, GB * P), F32).ap()
    taps_d = nc.dram_tensor("taps_d", (P + 112, SW), F32).ap()

    for name in ("c_landed x_landed params_landed ssm_landed pages_landed silu_ready ident_ready consts_ready "
                 "flipped flips_read ada_free ada_done act_ada prep_act prep_dve v_ready w_flipped w_read "
                 "w1_stored taps_stored p_stored zeros_stored p_ready mod_ready h_ready hi_done split_done chunk_done own_act "
                 "own_dve own_pool ytk_turned proj_ready u_stored v_stored k_stored vtok_read "
                 "head_staged pz_done state_step bias_landed carried w_saved y_saved p_exp_in p_ln p_s p_cs p_arg p_w p_pv att_p knew_staged vnew_landed "
                 "k_flipped kt_dve kt_act scored s_z s_e_in s_ln s_s s_r s_cs s_arg s_w s_pv att_s zn_done "
                 "uraw_landed w1_landed ug_ready w2_ready ug_flipped u_ready g_done g_read h0_landed scanned "
                 "kt_landed pt_landed us_ready y_done y_read y_stored state_stored ytk_landed y_pre y_gelu y_ready "
                 "glu_gate s_ready m_gate m_read merged_ready m_hi m_ready x_pre mean_done centred squared var_done var_ready "
                 "sd_ready rstd_ready normed h2_ready conv_landed halo conv_ev gelu_done f_ready ext_read rows_ready down_ready "
                 "rows_stored y_out angle_ready").split():
        sem(name)
    ring_landed = [sem(f"ring_landed{i}") for i in range(RING)]
    ada_landed = [sem(f"ada_landed{i}") for i in range(ADA_RING)]
    kpage_landed = [sem(f"kpage_landed{i}") for i in range(2)]
    vpage_landed = [sem(f"vpage_landed{i}") for i in range(PAGES)]
    acc_free = [sem(f"acc_free{i}") for i in range(2)]

    PROJ, GLU, MERGE, OUT = 0, 4 * KA, 5 * KA, 5 * KA + 4 * KD
    FFN = OUT + KD
    stages = [("proj", PROJ, KA, [KD] * 4), ("glu", GLU, KA // 4, [KA] * 4), ("merge", MERGE, KD, [KD, KA, KD, KA]),
              ("out", OUT, KD // 4, [KD] * 4)]
    n0, j0 = FFN, 0
    for q, nj in enumerate(QUARTERS):
        stages.append((f"up{q}", n0, nj // 2, [KD] * 4))
        stages.append((f"down{q}", n0 + 2 * nj, KD // 4, [nj] * 4))
        n0, j0 = n0 + 2 * nj + KD, j0 + nj
    ks_of = {s[0]: s[3] for s in stages}
    first_of = {s[0]: s[1] for s in stages}
    passes_of = {s[0]: s[2] for s in stages}
    next_of = {a[0]: b[0] for a, b in zip(stages[1:], stages[2:])}

    w_in_d = w_in[0].rearrange("(k p) c -> p k c", p=P)
    w_ada_d = w_ada[0].rearrange("(h k p) c -> h p k c", p=P, h=2)
    w_att_d = w_att_br[0].rearrange("(k p) c -> p k c", p=P)
    w_ssm_d = w_ssm_br[0].rearrange("(k p) c -> p k c", p=P)
    w_glu_d = w_glu[0].rearrange("(k p) c -> p k c", p=P)
    w_out_d = w_out[0].rearrange("(k p) c -> p k c", p=P)
    w_up_d = w_up[0].rearrange("(k p) c -> p k c", p=P)
    w_down_d = w_down[0].rearrange("(k p) c -> p k c", p=P)

    def alone(eng):
        eng.sem_inc(S["carried"], 1)

    def passes(eng, stage, own, per_pass, body):
        n = passes_of[stage]
        with eng.Fori(0, n - 1) as i:
            if own:
                own.begin(i, per_pass)
            body(i, ks_of[stage])
            if own:
                own.end(n - 1)
        body(n - 1, ks_of[next_of[stage]] if stage in next_of else None)

    def samples(ap):
        return ap[:, NP:T].rearrange("p (b t) -> p b t", b=SB)

    def late(t):
        return t[:, NP + 2:EXT].rearrange("p (b t) -> p b t", b=SB)[:, :, 0:ST]

    def per_sample(ap):
        return ap.unsqueeze(2).to_broadcast([P, SB, ST])

    def setup_turns():
        yield [(csil[0:NC, k * P:(k + 1) * P], NC) for k in range(KD)], P, cT[:].rearrange("p k c -> p (k c)")
        yield [(pr[:, i, :], P) for i in range(2)], P, par[:]
        yield [(prw[:, i, :], 2 * JF) for i in range(3)] + [(prd[:], KA)], P, cw[:]
        yield [(a_raw[:, i, :], GROUPS) for i in range(2)], P, small64[:, 0:2, :]
        for dst, v in ((b1, 0), (b2, 1)):
            for half in range(2):
                src = b_raw[:].rearrange("g v (p n) -> g (v p) n", n=GC)
                yield ([(src[:, v * GS:v * GS + P, 8 * half + n], GROUPS) for n in range(8)], P,
                       dst[:].rearrange("p g n -> p n g")[:, 8 * half:8 * half + 8, :])
        for dst, v in ((c1, 0), (c2, 1)):
            for half in range(2):
                src = c_raw[:].rearrange("g n v p -> g n (v p)")
                yield ([(src[:, 8 * half + n, v * GS:v * GS + P], GROUPS) for n in range(8)], P,
                       dst[:].rearrange("p g n -> p n g")[:, 8 * half:8 * half + 8, :])
        for k in range(KD):
            yield ([(xrows[0:min(P, T - t * P), t, k * P:(k + 1) * P], min(P, T - t * P)) for t in range(3)], P, xT[:, k, :])

    def proj_turns():
        for first, dst in ((0, stage), (3 * KA, vtok), (2 * KA, stage)):
            for half in range(2):
                for t in range(3):
                    rows = min(P, T - t * P)
                    yield ([(projT[:, first + 4 * half + c, t * P:t * P + rows], P) for c in range(4)], rows,
                           dst[0:rows, t, half * 512:half * 512 + 512])

    def state_turns():
        for v in range(2):
            yield ([(h0raw[:].rearrange("g b v p -> g b (v p)")[:, b, v * GS:v * GS + P], GROUPS) for b in range(SB)], P,
                   h0[:, v, :, :].rearrange("p g b -> p b g"))

    def final_state_turns():
        sources = [Z[:, 0, :, CP]] + [zf[:, :, b] for b in range(SB)]
        for first in (0, 4, 8):
            part_ = sources[first:first + 4]
            yield [(s, P) for s in part_], GROUPS, fin[:, first:first + len(part_), :]

    def conv_state_turns():
        for first in range(0, SB * 2, 4):
            yield ([(conv_raw[:, first + r, :], 2 * JF) for r in range(4)], P, conv_st[:, first:first + 4, :])

    def rows_out_turns():
        for first in range(0, NC * 2, 4):
            n = min(4, NC * 2 - first)
            yield [(rows_out[:, first + r, :], P) for r in range(n)], 2 * JF, rows_t[:, first:first + n, :]

    def y_turns():
        for quarter in range(4):
            for t in range(3):
                rows = min(P, T - t * P)
                yield ([(xT[:, 4 * quarter + c, t * P:t * P + rows], P) for c in range(4)], rows,
                       ytok[0:rows, t, quarter * 512:(quarter + 1) * 512])

    def width(sources):
        return sum(w for _, w in sources)

    rows_copied = []
    block = nc.Block()
    with block:

        @block.sync
        def _(sp):
            sp.dma_start(crows[0:1, :], c_prompt).then_inc(S["c_landed"], 16)
            sp.dma_start(crows[1:NC, :], c_sample).then_inc(S["c_landed"], 16)

            def load_ada(h, s, src):
                sp.wait_ge(S["ada_free"], h + 1)
                sp.dma_start(ada_ring[s][:], src).then_inc(ada_landed[s], 16)

            def ada_chunk(m, cc):
                for half in range(2):
                    load_ada(2 * m + half, (2 * cc + half) % ADA_RING, w_ada_d[half][:, :, ds(m * P, P)])

            lp = S["params_landed"]
            for a, b in ((0, b_ada), (96, ln1_g), (112, ln1_b)):
                n = b.shape[1] // P
                sp.dma_start(pr[a:a + n, 0, :], b[0].rearrange("(r c) -> r c", c=P)).then_inc(lp, 16)
            for a, b in ((0, conv_b), (88, ln2_g), (104, ln2_b), (120, b_glu)):
                n = b.shape[1] // P
                sp.dma_start(pr[a:a + n, 1, :], b[0].rearrange("(r c) -> r c", c=P)).then_inc(lp, 16)
            sp.dma_start(prw[:], conv_w[0].rearrange("i (r c) -> r i c", c=P)).then_inc(lp, 16)
            sp.dma_start(prd[:], ssm_d[0].rearrange("(r c) -> r c", c=P)).then_inc(lp, 16)
            with sp.Fori(0, 8) as i:
                for cc in range(4):
                    ada_chunk(i * 4 + cc, cc)

            def load(n, s, K, src):
                sp.wait_ge(S["split_done"], n + 1)
                alone(sp)
                sp.dma_start(ring[s][:, 0:K, :], src).then_inc(ring_landed[s], 16)

            sp.wait_ge(S["flipped"], 4 + 8 + KD)
            sp.wait_ge(S["zeros_stored"], 16)

            def proj_pass(i, column):
                for cc in range(4):
                    load(i * 4 + cc, cc, KD, w_in_d[:, :, ds(column + cc * P, P)])
                    for a in range(2):
                        ada_chunk(i * 8 + 2 * KD + 2 * cc + a, 2 * cc + a)

            with sp.Fori(0, 2) as i:
                proj_pass(i, i * (4 * P) + 3 * AW)
            with sp.Fori(2, 8) as i:
                proj_pass(i, i * (4 * P) - 2 * 4 * P)

            sp.dma_start(pages[:], page_table.rearrange("b n -> (b n)").unsqueeze(0)).then_inc(S["pages_landed"], 16)
            sp.wait_ge(S["pages_landed"], 16)
            sp.wait_ge(S["chunk_done"], 2 + GLU)
            sp.wait_ge(S["v_stored"], 32)
            ck = cache_k[0].rearrange("n t h d -> n t (h d)")
            cv = cache_v[0].rearrange("n t h d -> n t (h d)")
            vs = v_sample[0].rearrange("b t h d -> b t (h d)")
            with sp.Fori(0, SB) as i:
                ids = []
                for p in range(PAGES):
                    ids.append(sp.value_load(pages[0:1, ds(i * PAGES + p, 1)], min_val=0, max_val=n_phys - 1))
                    sp.wait_ge(S["k_flipped"], i * PAGES + p + 1)
                    sp.dma_start(kpage[p % 2][:], ck[ds(ids[p], 1)].rearrange("n t c -> (n t) c")).then_inc(kpage_landed[p % 2], 16)
                sp.wait_ge(S["s_pv"], i + 1)
                sp.dma_start(vnew[:], vs[ds(i, 1)].rearrange("b t c -> (b t) c")).then_inc(S["vnew_landed"], 16)
                for p in range(PAGES):
                    sp.dma_start(vpage[p][:], cv[ds(ids[p], 1)].rearrange("n t c -> (n t) c")).then_inc(vpage_landed[p], 16)

            sp.wait_ge(S["s_pv"], SB + 1)
            sp.wait_ge(S["att_p"], HEADS + 1)
            sp.wait_ge(S["u_stored"], 32)
            sp.wait_ge(S["w1_stored"], 16 * BATCHES)
            sp.dma_start(h0raw[:, :, 0, :], state_ssm_re[0].rearrange("b g p -> g b p")).then_inc(S["h0_landed"], 16)
            sp.dma_start(h0raw[:, :, 2, :], state_ssm_re[0].rearrange("b g p -> g b p")).then_inc(S["h0_landed"], 16)
            sp.dma_start(h0raw[:, :, 1, :], state_ssm_im[0].rearrange("b g p -> g b p")).then_inc(S["h0_landed"], 16)
            u_chunks = u_tok.rearrange("(c s) d -> c s d", s=CHUNK)
            with sp.Fori(0, BATCHES) as i:
                sp.wait_ge(S["g_done"], i + 1)
                sp.dma_start(Uraw[:], u_chunks[:, :, ds(i * P, P)]).then_inc(S["uraw_landed"], 16)
                sp.dma_start(W1[:], w1_d[ds(i, 1)].rearrange("o p (g m) -> (o p) g m", m=P)).then_inc(S["w1_landed"], 16)

            sp.wait_ge(S["g_done"], BATCHES + 1)
            sp.wait_ge(S["taps_stored"], 16 * BATCHES)
            sp.wait_ge(S["p_stored"], 16 * BATCHES)
            with sp.Fori(0, BATCHES) as i:
                sp.wait_ge(S["y_done"], i + 1)
                for s in range(CHUNK):
                    a = (CHUNK - 1 - s) * GC
                    sp.dma_start(Kt[:, s, :], taps_d[a:a + P, ds(i * P, P)]).then_inc(S["kt_landed"], 16)
                sp.dma_start(Pt[:], p_d[ds(i, 1)].rearrange("o p (g m) -> (o p) g m", m=P)).then_inc(S["pt_landed"], 16)
            sp.wait_ge(S["y_stored"], 16 * BATCHES)
            sp.wait_ge(S["scanned"], 1)
            yt = y_tok[0:NP].rearrange("(t p) d -> p t d", p=P)
            sp.dma_start(ytk[:, 0:2, :], yt).then_inc(S["ytk_landed"], 16)
            sp.dma_start(ytk[0:SB * ST, 2, :], y_tok[NP:T]).then_inc(S["ytk_landed"], 16)

            sp.wait_ge(S["y_pre"], KA)
            with sp.Fori(0, KA // 4) as i:
                for cc in range(4):
                    load(i * 4 + (GLU + cc), cc, KA, w_glu_d[:, :, ds((i * 4 + cc) * P, P)])
            with sp.Fori(0, KD) as i:
                load(i * 4 + MERGE, 0, KD, w_in_d[:, :, ds(i * P + 3 * AW + SW, P)])
                load(i * 4 + (MERGE + 1), 1, KA, w_att_d[:, :, ds(i * P, P)])
                load(i * 4 + (MERGE + 2), 2, KD, w_in_d[:, :, ds(i * P + 3 * AW + SW + D, P)])
                load(i * 4 + (MERGE + 3), 3, KA, w_ssm_d[:, :, ds(i * P, P)])
            with sp.Fori(0, KD // 4) as i:
                for cc in range(4):
                    load(i * 4 + (OUT + cc), cc, KD, w_out_d[:, :, ds((i * 4 + cc) * P, P)])
            sp.wait_ge(S["m_ready"], KD)
            sp.dma_start(conv_raw[:], state_conv[0].rearrange("b i (r c) -> r (b i) c", c=P)).then_inc(S["conv_landed"], 16)
            j0 = 0
            for q, nj in enumerate(QUARTERS):
                n0 = first_of[f"up{q}"]
                with sp.Fori(0, nj // 2) as i:
                    for cc in range(4):
                        column = (j0 + cc // 2) * P + (cc % 2) * FF
                        load(i * 4 + (n0 + cc), cc, KD, w_up_d[:, :, ds(i * (2 * P) + column, P)])
                n0 = first_of[f"down{q}"]
                with sp.Fori(0, KD // 4) as i:
                    for cc in range(4):
                        load(i * 4 + (n0 + cc), cc, nj, w_down_d[:, j0:j0 + nj, ds((i * 4 + cc) * P, P)])
                j0 += nj

            sp.wait_ge(S["flips_read"], 60)
            for o, r in ((conv_prompt[0], 0), (conv_sample[0], 2)):
                n = o.shape[0] * 2
                sp.dma_start(o.rearrange("b i (r c) -> r (b i) c", c=P), rows_t[:, r:r + n, :]).then_inc(S["rows_stored"], 16)
            sp.wait_ge(S["flips_read"], 72)
            sp.dma_start(y_prompt[0].rearrange("(t p) d -> p t d", p=P), ytok[:, 0:2, :]).then_inc(S["y_out"], 16)
            sp.dma_start(y_sample.rearrange("b t d -> (b t) d"), ytok[0:SB * ST, 2, :]).then_inc(S["y_out"], 16)
            sp.wait_ge(S["rows_stored"], 32)
            sp.wait_ge(S["y_out"], 32)

        @block.gpsimd
        def _(pool):
            g = nc.gpsimd
            for name in ("w_saved", "y_saved"):
                pool.sem_inc(S[name], 1)
            own = Own(pool, S["own_pool"])
            own.mark(g.memset(zeros[:], 0.0))
            own.mark(g.memset(ident[:], 0.0))
            own.mark(g.memset(later[:], 1.0))
            own.mark(g.memset(mean_of[:], 1.0 / D))
            own.mark(g.memset(masks[:], 0.0))
            own.mark(g.memset(mask_new[:], 0.0))
            own.mark(g.memset(sign[:], 1.0))
            own.step(g.memset(ones[:], 1.0))
            g.affine_select(out=ident[:], in_=ident[:], compare_op=ALU.not_equal, fill=1.0, base=0,
                            pattern=[[-1, P]], channel_multiplier=1).then_inc(S["ident_ready"], 1)
            own.mark(g.affine_select(out=later[:], in_=later[:], compare_op=ALU.is_ge, fill=0.0, base=0,
                                     pattern=[[-1, P]], channel_multiplier=1))
            for first in (0, 256):
                own.mark(g.affine_select(out=masks[:, first:first + P], in_=masks[:, first:first + P], compare_op=ALU.is_gt,
                                         fill=-1.0, base=0, pattern=[[1, P]], channel_multiplier=-1))
            mn = mask_new[:].rearrange("k (h q) -> k h q", h=HEADS)
            own.mark(g.affine_select(out=mn, in_=mn, compare_op=ALU.is_gt, fill=-1.0, base=0,
                                     pattern=[[0, HEADS], [1, ST]], channel_multiplier=-1))
            own.step(g.affine_select(out=sign[:, 0:1], in_=sign[:, 0:1], compare_op=ALU.is_gt, fill=-1.0, base=GS,
                                     pattern=[[0, 1]], channel_multiplier=-1))
            g.tensor_scalar(sign[:, 1:2], sign[:, 0:1], -1.0, None, ALU.mult).then_inc(S["consts_ready"], 1)
            pool.dma_start(taps_d[P:P + 112], zeros[:]).then_inc(S["zeros_stored"], 16)

            pool.wait_ge(S["prep_dve"], 1)
            with pool.Fori(0, BATCHES) as i:
                own.begin(i, 3)
                gs = ds(i * GB, GB)

                def power(t):
                    return t[:, gs, 1:CHUNK + 1].unsqueeze(3).to_broadcast([P, GB, CHUNK, GC])

                def rows(t):
                    return t[:, gs, :].unsqueeze(2).to_broadcast([P, GB, CHUNK, GC])

                def blocks(t):
                    return t[:].rearrange("p g (s n) -> p g s n", n=GC)

                own.mark(g.tensor_tensor(blocks(PT), power(pows[0]), rows(c1), ALU.mult))
                own.step(g.tensor_tensor(blocks(PX), power(pows[1]), rows(c2), ALU.mult))
                own.step(g.tensor_tensor(P_[:], PT[:], PX[:], ALU.add))
                pool.dma_start(p_d[ds(i, 1)].rearrange("o p c -> (o p) c"), P_[:].rearrange("p g m -> p (g m)")).then_inc(S["p_stored"], 16)
                pool.wait_ge(S["w_read"], i + 2)
                alone(pool)
                pool.dma_start(w1_d[ds(i, 1)].rearrange("o p c -> (o p) c"), w1s[:].rearrange("p g m -> p (g m)")).then_inc(S["w1_stored"], 16)
                pool.dma_start(taps_d[0:P, ds(i * P, P)], o_s[:]).then_inc(S["taps_stored"], 16)
                for name in ("p_stored", "w1_stored", "taps_stored"):
                    pool.wait_ge(S[name], i * 16 + 16)
                pool.sem_inc(S["w_saved"], 1)
                own.end(BATCHES)

            f = 4 + 8 + KD

            def store_rows(prompt, sample, src, name):
                pool.dma_start(prompt.rearrange("(t p) c -> p t c", p=P), src[:, 0:2, :]).then_inc(S[name], 16)
                pool.dma_start(sample, src[0:SB * ST, 2, :]).then_inc(S[name], 16)

            pool.wait_ge(S["flips_read"], f + 6)
            store_rows(u_tok[0:NP], u_tok[NP:T], stage, "u_stored")
            pool.wait_ge(S["flips_read"], f + 12)
            store_rows(v_prompt[0, 0].rearrange("t h d -> t (h d)"), v_sample[0].rearrange("b t h d -> (b t) (h d)"), vtok, "v_stored")
            pool.wait_ge(S["flips_read"], f + 18)
            store_rows(k_prompt[0, 0].rearrange("t h d -> t (h d)"), k_sample[0].rearrange("b t h d -> (b t) (h d)"), stage, "k_stored")

            pool.wait_ge(S["chunk_done"], 2 + GLU)
            own.mark(g.memset(sR[:], 0.0))
            own.mark(g.memset(sz[:], 0.0))
            own.mark(g.memset(se[:], 0.0))
            own.step(g.memset(sS[:], 0.0))
            pool.wait_ge(S["bias_landed"], 16)
            for q in range(ST):
                last = g.tensor_copy(bias_q[:].rearrange("p (h q) -> p h q", q=ST)[:, :, q], bias_h[:])
            own.step(last)
            with pool.Fori(0, SB) as i:
                own.begin(i, 7)
                pool.wait_ge(S["p_pv"], i + 1)
                own.step(g.tensor_copy(kh[:].unsqueeze(1), projT[:, ds(i + 2 * KA, 1), 0:NP]))
                g.tensor_copy(vh[:], vtok[:, 0:2, ds(i * HD, HD)]).then_inc(S["head_staged"], 1)
                pool.wait_ge(S["zn_done"], i + 1)
                g.tensor_copy(knew[:], projT[:, 2 * KA:3 * KA, ds(i * ST + NP, ST)]).then_inc(S["knew_staged"], 1)
                pool.wait_ge(S["s_s"], i + 1)
                alone(pool)
                own.step(g.tensor_copy(sR[:, PAGES - 2, :], sS[:, PAGES - 1, :]))
                for p in range(PAGES - 3, -1, -1):
                    ins = g.tensor_tensor(sR[:, p, :], sR[:, p + 1, :], sS[:, p + 1, :], ALU.add)
                    if p:
                        own.step(ins)
                    else:
                        ins.then_inc(S["s_r"], 1)
                own.end(SB)

            pool.wait_ge(S["s_pv"], SB + 1)
            with pool.Fori(0, BATCHES) as i:
                pool.wait_ge(S["uraw_landed"], i * 16 + 16)
                pool.wait_ge(S["ug_flipped"], i + 1)
                alone(pool)
                for gg in range(GB):
                    last = g.tensor_copy(Ug[:, gg, :].rearrange("c (s n) -> c s n", n=GC), Uraw[:, :, gg * GC:(gg + 1) * GC])
                last.then_inc(S["ug_ready"], 1)
            pool.wait_ge(S["scanned"], 1)
            y_chunks = y_tok.rearrange("(c s) d -> c s d", s=CHUNK)
            with pool.Fori(0, BATCHES) as i:
                pool.wait_ge(S["y_done"], i + 1)
                own.begin(i, 2)
                own.mark(g.tensor_copy(Us[:], U[:, ds(i * GB, GB), :]))
                own.mark(g.tensor_copy(Hs[:, :, 0:CP], Z[:, 0, ds(i * GB, GB), 0:CP]))
                g.tensor_copy(Hs[:, :, CP:CT], Z[:, 0, ds(i * GB, GB), CP + 1:CT + 1]).then_inc(S["us_ready"], 1)
                own.end(BATCHES)
                pool.wait_ge(S["y_read"], i + 2)
                pool.dma_start(y_chunks[:, :, ds(i * P, P)], Yt[:].rearrange("c s g n -> c s (g n)")).then_inc(S["y_stored"], 16)
                pool.wait_ge(S["y_stored"], i * 16 + 16)
                pool.sem_inc(S["y_saved"], 1)
            pool.wait_ge(S["flips_read"], f + 18 + 2 + 3)
            for o, r, b in ((ssm_re_prompt, 0, 0), (ssm_im_prompt, 1, 0), (ssm_re_sample, 0, 1), (ssm_im_sample, 1, 1)):
                n = SB if b else 1
                pool.dma_start(o[0].rearrange("b g p -> g b p"), fin[:, b:b + n, r * GS:(r + 1) * GS]).then_inc(S["state_stored"], 16)

            pool.wait_ge(S["flips_read"], f + 18 + 2 + 3 + 4)
            pool.wait_ge(S["h2_ready"], KD)
            for e in ext:
                own.mark(g.memset(e[:, 0:2], 0.0))
            own.settle()
            j0 = 0
            done = 0
            for q, nj in enumerate(QUARTERS):
                with pool.Fori(0, nj // 2) as i:
                    own.begin(i, 8)
                    for cc in range(4):
                        block_no = i * 2 + (j0 + cc // 2 + (cc % 2) * JF)
                        tail = ext[cc][:, NP + 2:EXT].rearrange("p (b t) -> p b t", b=SB)
                        n = i * 4 + (done + cc)
                        pool.wait_ge(S["ext_read"], n + 1)
                        own.settle()
                        g.tensor_copy(tail[:, :, 0:2], conv_st[:, :, ds(block_no, 1)].rearrange("p (b i) o -> p b (i o)", b=SB)).then_inc(S["halo"], 1)
                        pool.wait_ge(S["conv_ev"], n + 1)
                        own.mark(g.tensor_copy(rows_out[:, 0:2, ds(block_no, 1)], ext[cc][:, NP:NP + 2].unsqueeze(2)))
                        pool.wait_ge(acc_free[cc % 2], i * 2 + (first_of[f"up{q}"] // 2 + cc // 2 + 2))
                        own.mark(g.tensor_copy(rows_out[:, 2:2 + 2 * SB, ds(block_no, 1)].rearrange("p (b i) o -> p b (i o)", b=SB), tail[:, :, ST:ST + 2]))
                    own.end(nj // 2)
                j0 += nj
                done += 2 * nj
            own.settle()
            rows_copied.append(own.count)
            for name, n in (("u_stored", 32), ("v_stored", 32), ("k_stored", 32), ("state_stored", 64),
                            ("w1_stored", 16 * BATCHES), ("taps_stored", 16 * BATCHES),
                            ("p_stored", 16 * BATCHES), ("y_stored", 16 * BATCHES)):
                pool.wait_ge(S[name], n)

        @block.tensor
        def _(pe):
            t = nc.tensor
            turned = [0]

            def turn(turns, ready=None):
                for n, (sources, rows, _) in enumerate(turns):
                    if ready and n in ready:
                        ready[n]()
                    if turned[0] >= 4:
                        pe.wait_ge(S["flips_read"], turned[0] - 3)
                    b, c = bank[4 + turned[0] % 4], 0
                    for src, w in sources:
                        k = src.shape[0]
                        last = t.transpose(b[0:rows, c:c + w], src, ident[0:k, 0:k])
                        c += w
                    last.then_inc(S["flipped"], 1)
                    turned[0] += 1

            pe.sem_inc(S["ada_free"], ADA_RING)
            pe.sem_inc(S["chunk_done"], 2)
            pe.sem_inc(S["k_flipped"], 2)
            for name in ("scored", "g_done", "y_done", "ug_flipped", "p_pv", "zn_done", "s_pv", "w_flipped"):
                pe.sem_inc(S[name], 2 if name == "scored" else 1)

            pe.wait_ge(S["ident_ready"], 1)
            turn(setup_turns(), {0: lambda: pe.wait_ge(S["silu_ready"], 1), 1: lambda: pe.wait_ge(S["params_landed"], 9 * 16),
                                 3: lambda: pe.wait_ge(S["ssm_landed"], 11 * 16), 12: lambda: pe.wait_ge(S["x_landed"], 32)})

            def ada_chunk(m, landed, cc):
                pe.wait_ge(S["act_ada"], m + 1)
                b = bank[2 + cc % 2]
                for half in range(2):
                    s = (2 * cc + half) % ADA_RING
                    pe.wait_ge(ada_landed[s], landed)
                    for k in range(KD // 2):
                        last = t.matmul(b[:, 0:NC], ada_ring[s][:, k, :], cT[:, half * 8 + k, :],
                                        start=(half == 0 and k == 0), stop=(half == 1 and k == KD // 2 - 1))
                    last.then_inc(S["ada_free"], 1)

            with pe.Fori(0, 8) as i:
                for cc in range(4):
                    ada_chunk(i * 4 + cc, i * 32 + 16 * (cc // 2 + 1), cc)
                pe.wait_ge(S["v_ready"], i + 1)
                pe.wait_ge(S["w_read"], i + 1)
                for gg in range(GB):
                    t.transpose(bank[4 + gg // 4][:, (gg % 4) * P:(gg % 4 + 1) * P], V[:, gg, :], ident[:])
                for gg in range(GB):
                    last = t.matmul(bank[6][:, gg * GC:(gg + 1) * GC], V[:, gg, :],
                                    c1[:, ds(i * GB + gg, 1), :].rearrange("p o n -> p (o n)"), start=True, stop=True)
                last.then_inc(S["w_flipped"], 1)

            def product(n, cc, K, half_n, high, low):
                pe.wait_ge(S["split_done"], n + (1 + RING))
                pe.wait_ge(acc_free[cc % 2], half_n + 1)
                acc = bank[cc % 2][:, 0:T]
                a, b = wH[cc % 2], wL[cc % 2]
                for k in range(K):
                    t.matmul(acc, a[:, k, :], high[:, k, :], start=(k == 0), stop=False)
                    t.matmul(acc, a[:, k, :], low[:, k, :], start=False, stop=False)
                    last = t.matmul(acc, b[:, k, :], high[:, k, :], start=False, stop=(k == K - 1))
                last.then_inc(S["chunk_done"], 1)

            def products(i, n0, cc, K, high, low):
                product(i * 4 + (n0 + cc), cc, K, i * 2 + (n0 // 2 + cc // 2), high, low)

            pe.wait_ge(S["h_ready"], KD)
            with pe.Fori(0, KA) as i:
                for cc in range(4):
                    products(i, PROJ, cc, KD, hH, hL)
                    for a in range(2):
                        c2_ = 2 * cc + a
                        ada_chunk(i * 8 + (2 * KD + c2_), i * 64 + (8 * 16 * 2 + 16 * (c2_ // 2 + 1)), c2_)

            for a_ in acc_free:
                pe.wait_ge(a_, GLU // 2 + 1)
            turn(proj_turns())

            pe.wait_ge(S["consts_ready"], 1)
            pe.wait_ge(S["flips_read"], turned[0])
            with pe.Fori(0, SB) as i:
                def flip(p):
                    pe.wait_ge(kpage_landed[p % 2], i * 64 + 16 * (p // 2 + 1))
                    pe.wait_ge(S["kt_dve"], i * PAGES + (p + 1))
                    pe.wait_ge(S["kt_act"], i * PAGES + (p + 1))
                    for h in range(HEADS):
                        last = t.transpose(bank[h // 4][:, (h % 4) * P:(h % 4 + 1) * P], kpage[p % 2][:, h * HD:(h + 1) * HD], ident[:])
                    last.then_inc(S["k_flipped"], 1)

                def score(p):
                    pe.wait_ge(S["kt_dve"], i * PAGES + (p + 2))
                    pe.wait_ge(S["kt_act"], i * PAGES + (p + 2))
                    if p == 0:
                        pe.wait_ge(S["s_e_in"], i + 1)
                    for h in range(HEADS):
                        a = p * HQ + h * ST
                        last = t.matmul(bank[2][:, a:a + ST], kTp[p % 2][:, h, :],
                                        projT[:, KA + h, ds(i * ST + NP, ST)], start=True, stop=True)
                    last.then_inc(S["scored"], 1)

                flip(0)
                pe.wait_ge(S["head_staged"], i + 1)
                pe.wait_ge(S["att_p"], i + 1)
                q = projT[:, ds(i + KA, 1), :].rearrange("p o t -> p (o t)")
                t.matmul(bank[4][:, 0:NP], kh[:, 0:P], q[:, 0:NP], start=True, stop=True)
                t.matmul(bank[4][:, NP:NP + P], kh[:, P:NP], q[:, P:NP], start=True, stop=True).then_inc(S["pz_done"], 1)
                for p in range(1, PAGES):
                    flip(p)
                    score(p - 1)
                    if p == 3:
                        pe.wait_ge(S["p_s"], i + 1)
                        t.matmul(bank[5][:, 0:384], later[:], pS[:], start=True, stop=False)
                        t.matmul(bank[5][:, P:NP], ones[:], pS[:, NP:NP + P], start=False, stop=True).then_inc(S["p_cs"], 1)
                    if p == 6:
                        pe.wait_ge(S["p_w"], i + 1)
                        t.matmul(bank[4][:, 0:NP], vh[:, 0, :], pe_[:, 0:NP], start=True, stop=False)
                        t.matmul(bank[4][:, P:NP], vh[:, 1, :], pe_[:, NP:NP + P], start=False, stop=True).then_inc(S["p_pv"], 1)
                score(PAGES - 1)
                pe.wait_ge(S["knew_staged"], i + 1)
                alone(pe)
                for h in range(HEADS):
                    last = t.matmul(bank[7][0:ST, h * ST:(h + 1) * ST], knew[:, h, :],
                                    projT[:, KA + h, ds(i * ST + NP, ST)], start=True, stop=True)
                last.then_inc(S["zn_done"], 1)
                pe.wait_ge(S["s_s"], i + 1)
                t.matmul(bank[3][:], later[:], sS[:, 0:PAGES, :].rearrange("p a c -> p (a c)"), start=True, stop=False)
                t.matmul(bank[3][:], ones[0:ST, :], sS[0:ST, PAGES:PAGES + 1, :].to_broadcast([ST, PAGES, HQ]), start=False, stop=False)
                t.matmul(bank[7][0:ST, HQ:2 * HQ], later[0:ST, 0:ST], sS[0:ST, PAGES, :], start=True, stop=True)
                pe.wait_ge(S["s_r"], i + 1)
                t.matmul(bank[3][:], ones[:], sR[:, 0:PAGES, :].rearrange("p a c -> p (a c)"), start=False, stop=True).then_inc(S["s_cs"], 1)
                pe.wait_ge(S["s_w"], i + 1)
                pe.wait_ge(S["att_s"], i + 1)
                pe.wait_ge(S["vnew_landed"], i * 16 + 16)
                for p in range(PAGES):
                    pe.wait_ge(vpage_landed[p], i * 16 + 16)
                for h in range(HEADS):
                    o = bank[6][:, h * ST:(h + 1) * ST]
                    for p in range(PAGES):
                        t.matmul(o, vpage[p][:, h * HD:(h + 1) * HD], se[:, p, h * ST:(h + 1) * ST], start=(p == 0), stop=False)
                    last = t.matmul(o, vnew[:, h * HD:(h + 1) * HD], se[0:ST, PAGES, h * ST:(h + 1) * ST], start=False, stop=True)
                last.then_inc(S["s_pv"], 1)

            pe.wait_ge(S["att_s"], SB + 1)
            with pe.Fori(0, BATCHES) as i:
                pe.wait_ge(S["ug_ready"], i + 1)
                alone(pe)
                for gg in range(GB):
                    last = t.transpose(bank[4][:, gg * CT:(gg + 1) * CT], Ug[:, gg, :], ident[0:CT, 0:CT])
                last.then_inc(S["ug_flipped"], 1)
                pe.wait_ge(S["u_ready"], i + 1)
                pe.wait_ge(S["w2_ready"], i + 1)
                pe.wait_ge(S["g_read"], i + 1)
                for b, w in ((5, W1), (6, W2)):
                    for gg in range(GB):
                        last = t.matmul(bank[b][:, gg * CT:(gg + 1) * CT], w[:, gg, :],
                                        U[:, ds(i * GB + gg, 1), :].rearrange("p o c -> p (o c)"), start=True, stop=True)
                last.then_inc(S["g_done"], 1)
            pe.wait_ge(S["h0_landed"], 48)
            pe.wait_ge(S["g_read"], BATCHES + 1)
            turn(state_turns())
            pe.wait_ge(S["scanned"], 1)
            turn(final_state_turns())
            pe.wait_ge(S["flips_read"], turned[0])
            with pe.Fori(0, BATCHES) as i:
                pe.wait_ge(S["us_ready"], i + 1)
                pe.wait_ge(S["kt_landed"], i * (16 * CHUNK) + 16 * CHUNK)
                pe.wait_ge(S["pt_landed"], i * 16 + 16)
                pe.wait_ge(S["y_read"], i + 1)
                for gg in range(GB):
                    o = bank[4 + gg // 4][0:CT, (gg % 4) * P:(gg % 4 + 1) * P]
                    t.matmul(o.rearrange("c (s n) -> c s n", n=GC), Us[:, gg, :], Kt[:, :, gg * GC:(gg + 1) * GC], start=True, stop=False)
                    last = t.matmul(o, Hs[:, gg, :], Pt[:, gg, :], start=False, stop=True)
                last.then_inc(S["y_done"], 1)
            pe.wait_ge(S["y_read"], BATCHES + 1)
            pe.wait_ge(S["ytk_landed"], 32)
            for c in range(KA):
                if c >= 4:
                    pe.wait_ge(S["y_pre"], c - 3)
                for tt in range(3):
                    rows = min(P, T - tt * P)
                    last = t.transpose(bank[4 + c % 4][:, tt * P:tt * P + rows], ytk[0:rows, tt, c * P:(c + 1) * P], ident[0:rows, 0:rows])
                last.then_inc(S["ytk_turned"], 1)

            pe.wait_ge(S["y_ready"], KA)
            passes(pe, "glu", None, 0, lambda i, _: [products(i, GLU, cc, KA, ygH, ygL) for cc in range(4)])
            pe.wait_ge(S["s_ready"], KA)
            operands = [(KD, hH, hL), (KA, attH, attL), (KD, hH, hL), (KA, sH, sL)]
            passes(pe, "merge", None, 0, lambda i, _: [products(i, MERGE, cc, *operands[cc]) for cc in range(4)])
            pe.wait_ge(S["m_ready"], KD)
            passes(pe, "out", None, 0, lambda i, _: [products(i, OUT, cc, KD, mH, mL) for cc in range(4)])

            def layer_norm(nth):
                pe.wait_ge(S["x_pre"], KD * (nth + 1) + 1)
                for k in range(KD):
                    last = t.matmul(bank[2][:, 0:T], mean_of[:], xT[:, k, :], start=(k == 0), stop=(k == KD - 1))
                last.then_inc(S["mean_done"], 1)
                for k in range(KD):
                    pe.wait_ge(S["squared"], KD * nth + k + 1)
                    last = t.matmul(bank[3][:, 0:T], mean_of[:], centred_sq[:, k, :], start=(k == 0), stop=(k == KD - 1))
                last.then_inc(S["var_done"], 1)

            pe.wait_ge(S["conv_landed"], 16)
            turn(conv_state_turns())
            layer_norm(0)
            pe.wait_ge(S["h2_ready"], KD)
            down = 0
            for q, nj in enumerate(QUARTERS):
                n0 = first_of[f"up{q}"]
                passes(pe, f"up{q}", None, 0, lambda i, _, n0=n0: [products(i, n0, cc, KD, hH, hL) for cc in range(4)])
                down += nj
                pe.wait_ge(S["f_ready"], down + 1)
                n0 = first_of[f"down{q}"]
                passes(pe, f"down{q}", None, 0, lambda i, _, n0=n0, nj=nj: [products(i, n0, cc, nj, fH, fL) for cc in range(4)])
            pe.wait_ge(S["own_pool"], rows_copied[0])
            turn(rows_out_turns())
            layer_norm(1)
            pe.wait_ge(S["normed"], KD)
            turn(y_turns())

        @block.scalar
        def _(act):
            a = nc.scalar
            own = Own(act, S["own_act"])
            act.sem_inc(S["act_ada"], 2)
            act.sem_inc(S["w_read"], 1)
            act.sem_inc(S["kt_act"], 1)
            act.sem_inc(S["y_read"], 1)
            for s in acc_free:
                act.sem_inc(s, 1)
            act.dma_start(xrows[:, 0:2, :], x_prompt[0].rearrange("(t p) d -> p t d", p=P)).then_inc(S["x_landed"], 16)
            act.dma_start(xrows[0:SB * ST, 2, :], x_sample.rearrange("b t d -> (b t) d")).then_inc(S["x_landed"], 16)
            act.wait_ge(S["c_landed"], 32)
            a.activation(csil[:], crows[:], ACT.Sigmoid).then_inc(S["prep_act"], 1)
            for v in range(2):
                act.dma_start(a_raw[:, 0, v * GS:(v + 1) * GS], ssm_a_re[0]).then_inc(S["ssm_landed"], 16)
                act.dma_start(a_raw[:, 1, v * GS:(v + 1) * GS], ssm_a_im[0]).then_inc(S["ssm_landed"], 16)
            for v, (b, c) in enumerate(((ssm_b_re, ssm_c_re), (ssm_b_im, ssm_c_im), (ssm_b_re, ssm_c_re))):
                act.dma_start(b_raw[:, v, :], b[0].rearrange("g p n -> g (p n)")).then_inc(S["ssm_landed"], 16)
                act.dma_start(c_raw[:, :, v, :], c[0]).then_inc(S["ssm_landed"], 16)
            act.dma_start(log_dt[:], ssm_log_dt.to_broadcast([P, GROUPS])).then_inc(S["ssm_landed"], 16)
            act.dma_start(bias_h[:], sb_bias.to_broadcast([P, HEADS])).then_inc(S["bias_landed"], 16)

            act.wait_ge(S["angle_ready"], 1)
            a.activation(small64[:, 6, :], small64[:, 4, :], ACT.Sin).then_inc(S["prep_act"], 1)
            a.activation(small64[:, 7, :], small64[:, 4, :], ACT.Sin, scale=0.5).then_inc(S["prep_act"], 1)

            def ada_out(m, cc, credit=2):
                act.wait_ge(S["ada_free"], m * 2 + (ADA_RING + 2))
                a.activation(mod[:, ds(m, 1), :].rearrange("p o c -> p (o c)"), bank[2 + cc % 2][:, 0:NC], ACT.Identity,
                             bias=par[:, ds(m, 1)]).then_inc(S["act_ada"], 1)

            act.wait_ge(S["flips_read"], 4)
            with act.Fori(0, 8) as i:
                for cc in range(4):
                    ada_out(i * 4 + cc, cc)
                act.wait_ge(S["w_flipped"], i + 2)
                act.wait_ge(S["w_saved"], i + 1)
                a.activation(w1s[:, 0:4, :].rearrange("p g m -> p (g m)"), bank[4][:], ACT.Copy)
                a.activation(w1s[:, 4:8, :].rearrange("p g m -> p (g m)"), bank[5][:], ACT.Copy)
                a.activation(o_s[:], bank[6][:, 0:P], ACT.Copy).then_inc(S["w_read"], 1)

            def split_high(n, cc, K, n4):
                act.wait_ge(ring_landed[cc], n4 * 16 + 16)
                act.wait_ge(S["chunk_done"], n + 1)
                a.activation(wH[cc % 2][:, 0:K, :], ring[cc][:, 0:K, :], ACT.Copy).then_inc(S["hi_done"], 1)

            def split_ahead(i, n0, cc, next_ks, own_ks):
                c = cc + 2
                if c < 4:
                    split_high(i * 4 + (n0 + c), c, own_ks[c], i + n0 // 4)
                elif next_ks:
                    split_high(i * 4 + (n0 + c), c - 4, next_ks[c - 4], i + (n0 // 4 + 1))

            def start_stream(n0, ks):
                for c in range(2):
                    split_high(n0 + c, c, ks[c], n0 // 4)

            def wait_product(i, n0, cc):
                act.wait_ge(S["chunk_done"], i * 4 + (n0 + cc + 3))

            act.wait_ge(S["flips_read"], 12)
            act.wait_ge(S["p_stored"], 16 * BATCHES)
            act.wait_ge(S["w_flipped"], BATCHES + 1)
            start_stream(PROJ, [KD] * 4)

            def proj_pass(i, next_ks):
                for cc in range(4):
                    for e in range(2):
                        c2_ = 2 * cc + e
                        if e == 0:
                            wait_product(i, PROJ, cc)
                            a.activation(projT[:, ds(i * 4 + cc, 1), :].rearrange("p o t -> p (o t)"),
                                         bank[cc % 2][:, 0:T], ACT.Copy).then_inc(acc_free[cc % 2], 1)
                            split_ahead(i, PROJ, cc, next_ks, [KD] * 4)
                        ada_out(i * 8 + (2 * KD + c2_), c2_)

            act.wait_ge(S["w1_stored"], 16 * BATCHES)
            act.wait_ge(S["taps_stored"], 16 * BATCHES)
            with act.Fori(0, KA - 1) as i:
                proj_pass(i, [KD] * 4)
            proj_pass(KA - 1, None)

            act.wait_ge(S["flips_read"], 4 + 8 + KD + 18)
            with act.Fori(0, SB) as i:
                def read_page(p):
                    act.wait_ge(S["k_flipped"], i * PAGES + (p + 3))
                    act.wait_ge(S["scored"], i * PAGES + (p + 1))
                    a.activation(kTp[p % 2][:, 4:8, :].rearrange("p h k -> p (h k)"), bank[1][:], ACT.Copy).then_inc(S["kt_act"], 1)

                read_page(0)
                read_page(1)
                act.wait_ge(S["p_exp_in"], i + 1)
                own.begin(i, 2)
                own.step(a.activation(pe_[:], pe_[:], ACT.Exp))
                a.activation(pe_[:], pe_[:], ACT.Ln, bias=1.0).then_inc(S["p_ln"], 1)
                for p in (2, 3, 4):
                    read_page(p)
                act.wait_ge(S["p_arg"], i + 1)
                a.activation(pe_[:], pe_[:], ACT.Exp).then_inc(S["p_w"], 1)
                for p in (5, 6, 7):
                    read_page(p)
                act.wait_ge(S["s_e_in"], i + 2)
                own.step(a.activation(se[:], se[:], ACT.Exp))
                a.activation(se[:], se[:], ACT.Ln, bias=1.0).then_inc(S["s_ln"], 1)
                act.wait_ge(S["s_arg"], i + 1)
                a.activation(se[:], se[:], ACT.Exp).then_inc(S["s_w"], 1)
                own.end(SB)

            with act.Fori(0, BATCHES) as i:
                act.wait_ge(S["ug_flipped"], i + 2)
                a.activation(U[:, ds(i * GB, GB), :].rearrange("p g c -> p (g c)"), bank[4][:, 0:GB * CT], ACT.Copy).then_inc(S["u_ready"], 1)
            with act.Fori(0, BATCHES) as i:
                act.wait_ge(S["y_done"], i + 2)
                act.wait_ge(S["y_saved"], i + 1)
                for half in range(2):
                    for g4 in range(4):
                        last = a.activation(Yt[:, :, half * 4 + g4, :],
                                            bank[4 + half][0:CT, g4 * P:(g4 + 1) * P].rearrange("c (s n) -> c s n", n=GC), ACT.Copy)
                last.then_inc(S["y_read"], 1)
            for c in range(KA):
                act.wait_ge(S["y_pre"], c + 1)
                if c >= 2:
                    act.wait_ge(S["y_ready"], c - 1)
                a.activation(ygl[c % 2][:], ypre[c % 2][:], ACT.Gelu_apprx_tanh).then_inc(S["y_gelu"], 1)

            start_stream(GLU, ks_of["glu"])

            def glu_pass(i, next_ks):
                for cc in range(4):
                    wait_product(i, GLU, cc)
                    m = i * 4 + cc
                    if m >= 2:
                        act.wait_ge(S["s_ready"], m - 1)
                    a.activation(gate[cc % 2][:], bank[cc % 2][:, 0:T], ACT.Sigmoid,
                                 bias=par[:, P + 120 + m:P + 121 + m]).then_inc(acc_free[cc % 2], 1)
                    split_ahead(i, GLU, cc, next_ks, ks_of["glu"])

            glu_pass(0, ks_of["glu"])
            glu_pass(1, ks_of["merge"])

            def merge_pass(i, next_ks):
                for cc in range(4):
                    if cc % 2 == 0:
                        wait_product(i, MERGE, cc)
                        act.wait_ge(acc_free[1], i * 2 + (MERGE // 2 + cc // 2))
                        a.activation(gate[cc // 2][:], bank[0][:, 0:T], ACT.Sigmoid).then_inc(acc_free[0], 1)
                    split_ahead(i, MERGE, cc, next_ks, ks_of["merge"])

            act.wait_ge(S["s_ready"], KA)
            passes(act, "merge", None, 0, merge_pass)
            passes(act, "out", None, 0, lambda i, ks: [split_ahead(i, OUT, cc, ks, ks_of["out"]) for cc in range(4)])

            def layer_norm(nth, g0, b0):
                for k in range(KD):
                    act.wait_ge(S["centred"], KD * nth + k + 1)
                    a.activation(centred_sq[:, k, :], xT[:, k, :], ACT.Square).then_inc(S["squared"], 1)
                act.wait_ge(S["var_ready"], nth + 1)
                a.activation(sd[:], var[:], ACT.Sqrt).then_inc(S["sd_ready"], 1)

            layer_norm(0, 96, 112)
            conv = 0
            for q, nj in enumerate(QUARTERS):
                n0 = first_of[f"up{q}"]

                def up_pass(i, next_ks, n0=n0, conv=conv, q=q):
                    for cc in range(4):
                        wait_product(i, n0, cc)
                        act.wait_ge(S["halo"], i * 4 + (conv + cc + 1))
                        b = bank[cc % 2]
                        a.activation(ext[cc][:, 2:2 + NP], b[:, 0:NP], ACT.Copy).then_inc(S["conv_ev"], 1)
                        tail = ext[cc][:, NP + 2:EXT].rearrange("p (b t) -> p b t", b=SB)
                        a.activation(tail[:, :, 2:2 + ST], samples(b), ACT.Copy).then_inc(acc_free[cc % 2], 1)
                        split_ahead(i, n0, cc, next_ks, ks_of["up0"])
                        if cc % 2:
                            act.wait_ge(S["ext_read"], i * 4 + (conv + cc + 5))
                            a.activation(cvG[:, 0:EXT - 2], cvG[:, 0:EXT - 2], ACT.Gelu_apprx_tanh).then_inc(S["gelu_done"], 1)

                passes(act, f"up{q}", None, 0, up_pass)
                conv += 2 * nj
                n0 = first_of[f"down{q}"]
                passes(act, f"down{q}", None, 0,
                       lambda i, ks, n0=n0, q=q: [split_ahead(i, n0, cc, ks, ks_of[f"down{q}"]) for cc in range(4)])
            layer_norm(1, P + 88, P + 104)


        @block.vector
        def _(dve):
            v = nc.vector
            own = Own(dve, S["own_dve"])
            for name in ("kt_dve", "s_e_in", "att_p", "att_s", "g_read", "x_pre", "f_ready"):
                dve.sem_inc(S[name], 1)
            dve.sem_inc(S["split_done"], RING)
            dve.sem_inc(S["ext_read"], 4)
            MUL, ADD, SUB = ALU.mult, ALU.add, ALU.subtract
            flips = [0]

            def read_turns(turns):
                for sources, rows, dst in turns:
                    dve.wait_ge(S["flipped"], flips[0] + 1)
                    src = bank[4 + flips[0] % 4][0:rows, 0:width(sources)]
                    if len(dst.shape) == 3:
                        src = src.rearrange("p (a b) -> p a b", a=dst.shape[1])
                    v.tensor_copy(dst, src).then_inc(S["flips_read"], 1)
                    flips[0] += 1

            dve.wait_ge(S["prep_act"], 1)
            v.tensor_tensor(csil[:], csil[:], crows[:], MUL).then_inc(S["silu_ready"], 1)
            read_turns(setup_turns())
            dve.wait_ge(S["flips_read"], flips[0])
            dve.wait_ge(S["consts_ready"], 1)

            def s64(n):
                return small64[:, n, :]

            aR, aI, dt, expo, ang, mag, sn, shf, kk, rden, lb1, t0, t1_, fr, fi = (s64(n) for n in range(15))

            def exponential(out, x):
                own.step(v.tensor_scalar(kk, x, 1.0 / math.log(2.0), None, MUL))
                own.step(v.tensor_scalar(kk, kk, ROUND, None, ADD))
                own.step(v.tensor_scalar(kk, kk, ROUND, None, SUB))
                own.step(v.tensor_scalar(kk, kk, 127.0, -126.0, ALU.min, ALU.max))
                for c in LOG_2:
                    own.step(v.scalar_tensor_tensor(out=x, in0=kk, scalar=-c, in1=x, op0=MUL, op1=ADD))
                own.step(v.tensor_scalar(x, x, -1.0, 1.0, ALU.max, ALU.min))
                own.step(v.tensor_scalar(kk, kk, 127.0, 2.0 ** 23, ADD, MUL))
                own.step(v.tensor_copy(two_n[:], kk))
                own.step(v.tensor_scalar(out, x, 1.0 / math.factorial(8), 1.0 / math.factorial(7), MUL, ADD))
                for n in range(6, -1, -1):
                    own.step(v.tensor_tensor(out, out, x, MUL))
                    own.step(v.tensor_scalar(out, out, 1.0 / math.factorial(n), None, ADD))
                own.step(v.tensor_tensor(out, out, two_n[:].bitcast(F32), MUL))

            exponential(dt, log_dt[:])
            own.mark(v.tensor_tensor(expo, aR, dt, MUL))
            own.step(v.tensor_tensor(ang, aI, dt, MUL))
            own.step(v.tensor_scalar(kk, ang, 1.0 / (2.0 * math.pi), None, MUL))
            own.step(v.tensor_scalar(kk, kk, ROUND, None, ADD))
            own.step(v.tensor_scalar(kk, kk, ROUND, None, SUB))
            for c in TWO_PI:
                own.step(v.scalar_tensor_tensor(out=ang, in0=kk, scalar=-c, in1=ang, op0=MUL, op1=ADD))
            v.tensor_scalar(ang, ang, PI_IN, -PI_IN, ALU.min, ALU.max).then_inc(S["angle_ready"], 1)
            exponential(mag, expo)
            dve.wait_ge(S["prep_act"], 3)
            pR, pI = pows
            own.mark(v.memset(pR[:, :, 0], 1.0))
            own.mark(v.memset(pI[:, :, 0], 0.0))
            own.step(v.tensor_tensor(pI[:, :, 1], mag, sn, MUL))
            own.step(v.tensor_tensor(t0, shf, shf, MUL))
            own.step(v.tensor_scalar(t0, t0, -2.0, 1.0, MUL, ADD))
            own.step(v.tensor_tensor(pR[:, :, 1], mag, t0, MUL))
            scratch = [VT[:].rearrange("p g m -> p (g m)")[:, 0:4 * GROUPS], VT[:].rearrange("p g m -> p (g m)")[:, 4 * GROUPS:8 * GROUPS]]
            for n in (1, 2, 4):
                x, y = (z[:, 0:n * GROUPS].rearrange("p (g j) -> p g j", j=n) for z in scratch)

                def top(t):
                    return t[:, :, n:n + 1].to_broadcast([P, GROUPS, n])

                own.mark(v.tensor_tensor(x, pR[:, :, 1:n + 1], top(pR), MUL))
                own.step(v.tensor_tensor(y, pI[:, :, 1:n + 1], top(pI), MUL))
                own.step(v.tensor_tensor(pR[:, :, n + 1:2 * n + 1], x, y, SUB))
                own.mark(v.tensor_tensor(x, pR[:, :, 1:n + 1], top(pI), MUL))
                own.step(v.tensor_tensor(y, pI[:, :, 1:n + 1], top(pR), MUL))
                own.step(v.tensor_tensor(pI[:, :, n + 1:2 * n + 1], x, y, ADD))
            for s in range(CHUNK):
                own.mark(v.tensor_copy(revs[0][:, :, s], pR[:, :, CHUNK - 1 - s]))
                own.mark(v.tensor_copy(revs[1][:, :, s], pI[:, :, CHUNK - 1 - s]))
            own.mark(v.tensor_copy(lam8[:, 0, :], pR[:, :, CHUNK]))
            own.mark(v.tensor_copy(lam8[:, 1, :], pI[:, :, CHUNK]))
            own.mark(v.tensor_scalar(lam8[:, 2, :], pI[:, :, CHUNK], -1.0, None, MUL))
            own.mark(v.tensor_scalar(lb1, pR[:, :, 1], -1.0, None, ADD))
            own.mark(v.tensor_tensor(t0, aR, aR, MUL))
            own.step(v.tensor_tensor(t1_, aI, aI, MUL))
            own.step(v.tensor_tensor(t0, t0, t1_, ADD))
            own.step(v.reciprocal(rden, t0))
            own.mark(v.tensor_tensor(t0, lb1, aR, MUL))
            own.step(v.tensor_tensor(t1_, pI[:, :, 1], aI, MUL))
            own.step(v.tensor_tensor(t0, t0, t1_, ADD))
            own.step(v.tensor_tensor(fr, t0, rden, MUL))
            own.mark(v.tensor_tensor(t0, pI[:, :, 1], aR, MUL))
            own.step(v.tensor_tensor(t1_, lb1, aI, MUL))
            own.step(v.tensor_tensor(t0, t0, t1_, SUB))
            own.step(v.tensor_tensor(fi, t0, rden, MUL))
            own.mark(v.tensor_scalar(b2[:], b2[:], sign[:, 1:2], None, MUL))
            own.mark(v.tensor_scalar(c1[:], c1[:], sign[:, 0:1], None, MUL))
            own.step(v.tensor_scalar(c2[:], c2[:], -1.0, None, MUL))

            def over_n(z):
                return z.unsqueeze(2).to_broadcast([P, GROUPS, GC])

            own.mark(v.tensor_tensor(bb1[:], b1[:], over_n(fr), MUL))
            own.step(v.tensor_tensor(bt[:], b2[:], over_n(fi), MUL))
            own.step(v.tensor_tensor(bb1[:], bb1[:], bt[:], ADD))
            own.mark(v.tensor_tensor(bb2[:], b2[:], over_n(fr), MUL))
            own.step(v.tensor_tensor(bt[:], b1[:], over_n(fi), MUL))
            v.tensor_tensor(bb2[:], bb2[:], bt[:], SUB).then_inc(S["prep_dve"], 1)
            dve.wait_ge(S["prep_dve"], 1)

            with dve.Fori(0, BATCHES) as i:
                own.begin(i, 2)
                gs = ds(i * GB, GB)

                def blocks(z):
                    return z[:].rearrange("p g (s n) -> p g s n", n=GC)

                dve.wait_ge(S["w_flipped"], i + 1)
                for z, power, rows in ((V, revs[0], bb1), (VT, revs[1], bb2)):
                    ins = v.tensor_tensor(blocks(z), power[:, gs, :].unsqueeze(3).to_broadcast([P, GB, CHUNK, GC]),
                                          rows[:, gs, :].unsqueeze(2).to_broadcast([P, GB, CHUNK, GC]), MUL)
                    own.mark(ins)
                own.settle()
                v.tensor_tensor(V[:], V[:], VT[:], ADD).then_inc(S["v_ready"], 1)
                own.end(BATCHES)
                dve.wait_ge(S["v_ready"], i + 1)

            def modulate(k, shift, scale, high, low, ready, tmp):
                own.mark(v.tensor_scalar(tmp[:, 0:NP], xT[:, k, 0:NP], mod[:, scale + k, 0:1], mod[:, shift + k, 0:1], MUL, ADD))
                own.step(v.tensor_tensor(samples(tmp), samples(xT[:, k, :]), per_sample(mod[:, scale + k, 1:NC]), MUL))
                own.step(v.tensor_tensor(samples(tmp), samples(tmp), per_sample(mod[:, shift + k, 1:NC]), ADD))
                own.step(v.tensor_copy(high[:, k, :], tmp))
                v.tensor_tensor(low[:, k, :], tmp, high[:, k, :].bitcast(F32), SUB).then_inc(ready, 1)

            SH1, SC1, G1, SH2, SC2, G2 = (m * KD for m in range(MODS))
            dve.wait_ge(S["act_ada"], 2 + 2 * KD)
            own.step(v.tensor_scalar(mod[:, SC1:SC1 + KD, :], mod[:, SC1:SC1 + KD, :], 1.0, None, ADD))
            for k in range(KD):
                modulate(k, SH1, SC1, hH, hL, S["h_ready"], small64[:].rearrange("p a b -> p (a b)")[:, (k % 2) * T:(k % 2 + 1) * T])

            def split_low(n, cc, K):
                dve.wait_ge(S["hi_done"], n + 1)
                v.tensor_tensor(wL[cc % 2][:, 0:K, :], ring[cc][:, 0:K, :], wH[cc % 2][:, 0:K, :].bitcast(F32), SUB)\
                    .then_inc(S["split_done"], 1)

            def split_ahead(i, n0, cc, next_ks, own_ks):
                c = cc + 2
                if c < 4:
                    split_low(i * 4 + (n0 + c), c, own_ks[c])
                elif next_ks:
                    split_low(i * 4 + (n0 + c), c - 4, next_ks[c - 4])

            def start_stream(n0, ks):
                for c in range(2):
                    split_low(n0 + c, c, ks[c])

            start_stream(PROJ, [KD] * 4)

            def proj_pass(i, next_ks):
                for cc in range(4):
                    split_ahead(i, PROJ, cc, next_ks, [KD] * 4)

            with dve.Fori(0, KA - 1) as i:
                proj_pass(i, [KD] * 4)
            proj_pass(KA - 1, None)
            dve.wait_ge(S["act_ada"], 2 + MODS * KD)
            own.mark(v.tensor_scalar(mod[:, G1:G1 + KD, :], mod[:, G1:G1 + KD, :], 1.0, None, ADD))
            own.step(v.tensor_scalar(mod[:, SC2:, :], mod[:, SC2:, :], 1.0, None, ADD))
            f = flips[0]
            turns = list(proj_turns())
            read_turns(turns[0:12])
            dve.wait_ge(S["u_stored"], 32)
            read_turns(turns[12:])

            dve.wait_ge(S["k_stored"], 32)
            dve.wait_ge(S["bias_landed"], 16)
            new = sS[0:ST, PAGES, :]
            with dve.Fori(0, SB) as i:
                own.begin(i, 10)

                def read_page(p):
                    dve.wait_ge(S["k_flipped"], i * PAGES + (p + 3))
                    dve.wait_ge(S["scored"], i * PAGES + (p + 1))
                    v.tensor_copy(kTp[p % 2][:, 0:4, :].rearrange("p h k -> p (h k)"), bank[0][:]).then_inc(S["kt_dve"], 1)

                read_page(0)
                dve.wait_ge(S["pz_done"], i + 1)
                own.step(v.tensor_scalar(pz[:], bank[4][:, 0:384], SCALE, bias_h[:, ds(i, 1)], MUL, ADD))
                v.scalar_tensor_tensor(out=pe_[:], in0=pz[:], scalar=-1.0, in1=pz[:], op0=MUL, op1=ALU.min).then_inc(S["p_exp_in"], 1)
                read_page(1)
                read_page(2)
                dve.wait_ge(S["p_ln"], i + 1)
                own.step(v.scalar_tensor_tensor(out=pS[:], in0=pz[:], scalar=0.0, in1=pe_[:], op0=ALU.max, op1=ADD))
                v.scalar_tensor_tensor(out=pS[:], in0=masks[:], scalar=1.0, in1=pS[:], op0=ADD, op1=MUL).then_inc(S["p_s"], 1)
                read_page(3)
                read_page(4)
                dve.wait_ge(S["p_cs"], i + 1)
                own.step(v.tensor_tensor(pz[:], pz[:], bank[5][:, 0:384], SUB))
                v.scalar_tensor_tensor(out=pe_[:], in0=masks[:], scalar=1e30, in1=pz[:], op0=MUL, op1=ADD).then_inc(S["p_arg"], 1)
                for p in (5, 6, 7):
                    read_page(p)
                dve.wait_ge(S["p_pv"], i + 2)
                o = bank[4][:, 0:NP].unsqueeze(1)
                own.step(v.tensor_copy(attH[:, ds(i, 1), 0:NP], o))
                v.tensor_tensor(attL[:, ds(i, 1), 0:NP], o, attH[:, ds(i, 1), 0:NP].bitcast(F32), SUB).then_inc(S["att_p"], 1)

                dve.wait_ge(S["scored"], i * PAGES + (PAGES + 2))
                own.mark(v.scalar_tensor_tensor(out=sz[:, 0:PAGES, :], in0=bank[2][:].rearrange("p (a c) -> p a c", a=PAGES), scalar=SCALE,
                                                in1=bias_q[:].unsqueeze(1).to_broadcast([P, PAGES, HQ]), op0=MUL, op1=ADD))
                dve.wait_ge(S["zn_done"], i + 2)
                own.step(v.scalar_tensor_tensor(out=sz[0:ST, PAGES, :], in0=bank[7][0:ST, 0:HQ], scalar=SCALE, in1=bias_q[0:ST, :], op0=MUL, op1=ADD))
                v.scalar_tensor_tensor(out=se[:], in0=sz[:], scalar=-1.0, in1=sz[:], op0=MUL, op1=ALU.min).then_inc(S["s_e_in"], 1)
                dve.wait_ge(S["s_ln"], i + 1)
                own.step(v.scalar_tensor_tensor(out=sS[:], in0=sz[:], scalar=0.0, in1=se[:], op0=ALU.max, op1=ADD))
                v.scalar_tensor_tensor(out=new, in0=mask_new[:], scalar=1.0, in1=new, op0=ADD, op1=MUL).then_inc(S["s_s"], 1)
                dve.wait_ge(S["s_cs"], i + 1)
                own.mark(v.tensor_tensor(se[:, 0:PAGES, :], sz[:, 0:PAGES, :], bank[3][:].rearrange("p (a c) -> p a c", a=PAGES), SUB))
                own.step(v.tensor_tensor(sz[0:ST, PAGES, :], sz[0:ST, PAGES, :], bank[7][0:ST, HQ:2 * HQ], SUB))
                v.scalar_tensor_tensor(out=se[0:ST, PAGES, :], in0=mask_new[:], scalar=1e30, in1=sz[0:ST, PAGES, :], op0=MUL, op1=ADD)\
                    .then_inc(S["s_arg"], 1)
                dve.wait_ge(S["s_pv"], i + 2)
                o = bank[6][:, 0:HQ].rearrange("p (h q) -> p h q", q=ST)
                cols = ds(i * ST + NP, ST)
                own.step(v.tensor_copy(attH[:, :, cols], o))
                v.tensor_tensor(attL[:, :, cols], o, attH[:, :, cols].bitcast(F32), SUB).then_inc(S["att_s"], 1)
                own.end(SB)

            with dve.Fori(0, BATCHES) as i:
                dve.wait_ge(S["w1_landed"], i * 16 + 16)
                own.begin(i, 2)
                own.mark(v.tensor_scalar(W2[:, :, 0:GS], W1[:, :, GS:P], -1.0, None, MUL))
                v.tensor_copy(W2[:, :, GS:P], W1[:, :, 0:GS]).then_inc(S["w2_ready"], 1)
                dve.wait_ge(S["g_done"], i + 2)
                own.mark(v.tensor_copy(G[:, 0, ds(i * GB, GB), :], bank[5][:, 0:GB * CT].rearrange("p (g c) -> p g c", g=GB)))
                v.tensor_copy(G[:, 1, ds(i * GB, GB), :], bank[6][:, 0:GB * CT].rearrange("p (g c) -> p g c", g=GB)).then_inc(S["g_read"], 1)
                own.end(BATCHES)
            dve.wait_ge(S["g_read"], BATCHES + 1)
            own.step(v.memset(Z[:, :, :, 0], 0.0))
            read_turns(state_turns())
            dve.wait_ge(S["flips_read"], flips[0])
            own.step(v.tensor_scalar(h0[:, 1], h0[:, 1], sign[:, 1:2], None, MUL))
            l_re, l_im, l_neg = (lam8[:, n, :] for n in range(3))
            with dve.Fori(0, CP) as c:
                own.begin(c, 5)

                def state(n, half):
                    return Z[:, half, :, ds(c + n, 1)].rearrange("p g o -> p (g o)")

                for half in range(2):
                    own.mark(v.tensor_tensor(t1[:, half, :], state(0, half), l_re, MUL))
                    ins = v.tensor_tensor(t2[:, half, :], state(0, 1 - half), l_neg if half else l_im, MUL)
                    own.mark(ins)
                own.settle()
                own.step(v.tensor_tensor(t1[:], t1[:], t2[:], ADD))
                v.tensor_tensor(Z[:, :, :, ds(c + 1, 1)].rearrange("p v g o -> p v (g o)"), t1[:],
                                G[:, :, :, ds(c, 1)].rearrange("p v g o -> p v (g o)"), ADD).then_inc(S["state_step"], 1)
                dve.wait_ge(S["state_step"], c + 1)
                own.end(CP)

            def over_b(z):
                return z.unsqueeze(2).to_broadcast([P, GROUPS, SB])

            own.mark(v.tensor_copy(Z[:, 0, :, CP + 1:], h0[:, 0]))
            own.mark(v.tensor_tensor(zf[:], h0[:, 0], over_b(l_re), MUL))
            own.step(v.tensor_tensor(u1[:], h0[:, 1], over_b(l_im), MUL))
            own.step(v.tensor_tensor(zf[:], zf[:], u1[:], ADD))
            v.tensor_tensor(zf[:], zf[:], G[:, 0, :, CP:], ADD).then_inc(S["scanned"], 1)
            read_turns(final_state_turns())
            for c in range(KA):
                dve.wait_ge(S["ytk_turned"], c + 1)
                if c >= 2:
                    dve.wait_ge(S["y_gelu"], c - 1)
                v.scalar_tensor_tensor(out=ypre[c % 2][:], in0=projT[:, c, :], scalar=cw[:, 3 * 2 * JF + c:3 * 2 * JF + c + 1],
                                       in1=bank[4 + c % 4][:, 0:T], op0=MUL, op1=ADD).then_inc(S["y_pre"], 1)
                if c >= 1:
                    dve.wait_ge(S["y_gelu"], c)
                    own.step(v.tensor_copy(ygH[:, c - 1, :], ygl[(c - 1) % 2][:]))
                    v.tensor_tensor(ygL[:, c - 1, :], ygl[(c - 1) % 2][:], ygH[:, c - 1, :].bitcast(F32), SUB).then_inc(S["y_ready"], 1)
            c = KA
            dve.wait_ge(S["y_gelu"], c)
            own.step(v.tensor_copy(ygH[:, c - 1, :], ygl[(c - 1) % 2][:]))
            v.tensor_tensor(ygL[:, c - 1, :], ygl[(c - 1) % 2][:], ygH[:, c - 1, :].bitcast(F32), SUB).then_inc(S["y_ready"], 1)

            start_stream(GLU, ks_of["glu"])
            for m in range(KA):
                i, cc = m // 4, m % 4
                dve.wait_ge(S["y_ready"], KA)
                dve.wait_ge(acc_free[cc % 2], (GLU + m) // 2 + 2)
                dve.wait_ge(S["s_ready"], m)
                own.step(v.tensor_tensor(part[0][:], ygH[:, m, :].bitcast(F32), ygL[:, m, :].bitcast(F32), ADD))
                own.step(v.tensor_tensor(part[0][:], part[0][:], gate[cc % 2][:], MUL))
                own.step(v.tensor_copy(sH[:, m, :], part[0][:]))
                v.tensor_tensor(sL[:, m, :], part[0][:], sH[:, m, :].bitcast(F32), SUB).then_inc(S["s_ready"], 1)
                split_ahead(i, GLU, cc, ks_of["glu"] if i == 0 else ks_of["merge"], ks_of["glu"])

            def merge_pass(i, next_ks):
                for cc in range(4):
                    if cc % 2:
                        h = cc // 2
                        dve.wait_ge(acc_free[0], i * 2 + (MERGE // 2 + h + 2))
                        dve.wait_ge(S["chunk_done"], i * 4 + (MERGE + cc + 3))
                        v.tensor_tensor(part[h][:], bank[1][:, 0:T], gate[h][:], MUL).then_inc(acc_free[1], 1)
                    if cc == 3:
                        dve.wait_ge(acc_free[1], i * 2 + (MERGE // 2 + 3))
                        v.tensor_tensor(merged[:, ds(i, 1), :].rearrange("p o t -> p (o t)"), part[0][:], part[1][:], ADD).then_inc(S["merged_ready"], 1)
                    split_ahead(i, MERGE, cc, next_ks, ks_of["merge"])

            passes(dve, "merge", None, 0, merge_pass)
            dve.wait_ge(S["merged_ready"], KD)
            dve.wait_ge(S["chunk_done"], OUT + 2)
            for k in range(KD):
                own.step(v.tensor_copy(mH[:, k, :], merged[:, k, :]))
                v.tensor_tensor(mL[:, k, :], merged[:, k, :], mH[:, k, :].bitcast(F32), SUB).then_inc(S["m_ready"], 1)

            def residual(src, m, gain, ready, free=None):
                r = res[0]
                col = mod[:, ds(m + gain, 1), :].rearrange("p o c -> p (o c)")
                own.mark(v.tensor_scalar(r[:, 0:NP], src[:, 0:NP], col[:, 0:1], None, MUL))
                ins = v.tensor_tensor(samples(r[:]), samples(src), per_sample(col[:, 1:NC]), MUL)
                if free:
                    ins.then_inc(free[0], 1)
                    own.settle()
                    dve.wait_ge(free[0], free[1])
                else:
                    own.step(ins)
                x = xT[:, ds(m, 1), :].rearrange("p o t -> p (o t)")
                v.scalar_tensor_tensor(out=x, in0=x, scalar=ALPHA, in1=r[:], op0=MUL, op1=ADD).then_inc(ready, 1)

            def out_pass(i, next_ks):
                for cc in range(4):
                    dve.wait_ge(S["chunk_done"], i * 4 + (OUT + cc + 3))
                    dve.wait_ge(S["x_pre"], i * 4 + (cc + 1))
                    residual(bank[cc % 2][:, 0:T], i * 4 + cc, G1, S["x_pre"], (acc_free[cc % 2], i * 2 + (OUT // 2 + cc // 2 + 2)))
                    split_ahead(i, OUT, cc, next_ks, ks_of["out"])

            passes(dve, "out", own, 4, out_pass)

            def layer_norm(nth, g0, b0):
                dve.wait_ge(S["mean_done"], nth + 1)
                own.step(v.tensor_copy(mu[:], bank[2][:, 0:T]))
                for k in range(KD):
                    v.tensor_tensor(xT[:, k, :], xT[:, k, :], mu[:], SUB).then_inc(S["centred"], 1)
                dve.wait_ge(S["var_done"], nth + 1)
                v.tensor_scalar(var[:], bank[3][:, 0:T], EPS, None, ADD).then_inc(S["var_ready"], 1)
                dve.wait_ge(S["sd_ready"], nth + 1)
                own.step(v.reciprocal(rstd[:], sd[:]))
                own.step(v.tensor_tensor(newton[:], rstd[:], rstd[:], MUL))
                own.step(v.tensor_tensor(newton[:], newton[:], var[:], MUL))
                own.step(v.tensor_scalar(newton[:], newton[:], -0.5, 1.5, MUL, ADD))
                own.step(v.tensor_tensor(rstd[:], rstd[:], newton[:], MUL))
                for k in range(KD):
                    own.step(v.tensor_tensor(xT[:, k, :], xT[:, k, :], rstd[:], MUL))
                    ins = v.tensor_scalar(xT[:, k, :], xT[:, k, :], par[:, g0 + k:g0 + k + 1], par[:, b0 + k:b0 + k + 1], MUL, ADD)
                    if nth:
                        ins.then_inc(S["normed"], 1)
                    else:
                        own.step(ins)
                        modulate(k, SH2, SC2, hH, hL, S["h2_ready"], res[k % 2][:])

            dve.wait_ge(S["state_stored"], 64)
            read_turns(conv_state_turns())
            layer_norm(0, 96, 112)

            done, pairs = 0, 0
            j0 = 0
            for q, nj in enumerate(QUARTERS):
                n0 = first_of[f"up{q}"]

                def up_pass(i, next_ks):
                    for cc in range(4):
                        split_ahead(i, n0, cc, next_ks, ks_of["up0"])
                        n = i * 4 + (done + cc)
                        ch = i * 2 + (j0 + cc // 2 + (cc % 2) * JF)
                        dst = cvG if cc % 2 else cvV
                        dve.wait_ge(S["halo"], n + 1)
                        dve.wait_ge(S["conv_ev"], n + 1)
                        dve.wait_ge(acc_free[cc % 2], i * 2 + (n0 // 2 + cc // 2 + 2))
                        e = ext[cc]
                        own.step(v.tensor_scalar(dst[:, 0:EXT - 2], e[:, 0:EXT - 2], cw[:, ds(ch, 1)], par[:, ds(ch + P, 1)], MUL, ADD))
                        own.step(v.scalar_tensor_tensor(out=dst[:, 0:EXT - 2], in0=e[:, 1:EXT - 1], scalar=cw[:, ds(ch + 2 * JF, 1)], in1=dst[:, 0:EXT - 2], op0=MUL, op1=ADD))
                        v.scalar_tensor_tensor(out=dst[:, 0:EXT - 2], in0=e[:, 2:EXT], scalar=cw[:, ds(ch + 4 * JF, 1)],
                                               in1=dst[:, 0:EXT - 2], op0=MUL, op1=ADD).then_inc(S["ext_read"], 1)
                        dve.wait_ge(S["ext_read"], n + 5)
                        if cc % 2:
                            j = i * 2 + cc // 2
                            dve.wait_ge(S["gelu_done"], i * 2 + (pairs + cc // 2 + 1))
                            dve.wait_ge(S["f_ready"], i * 2 + (pairs + cc // 2 + 1))
                            own.mark(v.tensor_tensor(prod[:, 0:NP], cvV[:, 0:NP], cvG[:, 0:NP], MUL))
                            own.step(v.tensor_tensor(samples(prod[:]), late(cvV), late(cvG), MUL))
                            own.step(v.tensor_copy(fH[:, ds(j, 1), :], prod[:].unsqueeze(1)))
                            v.tensor_tensor(fL[:, ds(j, 1), :], prod[:].unsqueeze(1), fH[:, ds(j, 1), :].bitcast(F32), SUB).then_inc(S["f_ready"], 1)

                passes(dve, f"up{q}", own, 14, up_pass)
                done += 2 * nj
                pairs += nj
                n0 = first_of[f"down{q}"]

                def down_pass(i, next_ks):
                    for cc in range(4):
                        dve.wait_ge(S["chunk_done"], i * 4 + (n0 + cc + 3))
                        y = yacc[:, ds(i * 4 + cc, 1), :].rearrange("p o t -> p (o t)")
                        acc = bank[cc % 2][:, 0:T]
                        ins = v.tensor_tensor(y, y, acc, ADD) if q else v.tensor_copy(y, acc)
                        ins.then_inc(acc_free[cc % 2], 1)
                        split_ahead(i, n0, cc, next_ks, ks_of[f"down{q}"])

                passes(dve, f"down{q}", None, 0, down_pass)
                j0 += nj
            for s in acc_free:
                dve.wait_ge(s, (FFN + sum(2 * nj + KD for nj in QUARTERS)) // 2 + 1)
            for m in range(KD):
                residual(yacc[:, m, :], m, G2, S["x_pre"])
                dve.wait_ge(S["x_pre"], KD + m + 2)
            read_turns(rows_out_turns())
            layer_norm(1, P + 88, P + 104)
            read_turns(y_turns())


_INS = ["x_prompt", "x_sample", "cache_k", "cache_v", "state_ssm_re", "state_ssm_im", "state_conv", "page_table",
        "c_prompt", "c_sample", "w_ada", "b_ada", "w_in", "w_att_br", "w_ssm_br", "w_out", "sb_bias",
        "ssm_a_re", "ssm_a_im", "ssm_log_dt", "ssm_b_re", "ssm_b_im", "ssm_c_re", "ssm_c_im", "ssm_d",
        "w_glu", "b_glu", "ln1_g", "ln1_b", "w_up", "conv_w", "conv_b", "w_down", "ln2_g", "ln2_b"]
_OUTS = [(1, NP, D), (SB, ST, D), (1, 1, NP, HEADS, HD), (1, 1, NP, HEADS, HD), (1, 1, GROUPS, GS), (1, 1, GROUPS, GS),
         (1, 1, 2, 2 * FF), (1, SB, ST, HEADS, HD), (1, SB, ST, HEADS, HD), (1, SB, GROUPS, GS), (1, SB, GROUPS, GS),
         (1, SB, 2, 2 * FF)]


def kernel(**inputs):
    import numpy as np
    import concourse.bacc as bacc
    from concourse.bass_utils import run_bass_kernel_spmd

    nc = bacc.Bacc("TRN2", target_bir_lowering=False, num_devices=1)
    arrays, args = {}, []
    for name in _INS:
        a = np.ascontiguousarray(inputs[name])
        arrays[f"in_{name}"] = a
        args.append(nc.dram_tensor(f"in_{name}", a.shape, mybir.dt.from_np(a.dtype), kind="ExternalInput").ap())
    for i, shape in enumerate(_OUTS):
        args.append(nc.dram_tensor(f"out_{i}", shape, F32, kind="ExternalOutput").ap())
    hybrid_step(nc, *args)
    r = run_bass_kernel_spmd(nc, [arrays], core_ids=[0])
    return tuple(r.results[0][f"out_{i}"] for i in range(len(_OUTS)))
```

```python
import math

import concourse.bass as bass
from concourse import mybir

P = 128
F32 = mybir.dt.float32
F32R = mybir.dt.float32r
I32 = mybir.dt.int32
ALU = mybir.AluOpType
ACT = mybir.ActivationFunctionType
ds = bass.ds

D = 2048
NP = 256
SB, ST = 8, 8
T = NP + SB * ST
HEADS, HD = 8, 128
AW = HEADS * HD
SW = D - AW
GROUPS, GC, GS = 64, 16, 64
FF = 5632
PAGE, PAGES = 128, 8
KD = D // P
KA = AW // P
JF = FF // P
MODS = 6
NC = 1 + SB
CHUNK = 8
CP = NP // CHUNK
CT = CP + SB
GB = P // GC
BATCHES = GROUPS // GB
ALPHA = 2.0 ** 0.25
EPS = 1e-5
SCALE = HD ** -0.5
EXT = 2 + NP + SB * (2 + ST)
QUARTERS = [12, 12, 10, 10]

TWO_PI = (6.28125, 0.0019350051879882812, 2.0 * math.pi - 6.28125 - 0.0019350051879882812)
ROUND = 1.5 * 2.0 ** 23
PI_IN = 3.1415925
LOG_2 = (0.693359375, math.log(2.0) - 0.693359375)

RING = 4
BLOCK = 512
KSLOTS = 3


class Own:

    def __init__(self, eng, sem):
        self.eng, self.sem, self.count, self.index = eng, sem, 0, None

    def begin(self, index, per_pass, first=0):
        self.index, self.per_pass, self.k, self.first = index, per_pass, 0, first

    def end(self, passes):
        assert self.k == self.per_pass, (self.k, self.per_pass)
        self.count, self.index = self.count + passes * self.per_pass, None

    def mark(self, instruction):
        instruction.then_inc(self.sem, 1)
        if self.index is None:
            self.count += 1
        else:
            self.k += 1

    def settle(self):
        at = self.count if self.index is None else self.index * self.per_pass + (self.count - self.first * self.per_pass + self.k)
        self.eng.wait_ge(self.sem, at)

    def step(self, instruction):
        self.mark(instruction)
        self.settle()


def hybrid_step(nc, x_prompt, x_sample, cache_k, cache_v, state_ssm_re, state_ssm_im, state_conv, page_table,
                c_prompt, c_sample, w_ada, b_ada, w_in, w_att_br, w_ssm_br, w_out, sb_bias,
                ssm_a_re, ssm_a_im, ssm_log_dt, ssm_b_re, ssm_b_im, ssm_c_re, ssm_c_im, ssm_d,
                w_glu, b_glu, ln1_g, ln1_b, w_up, conv_w, conv_b, w_down, ln2_g, ln2_b,
                y_prompt, y_sample, k_prompt, v_prompt, ssm_re_prompt, ssm_im_prompt, conv_prompt,
                k_sample, v_sample, ssm_re_sample, ssm_im_sample, conv_sample):
    n_phys = cache_k.shape[1]
    S = {}

    def sem(name):
        S[name] = nc.alloc_semaphore(name)
        return S[name]

    base = (nc.sbuf_base + 127) // 128 * 128

    def at(name, shape, offset, dtype=F32):
        return nc.alloc_sbuf_tensor_at(name, shape, dtype, offset=base + offset)

    CH = T * 4
    small, r_x, r_h = 0, 16384, 16384 + KD * CH
    r_ring = r_h + 2 * KD * CH
    r_split = r_ring + RING * KD * P * 4
    r_u = r_split + 4 * KD * P * 4
    r_q, r_k, r_v = r_u + KA * CH, r_u + 2 * KA * CH, r_u + 3 * KA * CH
    r_vtok = r_v + KA * CH
    r_attl = r_vtok + 3 * AW * 4
    r_tail = r_attl + KA * CH

    mod = at("mod", [P, MODS * KD, NC], small)
    par = at("par", [P, 256], small + 3456)
    cw = at("cw", [P, 3 * 2 * JF + KA], small + 4480)
    ident = at("ident", [P, P], small + 5568)
    mean_of = at("mean_of", [P, P], small + 6080)
    later = at("later", [P, P], small + 6592)
    ones = at("ones", [P, P], small + 7104)
    r_small2 = small + 7616
    masks = at("masks", [P, 384], small + 13312)
    lam8 = at("lam8", [P, 3, GROUPS], small + 14848)
    bias_h = at("bias_h", [P, HEADS], small + 15616)
    sign = at("sign", [P, 2], small + 15648)
    pages = at("pages", [1, SB * PAGES], small + 15680, I32)
    mask_new = at("mask_new", [ST, HEADS * ST], small + 15936)

    xT = at("xT", [P, KD, T], r_x)
    hH, hL = (at(n, [P, KD, T], r_h + i * KD * CH, F32R) for i, n in enumerate(("hH", "hL")))
    ring = [at(f"ring{i}", [P, KD, P], r_ring + i * KD * P * 4) for i in range(RING)]
    wH = [at(f"wH{i}", [P, KD, P], r_split + 2 * i * KD * P * 4, F32R) for i in range(2)]
    wL = [at(f"wL{i}", [P, KD, P], r_split + (2 * i + 1) * KD * P * 4, F32R) for i in range(2)]
    wH.append(at("wH2", [P, KD, P], r_vtok, F32R))
    wL.append(at("wL2", [P, KD, P], r_vtok + KD * P * 4, F32R))
    projT = at("projT", [P, 4 * KA, T], r_u)

    xrows = at("xrows", [P, 3, D], r_h)
    crows = at("crows", [NC, D], r_h + 24576)
    csil = at("csil", [NC, D], r_h + 32768)
    b_raw = at("b_raw", [GROUPS, 3, GS * GC], r_u + 8704)
    c_raw = at("c_raw", [GROUPS, GC, 3, GS], r_u + 8704 + 12288)
    zeros = at("zeros", [112, AW], r_u + 8704 + 24576 + 512)
    r_tail2 = r_vtok + 16384
    pr = at("pr", [P, 2, P], r_tail2)
    prw = at("prw", [2 * JF, 3, P], r_tail2 + 1024)
    prd = at("prd", [KA, P], r_tail2 + 2560)
    a_raw = at("a_raw", [GROUPS, 2, P], r_tail2 + 3072)
    log_dt = at("log_dt", [P, GROUPS], r_tail2 + 4096)
    small64 = at("small64", [P, 20, GROUPS], r_tail2 + 4352)
    two_n = at("two_n", [P, GROUPS], r_tail2 + 4352 + 5120 + 576, I32)
    cT = at("cT", [P, KD, NC], r_tail2 + 4352 + 5120)
    cHL = at("cHL", [P, KD, 2 * NC], r_small2, F32R)
    ada_rows = at("ada_rows", [2 * NC, BLOCK], r_small2 + 1152)
    add_up = at("add_up", [2 * NC, NC], r_small2 + 3200)
    pows = [at(f"pow{n}", [P, GROUPS, CHUNK + 1], r_u + i * 2304) for i, n in enumerate(("R", "I"))]
    revs = [at(f"rev{n}", [P, GROUPS, CHUNK], r_u + 4608 + i * 2048) for i, n in enumerate(("R", "I"))]
    b1, b2, c1, c2 = (at(n, [P, GROUPS, GC], r_vtok + i * 4096) for i, n in enumerate(("b1", "b2", "c1", "c2")))
    bb1, bb2, bt = (at(n, [P, GROUPS, GC], r_h + 24576 + i * 4096) for i, n in enumerate(("bb1", "bb2", "bt")))
    V, VT, PT, PX, P_, w1s = (at(n, [P, GB, P], r_u + 8704 + i * 4096)
                              for i, n in enumerate(("V", "VT", "PT", "PX", "Pm", "w1s")))
    o_s = at("o_s", [P, P], r_u + 8704 + 6 * 4096)

    vtok = at("vtok", [P, 3, AW], r_vtok)
    stage = at("stage", [P, 3, AW], r_attl)

    vpage = [at(f"vpage{i}", [P, AW], r_ring + i * 4096) for i in range(PAGES)]
    kpage = [at(f"kpage{i}", [P, AW], o) for i, o in enumerate((r_split, r_split + 4096, r_vtok + 2 * AW * 4))]
    kTp = [at(f"kTp{i}", [P, HEADS, PAGE], r_split + 8192 + i * 4096) for i in range(2)]
    HQ = HEADS * ST
    sz, se, sS, sR = (at(n, [P, PAGES + 1, HQ], r_split + 16384 + i * 2304) for i, n in enumerate(("sz", "se", "sS", "sR")))
    pz, pe_, pS = (at(n, [P, 384], r_split + 25600 + i * 1536) for i, n in enumerate(("pz", "pe_", "pS")))
    q_block = at("q_block", [P, HEADS * (HQ + ST)], r_split + 30208)
    z_rows = at("z_rows", [HQ, PAGES, PAGE], r_tail)
    zn_rows = at("zn_rows", [HQ, ST], r_small2 + 5120)
    o_rows = at("o_rows", [ST, AW], r_split + 16384 + 2 * 2304)
    kh = at("kh", [P, NP], r_small2 + 4096)
    vh = at("vh", [P, 2, HD], r_tail + 4096)
    bias_q = at("bias_q", [P, HQ], r_split + 32512)
    vnew = at("vnew", [ST, AW], r_small2)
    attH, attL = at("attH", [P, KA, T], r_v, F32R), at("attL", [P, KA, T], r_attl, F32R)

    U = at("U", [P, GROUPS, CT], r_q)
    G = at("G", [P, 2, GROUPS, CT], r_ring)
    Z = at("Z", [P, 2, GROUPS, CT + 1], r_ring + 20480)
    r_ssm = r_ring + 20480 + 20992
    W1 = at("W1", [P, GB, P], r_ssm)
    W2 = at("W2", [P, GB, P], r_ssm + 4096)
    Uraw = at("Uraw", [CT, CHUNK, P], r_ssm + 8192)
    Ug = at("Ug", [CT, GB, P], r_ssm + 12288)
    Kt = at("Kt", [P, CHUNK, P], r_ssm)
    Pt = at("Pt", [P, GB, P], r_ssm + 4096)
    Yt = at("Yt", [CT, CHUNK, GB, GC], r_ssm + 8192)
    Us = at("Us", [P, GB, CT], r_ssm + 12288)
    Hs = at("Hs", [P, GB, CT], r_ssm + 12288 + 1280)
    h0raw = at("h0raw", [GROUPS, SB, 3, GS], r_k)
    h0 = at("h0", [P, 2, GROUPS, SB], r_vtok)
    t1 = at("t1", [P, 2, GROUPS], r_vtok + 4096)
    t2 = at("t2", [P, 2, GROUPS], r_vtok + 4096 + 512)
    u1 = at("u1", [P, GROUPS, SB], r_vtok + 5120)
    zf = at("zf", [P, GROUPS, SB], r_vtok + 7168)
    fin = at("fin", [GROUPS, NC, P], r_small2)
    ytk = at("ytk", [P, 3, SW], r_ring)
    ypre = [at(f"ypre{i}", [P, T], r_vtok + i * CH) for i in range(2)]
    ygl = [at(f"ygl{i}", [P, T], r_vtok + (2 + i) * CH) for i in range(2)]

    ygH, ygL = at("ygH", [P, KA, T], r_q, F32R), at("ygL", [P, KA, T], r_k, F32R)
    sH, sL = at("sH", [P, KA, T], r_u, F32R), at("sL", [P, KA, T], r_vtok, F32R)
    merged = at("merged", [P, KD, T], r_q)
    gate = [at(f"gate{i}", [P, T], r_tail + i * CH) for i in range(2)]
    part = [at(f"part{i}", [P, T], r_tail + (2 + i) * CH) for i in range(2)]
    mH, mL = (at(n, [P, KD, T], r_h + i * KD * CH, F32R) for i, n in enumerate(("mH", "mL")))

    centred_sq = at("centred_sq", [P, KD, T], r_u)
    mu, var, sd, rstd, newton = (at(n, [P, T], r_u + (KD + i) * CH) for i, n in enumerate(("mu", "var", "sd", "rstd", "newton")))
    res = [at(f"res{i}", [P, T], r_u + (KD + 5 + i) * CH) for i in range(2)]

    conv_raw = at("conv_raw", [2 * JF, SB * 2, P], r_u + (KD + 7) * CH)
    conv_st = at("conv_st", [P, SB * 2, 2 * JF], r_small2)
    fH, fL = (at(n, [P, QUARTERS[0], T], r_u + i * QUARTERS[0] * CH, F32R) for i, n in enumerate(("fH", "fL")))
    yacc = at("yacc", [P, KD, T], r_u + 24 * CH)
    r_f, EB = r_u + 40 * CH, (EXT * 4 + 31) // 32 * 32
    ext = [at(f"ext{i}", [P, EXT], r_f + i * EB) for i in range(4)]
    cvV, cvG = (at(n, [P, EXT], r_f + (4 + i) * EB) for i, n in enumerate(("cvV", "cvG")))
    prod = at("prod", [P, T], r_f + 6 * EB)
    rows_out = at("rows_out", [P, NC * 2, 2 * JF], r_f + 6 * EB + CH)
    rows_t = at("rows_t", [2 * JF, NC * 2, P], r_h)
    ytok = at("ytok", [P, 3, D], r_ring)

    bank = [nc.alloc_psum_tensor(f"bank{i}", [P, 512], F32) for i in range(8)]

    u_tok = nc.dram_tensor("u_tok", (T, SW), F32).ap()
    y_tok = nc.dram_tensor("y_tok", (T, SW), F32).ap()
    w1_d = nc.dram_tensor("w1_d", (BATCHES, P, GB * P), F32).ap()
    p_d = nc.dram_tensor("p_d", (BATCHES, P, GB * P), F32).ap()
    taps_d = nc.dram_tensor("taps_d", (P + 112, SW), F32).ap()

    for name in ("c_landed x_landed params_landed ssm_landed pages_landed silu_ready ident_ready consts_ready "
                 "flipped flips_read ada_copied ada_turned ada_mod prep_act prep_dve v_ready w_flipped w_read "
                 "w1_stored taps_stored p_stored zeros_stored p_ready mod_ready h_ready hi_done split_done chunk_done own_act "
                 "own_dve own_pool ytk_turned proj_ready u_stored v_stored k_stored vtok_read "
                 "head_staged pz_done state_step bias_landed carried w_saved y_saved p_exp_in p_ln p_s p_cs p_arg p_w p_pv att_p q_staged z_copied zn_copied z_turned pv_rows o_act o_dve vnew_landed "
                 "k_flipped kt_dve kt_act scored s_z s_e_in s_ln s_s s_r s_cs s_arg s_w s_pv att_s zn_done "
                 "uraw_landed w1_landed ug_ready w2_ready ug_flipped u_ready g_done g_read h0_landed scanned "
                 "kt_landed pt_landed us_ready y_done y_read y_stored state_stored ytk_landed y_pre y_gelu y_ready "
                 "glu_gate s_ready m_gate m_read merged_ready m_hi m_ready x_pre mean_done centred squared var_done var_ready "
                 "sd_ready rstd_ready normed h2_ready conv_landed halo conv_ev gelu_done f_ready ext_read rows_ready down_ready "
                 "rows_stored y_out angle_ready c_split bias_spread").split():
        sem(name)
    ring_landed = [sem(f"ring_landed{i}") for i in range(RING)]
    kpage_landed = [sem(f"kpage_landed{i}") for i in range(KSLOTS)]
    vpage_landed = [sem(f"vpage_landed{i}") for i in range(PAGES)]
    acc_free = [sem(f"acc_free{i}") for i in range(2)]

    UNITS = D // BLOCK
    ADA1, PROJ = 0, 2 * UNITS * UNITS
    UNITS_LEFT = MODS * UNITS * UNITS - PROJ
    GLU = PROJ + 4 * KA + UNITS_LEFT
    MERGE, OUT = GLU + KA, GLU + KA + 4 * KD
    FFN = OUT + KD
    stages = [("glu", GLU, KA // 4, [KA] * 4), ("merge", MERGE, KD, [KD, KA, KD, KA]),
              ("out", OUT, KD // 4, [KD] * 4)]
    def nth_pair(n):
        return (n - (GLU - 4 * KA)) // 2

    items = [("unit", 0), ("unit", 1), ("chunk", 0), ("unit", 2), ("unit", 3), ("chunk", 1),
             ("unit", 4), ("unit", 5), ("chunk", 2), ("unit", 6), ("unit", 7), ("chunk", 3)]
    ITEMS = len(items)
    n0, j0 = FFN, 0
    for q, nj in enumerate(QUARTERS):
        stages.append((f"up{q}", n0, nj // 2, [KD] * 4))
        stages.append((f"down{q}", n0 + 2 * nj, KD // 4, [nj] * 4))
        n0, j0 = n0 + 2 * nj + KD, j0 + nj
    ks_of = {s[0]: s[3] for s in stages}
    first_of = {s[0]: s[1] for s in stages}
    passes_of = {s[0]: s[2] for s in stages}
    next_of = {a[0]: b[0] for a, b in zip(stages, stages[1:])}

    w_in_d = w_in[0].rearrange("(k p) c -> p k c", p=P)
    w_ada_d = w_ada[0].rearrange("(u k p) c -> u p k c", p=P, u=UNITS)
    w_att_d = w_att_br[0].rearrange("(k p) c -> p k c", p=P)
    w_ssm_d = w_ssm_br[0].rearrange("(k p) c -> p k c", p=P)
    w_glu_d = w_glu[0].rearrange("(k p) c -> p k c", p=P)
    w_out_d = w_out[0].rearrange("(k p) c -> p k c", p=P)
    w_up_d = w_up[0].rearrange("(k p) c -> p k c", p=P)
    w_down_d = w_down[0].rearrange("(k p) c -> p k c", p=P)

    def wide(t):
        return t[:].rearrange("p k c -> p (k c)").rearrange("p (k c) -> p k c", c=BLOCK)

    def last_in_slot(p):
        return p - KSLOTS if p >= KSLOTS else max(range(p, PAGES, KSLOTS)) - PAGES

    def alone(eng):
        eng.sem_inc(S["carried"], 1)

    def passes(eng, stage, own, per_pass, body):
        n = passes_of[stage]
        with eng.Fori(0, n - 1) as i:
            if own:
                own.begin(i, per_pass)
            body(i, ks_of[stage])
            if own:
                own.end(n - 1)
        body(n - 1, ks_of[next_of[stage]] if stage in next_of else None)

    def samples(ap):
        return ap[:, NP:T].rearrange("p (b t) -> p b t", b=SB)

    def late(t):
        return t[:, NP + 2:EXT].rearrange("p (b t) -> p b t", b=SB)[:, :, 0:ST]

    def per_sample(ap):
        return ap.unsqueeze(2).to_broadcast([P, SB, ST])

    def setup_turns():
        yield [(csil[0:NC, k * P:(k + 1) * P], NC) for k in range(KD)], P, cT[:].rearrange("p k c -> p (k c)")
        yield [(pr[:, i, :], P) for i in range(2)], P, par[:]
        yield [(prw[:, i, :], 2 * JF) for i in range(3)] + [(prd[:], KA)], P, cw[:]
        yield [(a_raw[:, i, :], GROUPS) for i in range(2)], P, small64[:, 0:2, :]
        for dst, v in ((b1, 0), (b2, 1)):
            for half in range(2):
                src = b_raw[:].rearrange("g v (p n) -> g (v p) n", n=GC)
                yield ([(src[:, v * GS:v * GS + P, 8 * half + n], GROUPS) for n in range(8)], P,
                       dst[:].rearrange("p g n -> p n g")[:, 8 * half:8 * half + 8, :])
        for dst, v in ((c1, 0), (c2, 1)):
            for half in range(2):
                src = c_raw[:].rearrange("g n v p -> g n (v p)")
                yield ([(src[:, 8 * half + n, v * GS:v * GS + P], GROUPS) for n in range(8)], P,
                       dst[:].rearrange("p g n -> p n g")[:, 8 * half:8 * half + 8, :])
        for k in range(KD):
            yield ([(xrows[0:min(P, T - t * P), t, k * P:(k + 1) * P], min(P, T - t * P)) for t in range(3)], P, xT[:, k, :])

    def proj_turns():
        for first, dst in ((0, stage), (3 * KA, vtok), (2 * KA, stage)):
            for half in range(2):
                for t in range(3):
                    rows = min(P, T - t * P)
                    yield ([(projT[:, first + 4 * half + c, t * P:t * P + rows], P) for c in range(4)], rows,
                           dst[0:rows, t, half * 512:half * 512 + 512])

    def state_turns():
        for v in range(2):
            yield ([(h0raw[:].rearrange("g b v p -> g b (v p)")[:, b, v * GS:v * GS + P], GROUPS) for b in range(SB)], P,
                   h0[:, v, :, :].rearrange("p g b -> p b g"))

    def final_state_turns():
        sources = [Z[:, 0, :, CP]] + [zf[:, :, b] for b in range(SB)]
        for first in (0, 4, 8):
            part_ = sources[first:first + 4]
            yield [(s, P) for s in part_], GROUPS, fin[:, first:first + len(part_), :]

    def conv_state_turns():
        for first in range(0, SB * 2, 4):
            yield ([(conv_raw[:, first + r, :], 2 * JF) for r in range(4)], P, conv_st[:, first:first + 4, :])

    def rows_out_turns():
        for first in range(0, NC * 2, 4):
            n = min(4, NC * 2 - first)
            yield [(rows_out[:, first + r, :], P) for r in range(n)], 2 * JF, rows_t[:, first:first + n, :]

    def y_turns():
        for quarter in range(4):
            for t in range(3):
                rows = min(P, T - t * P)
                yield ([(xT[:, 4 * quarter + c, t * P:t * P + rows], P) for c in range(4)], rows,
                       ytok[0:rows, t, quarter * 512:(quarter + 1) * 512])

    def width(sources):
        return sum(w for _, w in sources)

    rows_copied = []
    block = nc.Block()
    with block:

        @block.sync
        def _(sp):
            sp.dma_start(crows[0:1, :], c_prompt).then_inc(S["c_landed"], 16)
            sp.dma_start(crows[1:NC, :], c_sample).then_inc(S["c_landed"], 16)

            def load(n, s, K, src):
                sp.wait_ge(S["split_done"], n + 1)
                alone(sp)
                sp.dma_start(ring[s][:, 0:K, :], src).then_inc(ring_landed[s], 16)

            def load_unit(n, s, block_no, unit):
                sp.wait_ge(S["split_done"], n + 1)
                alone(sp)
                sp.dma_start(wide(ring[s]), w_ada_d[unit][:, :, ds(block_no * BLOCK, BLOCK)]).then_inc(ring_landed[s], 16)

            lp = S["params_landed"]
            for a, b in ((0, b_ada), (96, ln1_g), (112, ln1_b)):
                n = b.shape[1] // P
                sp.dma_start(pr[a:a + n, 0, :], b[0].rearrange("(r c) -> r c", c=P)).then_inc(lp, 16)
            for a, b in ((0, conv_b), (88, ln2_g), (104, ln2_b), (120, b_glu)):
                n = b.shape[1] // P
                sp.dma_start(pr[a:a + n, 1, :], b[0].rearrange("(r c) -> r c", c=P)).then_inc(lp, 16)
            sp.dma_start(prw[:], conv_w[0].rearrange("i (r c) -> r i c", c=P)).then_inc(lp, 16)
            sp.dma_start(prd[:], ssm_d[0].rearrange("(r c) -> r c", c=P)).then_inc(lp, 16)
            with sp.Fori(0, 2 * UNITS) as i:
                for u in range(UNITS):
                    load_unit(i * UNITS + u, u, i, u)

            def proj_pass(i, column):
                for x, (kind, m) in enumerate(items):
                    if kind == "unit":
                        load_unit(i * ITEMS + (PROJ + x), x % RING, i * 2 + (2 * UNITS + m // UNITS), m % UNITS)
                    else:
                        load(i * ITEMS + (PROJ + x), x % RING, KD, w_in_d[:, :, ds(column + m * P, P)])

            with sp.Fori(0, 2) as i:
                proj_pass(i, i * (4 * P) + 3 * AW)
            with sp.Fori(2, 8) as i:
                proj_pass(i, i * (4 * P) - 2 * 4 * P)

            sp.dma_start(pages[:], page_table.rearrange("b n -> (b n)").unsqueeze(0)).then_inc(S["pages_landed"], 16)
            sp.wait_ge(S["pages_landed"], 16)
            sp.wait_ge(S["chunk_done"], 2 + GLU)
            sp.wait_ge(S["v_stored"], 32)
            sp.wait_ge(S["k_stored"], 32)
            ck = cache_k[0].rearrange("n t h d -> n t (h d)")
            cv = cache_v[0].rearrange("n t h d -> n t (h d)")
            vs = v_sample[0].rearrange("b t h d -> b t (h d)")

            def page(i, p):
                return ds(sp.value_load(pages[0:1, ds(i * PAGES + p, 1)], min_val=0, max_val=n_phys - 1), 1)

            def attend(i, front=True, back=True):
                j = i - 1
                for p in range(PAGES):
                    if front:
                        here = page(i, p)
                        sp.wait_ge(S["k_flipped"], i * PAGES + (last_in_slot(p) + 1 + KSLOTS))
                        sp.dma_start(kpage[p % KSLOTS][:], ck[here].rearrange("n t c -> (n t) c")).then_inc(kpage_landed[p % KSLOTS], 16)
                    if back and p == PAGES // 2 - 1:
                        sp.wait_ge(S["pv_rows"], j + 1)
                        sp.dma_start(vnew[:], vs[ds(j, 1)].rearrange("b t c -> (b t) c")).then_inc(S["vnew_landed"], 16)
                    if back and p >= PAGES // 2:
                        for n in (2 * p - PAGES, 2 * p - PAGES + 1):
                            sp.dma_start(vpage[n][:], cv[page(j, n)].rearrange("n t c -> (n t) c")).then_inc(vpage_landed[n], 16)

            attend(0, back=False)
            with sp.Fori(1, SB) as i:
                attend(i)
            attend(SB, front=False)

            sp.wait_ge(S["s_pv"], SB + 1)
            sp.wait_ge(S["att_p"], HEADS + 1)
            sp.wait_ge(S["u_stored"], 32)
            sp.wait_ge(S["w1_stored"], 16 * BATCHES)
            sp.dma_start(h0raw[:, :, 0, :], state_ssm_re[0].rearrange("b g p -> g b p")).then_inc(S["h0_landed"], 16)
            sp.dma_start(h0raw[:, :, 2, :], state_ssm_re[0].rearrange("b g p -> g b p")).then_inc(S["h0_landed"], 16)
            sp.dma_start(h0raw[:, :, 1, :], state_ssm_im[0].rearrange("b g p -> g b p")).then_inc(S["h0_landed"], 16)
            u_chunks = u_tok.rearrange("(c s) d -> c s d", s=CHUNK)
            with sp.Fori(0, BATCHES) as i:
                sp.wait_ge(S["g_done"], i + 1)
                sp.dma_start(Uraw[:], u_chunks[:, :, ds(i * P, P)]).then_inc(S["uraw_landed"], 16)
                sp.dma_start(W1[:], w1_d[ds(i, 1)].rearrange("o p (g m) -> (o p) g m", m=P)).then_inc(S["w1_landed"], 16)

            sp.wait_ge(S["g_done"], BATCHES + 1)
            sp.wait_ge(S["taps_stored"], 16 * BATCHES)
            sp.wait_ge(S["p_stored"], 16 * BATCHES)
            with sp.Fori(0, BATCHES) as i:
                sp.wait_ge(S["y_done"], i + 1)
                for s in range(CHUNK):
                    a = (CHUNK - 1 - s) * GC
                    sp.dma_start(Kt[:, s, :], taps_d[a:a + P, ds(i * P, P)]).then_inc(S["kt_landed"], 16)
                sp.dma_start(Pt[:], p_d[ds(i, 1)].rearrange("o p (g m) -> (o p) g m", m=P)).then_inc(S["pt_landed"], 16)
            sp.wait_ge(S["y_stored"], 16 * BATCHES)
            sp.wait_ge(S["scanned"], 1)
            yt = y_tok[0:NP].rearrange("(t p) d -> p t d", p=P)
            sp.dma_start(ytk[:, 0:2, :], yt).then_inc(S["ytk_landed"], 16)
            sp.dma_start(ytk[0:SB * ST, 2, :], y_tok[NP:T]).then_inc(S["ytk_landed"], 16)

            sp.wait_ge(S["y_pre"], KA)
            with sp.Fori(0, KA // 4) as i:
                for cc in range(4):
                    load(i * 4 + (GLU + cc), cc, KA, w_glu_d[:, :, ds((i * 4 + cc) * P, P)])
            with sp.Fori(0, KD) as i:
                load(i * 4 + MERGE, 0, KD, w_in_d[:, :, ds(i * P + 3 * AW + SW, P)])
                load(i * 4 + (MERGE + 1), 1, KA, w_att_d[:, :, ds(i * P, P)])
                load(i * 4 + (MERGE + 2), 2, KD, w_in_d[:, :, ds(i * P + 3 * AW + SW + D, P)])
                load(i * 4 + (MERGE + 3), 3, KA, w_ssm_d[:, :, ds(i * P, P)])
            with sp.Fori(0, KD // 4) as i:
                for cc in range(4):
                    load(i * 4 + (OUT + cc), cc, KD, w_out_d[:, :, ds((i * 4 + cc) * P, P)])
            sp.wait_ge(S["m_ready"], KD)
            sp.dma_start(conv_raw[:], state_conv[0].rearrange("b i (r c) -> r (b i) c", c=P)).then_inc(S["conv_landed"], 16)
            j0 = 0
            for q, nj in enumerate(QUARTERS):
                n0 = first_of[f"up{q}"]
                with sp.Fori(0, nj // 2) as i:
                    for cc in range(4):
                        column = (j0 + cc // 2) * P + (cc % 2) * FF
                        load(i * 4 + (n0 + cc), cc, KD, w_up_d[:, :, ds(i * (2 * P) + column, P)])
                n0 = first_of[f"down{q}"]
                with sp.Fori(0, KD // 4) as i:
                    for cc in range(4):
                        load(i * 4 + (n0 + cc), cc, nj, w_down_d[:, j0:j0 + nj, ds((i * 4 + cc) * P, P)])
                j0 += nj

            sp.wait_ge(S["flips_read"], 60)
            for o, r in ((conv_prompt[0], 0), (conv_sample[0], 2)):
                n = o.shape[0] * 2
                sp.dma_start(o.rearrange("b i (r c) -> r (b i) c", c=P), rows_t[:, r:r + n, :]).then_inc(S["rows_stored"], 16)
            sp.wait_ge(S["flips_read"], 72)
            sp.dma_start(y_prompt[0].rearrange("(t p) d -> p t d", p=P), ytok[:, 0:2, :]).then_inc(S["y_out"], 16)
            sp.dma_start(y_sample.rearrange("b t d -> (b t) d"), ytok[0:SB * ST, 2, :]).then_inc(S["y_out"], 16)
            sp.wait_ge(S["rows_stored"], 32)
            sp.wait_ge(S["y_out"], 32)

        @block.gpsimd
        def _(pool):
            g = nc.gpsimd
            for name in ("w_saved", "y_saved"):
                pool.sem_inc(S[name], 1)
            own = Own(pool, S["own_pool"])
            own.mark(g.memset(zeros[:], 0.0))
            own.mark(g.memset(ident[:], 0.0))
            own.mark(g.memset(later[:], 1.0))
            own.mark(g.memset(mean_of[:], 1.0 / D))
            own.mark(g.memset(masks[:], 0.0))
            own.mark(g.memset(mask_new[:], 0.0))
            own.mark(g.memset(sign[:], 1.0))
            own.step(g.memset(ones[:], 1.0))
            g.affine_select(out=ident[:], in_=ident[:], compare_op=ALU.not_equal, fill=1.0, base=0,
                            pattern=[[-1, P]], channel_multiplier=1).then_inc(S["ident_ready"], 1)
            own.mark(g.affine_select(out=later[:], in_=later[:], compare_op=ALU.is_ge, fill=0.0, base=0,
                                     pattern=[[-1, P]], channel_multiplier=1))
            for first in (0, 256):
                own.mark(g.affine_select(out=masks[:, first:first + P], in_=masks[:, first:first + P], compare_op=ALU.is_gt,
                                         fill=-1.0, base=0, pattern=[[1, P]], channel_multiplier=-1))
            mn = mask_new[:].rearrange("k (h q) -> k h q", h=HEADS)
            own.mark(g.affine_select(out=mn, in_=mn, compare_op=ALU.is_gt, fill=-1.0, base=0,
                                     pattern=[[0, HEADS], [1, ST]], channel_multiplier=-1))
            own.step(g.affine_select(out=sign[:, 0:1], in_=sign[:, 0:1], compare_op=ALU.is_gt, fill=-1.0, base=GS,
                                     pattern=[[0, 1]], channel_multiplier=-1))
            g.tensor_scalar(sign[:, 1:2], sign[:, 0:1], -1.0, None, ALU.mult).then_inc(S["consts_ready"], 1)
            pool.dma_start(taps_d[P:P + 112], zeros[:]).then_inc(S["zeros_stored"], 16)

            pool.wait_ge(S["prep_dve"], 1)
            with pool.Fori(0, BATCHES) as i:
                own.begin(i, 3)
                gs = ds(i * GB, GB)

                def power(t):
                    return t[:, gs, 1:CHUNK + 1].unsqueeze(3).to_broadcast([P, GB, CHUNK, GC])

                def rows(t):
                    return t[:, gs, :].unsqueeze(2).to_broadcast([P, GB, CHUNK, GC])

                def blocks(t):
                    return t[:].rearrange("p g (s n) -> p g s n", n=GC)

                own.mark(g.tensor_tensor(blocks(PT), power(pows[0]), rows(c1), ALU.mult))
                own.step(g.tensor_tensor(blocks(PX), power(pows[1]), rows(c2), ALU.mult))
                own.step(g.tensor_tensor(P_[:], PT[:], PX[:], ALU.add))
                pool.dma_start(p_d[ds(i, 1)].rearrange("o p c -> (o p) c"), P_[:].rearrange("p g m -> p (g m)")).then_inc(S["p_stored"], 16)
                pool.wait_ge(S["w_read"], i + 2)
                alone(pool)
                pool.dma_start(w1_d[ds(i, 1)].rearrange("o p c -> (o p) c"), w1s[:].rearrange("p g m -> p (g m)")).then_inc(S["w1_stored"], 16)
                pool.dma_start(taps_d[0:P, ds(i * P, P)], o_s[:]).then_inc(S["taps_stored"], 16)
                for name in ("p_stored", "w1_stored", "taps_stored"):
                    pool.wait_ge(S[name], i * 16 + 16)
                pool.sem_inc(S["w_saved"], 1)
                own.end(BATCHES)

            f = 4 + 8 + KD

            def store_rows(prompt, sample, src, name):
                pool.dma_start(prompt.rearrange("(t p) c -> p t c", p=P), src[:, 0:2, :]).then_inc(S[name], 16)
                pool.dma_start(sample, src[0:SB * ST, 2, :]).then_inc(S[name], 16)

            pool.wait_ge(S["flips_read"], f + 6)
            store_rows(u_tok[0:NP], u_tok[NP:T], stage, "u_stored")
            pool.wait_ge(S["flips_read"], f + 12)
            store_rows(v_prompt[0, 0].rearrange("t h d -> t (h d)"), v_sample[0].rearrange("b t h d -> (b t) (h d)"), vtok, "v_stored")
            pool.wait_ge(S["flips_read"], f + 18)
            store_rows(k_prompt[0, 0].rearrange("t h d -> t (h d)"), k_sample[0].rearrange("b t h d -> (b t) (h d)"), stage, "k_stored")

            pool.wait_ge(S["chunk_done"], 2 + GLU)
            own.mark(g.memset(sR[:], 0.0))
            own.mark(g.memset(sz[:], 0.0))
            own.mark(g.memset(se[:], 0.0))
            own.mark(g.memset(q_block[:], 0.0))
            own.step(g.memset(sS[:], 0.0))
            pool.wait_ge(S["bias_landed"], 16)
            for q in range(ST):
                last = g.tensor_copy(bias_q[:].rearrange("p (h q) -> p h q", q=ST)[:, :, q], bias_h[:])
            last.then_inc(S["bias_spread"], 1)

            def attend(i, front=True, back=True):
                j = i - 1
                if front:
                    pool.wait_ge(S["scored"], i * PAGES + 2)
                    g.tensor_copy(q_block[:].rearrange("p (h c) -> p h c", h=HEADS)[:, :, 0:ST],
                                  projT[:, KA:2 * KA, ds(i * ST + NP, ST)]).then_inc(S["q_staged"], 1)
                if back:
                    pool.wait_ge(S["p_pv"], j + 1)
                    own.step(g.tensor_copy(kh[:].unsqueeze(1), projT[:, ds(j + 2 * KA, 1), 0:NP]))
                    g.tensor_copy(vh[:], vtok[:, 0:2, ds(j * HD, HD)]).then_inc(S["head_staged"], 1)
                if back:
                    pool.wait_ge(S["s_s"], j + 1)
                    alone(pool)
                    own.step(g.tensor_copy(sR[:, PAGES - 2, :], sS[:, PAGES - 1, :]))
                    for p in range(PAGES - 3, -1, -1):
                        ins = g.tensor_tensor(sR[:, p, :], sR[:, p + 1, :], sS[:, p + 1, :], ALU.add)
                        if p:
                            own.step(ins)
                        else:
                            ins.then_inc(S["s_r"], 1)

            attend(0, back=False)
            with pool.Fori(1, SB) as i:
                own.begin(i, 7, first=1)
                attend(i)
                own.end(SB - 1)
            attend(SB, front=False)

            pool.wait_ge(S["s_pv"], SB + 1)
            with pool.Fori(0, BATCHES) as i:
                pool.wait_ge(S["uraw_landed"], i * 16 + 16)
                pool.wait_ge(S["ug_flipped"], i + 1)
                alone(pool)
                for gg in range(GB):
                    last = g.tensor_copy(Ug[:, gg, :].rearrange("c (s n) -> c s n", n=GC), Uraw[:, :, gg * GC:(gg + 1) * GC])
                last.then_inc(S["ug_ready"], 1)
            pool.wait_ge(S["scanned"], 1)
            y_chunks = y_tok.rearrange("(c s) d -> c s d", s=CHUNK)
            with pool.Fori(0, BATCHES) as i:
                pool.wait_ge(S["y_done"], i + 1)
                own.begin(i, 2)
                own.mark(g.tensor_copy(Us[:], U[:, ds(i * GB, GB), :]))
                own.mark(g.tensor_copy(Hs[:, :, 0:CP], Z[:, 0, ds(i * GB, GB), 0:CP]))
                g.tensor_copy(Hs[:, :, CP:CT], Z[:, 0, ds(i * GB, GB), CP + 1:CT + 1]).then_inc(S["us_ready"], 1)
                own.end(BATCHES)
                pool.wait_ge(S["y_read"], i + 2)
                pool.dma_start(y_chunks[:, :, ds(i * P, P)], Yt[:].rearrange("c s g n -> c s (g n)")).then_inc(S["y_stored"], 16)
                pool.wait_ge(S["y_stored"], i * 16 + 16)
                pool.sem_inc(S["y_saved"], 1)
            pool.wait_ge(S["flips_read"], f + 18 + 2 + 3)
            for o, r, b in ((ssm_re_prompt, 0, 0), (ssm_im_prompt, 1, 0), (ssm_re_sample, 0, 1), (ssm_im_sample, 1, 1)):
                n = SB if b else 1
                pool.dma_start(o[0].rearrange("b g p -> g b p"), fin[:, b:b + n, r * GS:(r + 1) * GS]).then_inc(S["state_stored"], 16)

            pool.wait_ge(S["flips_read"], f + 18 + 2 + 3 + 4)
            pool.wait_ge(S["h2_ready"], KD)
            for e in ext:
                own.mark(g.memset(e[:, 0:2], 0.0))
            own.settle()
            j0 = 0
            done = 0
            for q, nj in enumerate(QUARTERS):
                with pool.Fori(0, nj // 2) as i:
                    own.begin(i, 8)
                    for cc in range(4):
                        block_no = i * 2 + (j0 + cc // 2 + (cc % 2) * JF)
                        tail = ext[cc][:, NP + 2:EXT].rearrange("p (b t) -> p b t", b=SB)
                        n = i * 4 + (done + cc)
                        pool.wait_ge(S["ext_read"], n + 1)
                        own.settle()
                        g.tensor_copy(tail[:, :, 0:2], conv_st[:, :, ds(block_no, 1)].rearrange("p (b i) o -> p b (i o)", b=SB)).then_inc(S["halo"], 1)
                        pool.wait_ge(S["conv_ev"], n + 1)
                        own.mark(g.tensor_copy(rows_out[:, 0:2, ds(block_no, 1)], ext[cc][:, NP:NP + 2].unsqueeze(2)))
                        pool.wait_ge(acc_free[cc % 2], i * 2 + (nth_pair(first_of[f"up{q}"]) + cc // 2 + 2))
                        own.mark(g.tensor_copy(rows_out[:, 2:2 + 2 * SB, ds(block_no, 1)].rearrange("p (b i) o -> p b (i o)", b=SB), tail[:, :, ST:ST + 2]))
                    own.end(nj // 2)
                j0 += nj
                done += 2 * nj
            own.settle()
            rows_copied.append(own.count)
            for name, n in (("u_stored", 32), ("v_stored", 32), ("k_stored", 32), ("state_stored", 64),
                            ("w1_stored", 16 * BATCHES), ("taps_stored", 16 * BATCHES),
                            ("p_stored", 16 * BATCHES), ("y_stored", 16 * BATCHES)):
                pool.wait_ge(S[name], n)

        @block.tensor
        def _(pe):
            t = nc.tensor
            turned = [0]

            def turn(turns, ready=None):
                for n, (sources, rows, _) in enumerate(turns):
                    if ready and n in ready:
                        ready[n]()
                    if turned[0] >= 4:
                        pe.wait_ge(S["flips_read"], turned[0] - 3)
                    b, c = bank[4 + turned[0] % 4], 0
                    for src, w in sources:
                        k = src.shape[0]
                        last = t.transpose(b[0:rows, c:c + w], src, ident[0:k, 0:k])
                        c += w
                    last.then_inc(S["flipped"], 1)
                    turned[0] += 1

            pe.sem_inc(S["ada_turned"], 1)
            pe.sem_inc(S["chunk_done"], 2)
            pe.sem_inc(S["k_flipped"], KSLOTS)
            for name in ("scored", "g_done", "y_done", "ug_flipped", "p_pv", "zn_done", "s_pv", "w_flipped", "z_turned", "pv_rows"):
                pe.sem_inc(S[name], 2 if name == "scored" else 1)

            pe.wait_ge(S["ident_ready"], 1)
            setup = list(setup_turns())
            turn(setup[:12], {0: lambda: pe.wait_ge(S["silu_ready"], 1), 1: lambda: pe.wait_ge(S["params_landed"], 9 * 16),
                              3: lambda: pe.wait_ge(S["ssm_landed"], 11 * 16)})

            def ada_unit(n, buf, block_no, unit):
                pe.wait_ge(S["split_done"], n + (1 + RING))
                if unit == 0:
                    pe.wait_ge(S["ada_copied"], block_no + 1)
                    alone(pe)
                rows = bank[2][0:2 * NC, :]
                for k in range(BLOCK // P):
                    c = cHL[:, unit * (BLOCK // P) + k, :]
                    t.matmul(rows, c, wide(wH[buf])[:, k, :], start=(unit == 0 and k == 0), stop=False)
                    last = t.matmul(rows, c, wide(wL[buf])[:, k, :], start=False, stop=(unit == UNITS - 1 and k == BLOCK // P - 1))
                last.then_inc(S["chunk_done"], 1)

            def ada_turn(block_no):
                pe.wait_ge(S["ada_copied"], block_no + 2)
                pe.wait_ge(S["ada_mod"], block_no + 1)
                for c in range(BLOCK // P):
                    last = t.matmul(bank[3][:, c * NC:(c + 1) * NC], ada_rows[:, c * P:(c + 1) * P], add_up[:], start=True, stop=True)
                last.then_inc(S["ada_turned"], 1)

            pe.wait_ge(S["c_split"], 1)
            with pe.Fori(0, UNITS) as i:
                for u in range(UNITS):
                    ada_unit(i * UNITS + u, u % 2, i, u)
                ada_turn(i)
            turn(setup[12:], {0: lambda: pe.wait_ge(S["x_landed"], 32)})
            with pe.Fori(UNITS, 2 * UNITS) as i:
                for u in range(UNITS):
                    ada_unit(i * UNITS + u, u % 2, i, u)
                for e in range(2):
                    b = i * 2 + (e - 2 * UNITS)
                    pe.wait_ge(S["v_ready"], b + 1)
                    pe.wait_ge(S["w_read"], b + 1)
                    for gg in range(GB):
                        t.transpose(bank[4 + gg // 4][:, (gg % 4) * P:(gg % 4 + 1) * P], V[:, gg, :], ident[:])
                    for gg in range(GB):
                        last = t.matmul(bank[6][:, gg * GC:(gg + 1) * GC], V[:, gg, :],
                                        c1[:, ds(b * GB + gg, 1), :].rearrange("p o n -> p (o n)"), start=True, stop=True)
                    last.then_inc(S["w_flipped"], 1)
                    if e == 0:
                        ada_turn(i)

            def product(n, cc, K, half_n, high, low, buf=None):
                pe.wait_ge(S["split_done"], n + (1 + RING))
                pe.wait_ge(acc_free[cc % 2], half_n + 1)
                acc = bank[cc % 2][:, 0:T]
                buf = cc % 2 if buf is None else buf
                a, b = wH[buf], wL[buf]
                for k in range(K):
                    t.matmul(acc, a[:, k, :], high[:, k, :], start=(k == 0), stop=False)
                    t.matmul(acc, a[:, k, :], low[:, k, :], start=False, stop=False)
                    last = t.matmul(acc, b[:, k, :], high[:, k, :], start=False, stop=(k == K - 1))
                last.then_inc(S["chunk_done"], 1)

            def products(i, n0, cc, K, high, low):
                product(i * 4 + (n0 + cc), cc, K, i * 2 + (nth_pair(n0) + cc // 2), high, low)

            pe.wait_ge(S["h_ready"], KD)
            with pe.Fori(0, KA) as i:
                for x, (kind, m) in enumerate(items):
                    n = i * ITEMS + (PROJ + x)
                    if kind == "unit":
                        ada_unit(n, x % 3, i * 2 + (2 * UNITS + m // UNITS), m % UNITS)
                    else:
                        product(n, m, KD, i * 2 + m // 2, hH, hL, x % 3)
                        if m % 2:
                            ada_turn(i * 2 + (2 * UNITS + m // 2))

            for a_ in acc_free:
                pe.wait_ge(a_, nth_pair(GLU) + 1)
            turn(proj_turns())

            pe.wait_ge(S["consts_ready"], 1)
            pe.wait_ge(S["flips_read"], turned[0])

            def attend(i, front=True, back=True):
                j = i - 1

                def flip(p):
                    pe.wait_ge(kpage_landed[p % KSLOTS], i * (16 * len(range(p % KSLOTS, PAGES, KSLOTS))) + 16 * (p // KSLOTS + 1))
                    pe.wait_ge(S["kt_dve"], i * PAGES + (p + 1))
                    pe.wait_ge(S["kt_act"], i * PAGES + (p + 1))
                    for h in range(HEADS):
                        last = t.transpose(bank[h // 4][:, (h % 4) * P:(h % 4 + 1) * P], kpage[p % KSLOTS][:, h * HD:(h + 1) * HD], ident[:])
                    last.then_inc(S["k_flipped"], 1)

                def score(p):
                    pe.wait_ge(S["kt_dve"], i * PAGES + (p + 2))
                    pe.wait_ge(S["kt_act"], i * PAGES + (p + 2))
                    if p % 4 == 0:
                        pe.wait_ge(S["z_copied"], i * 2 + (p // 4 + 1))
                    for h in range(HEADS):
                        last = t.matmul(bank[7][0:HQ, (p % 4) * PAGE:(p % 4 + 1) * PAGE], q_block[:, h * HQ:(h + 1) * HQ],
                                        kTp[p % 2][:, h, :], start=(h == 0), stop=(h == HEADS - 1))
                    last.then_inc(S["scored"], 1)

                def new_scores():
                    pe.wait_ge(S["q_staged"], i + 1)
                    alone(pe)
                    for h in range(HEADS):
                        last = t.matmul(bank[6][0:HQ, 0:ST], q_block[:, h * HQ:(h + 1) * HQ],
                                        projT[:, 2 * KA + h, ds(i * ST + NP, ST)], start=(h == 0), stop=(h == HEADS - 1))
                    last.then_inc(S["zn_done"], 1)

                def turn_scores(first):
                    pe.wait_ge(S["z_copied"], i * 2 + (first // 4 + 2))
                    if first == 0:
                        pe.wait_ge(S["s_e_in"], i + 1)
                    alone(pe)
                    for p in range(first, first + 4):
                        t.transpose(bank[2][:, p * HQ:(p + 1) * HQ], z_rows[:, p, :], ident[0:HQ, 0:HQ])

                def head_scores():
                    pe.wait_ge(S["head_staged"], j + 1)
                    pe.wait_ge(S["att_p"], j + 1)
                    pe.wait_ge(S["att_s"], j + 1)
                    q = projT[:, ds(j + KA, 1), :].rearrange("p o t -> p (o t)")
                    t.matmul(bank[4][:, 0:NP], kh[:, 0:P], q[:, 0:NP], start=True, stop=True)
                    t.matmul(bank[4][:, NP:NP + P], kh[:, P:NP], q[:, P:NP], start=True, stop=True).then_inc(S["pz_done"], 1)

                def sums():
                    pe.wait_ge(S["s_s"], j + 1)
                    pe.wait_ge(S["p_s"], j + 1)
                    alone(pe)
                    t.matmul(bank[4][0:ST, 384:384 + HQ], later[0:ST, 0:ST], sS[0:ST, PAGES, :], start=True, stop=True)
                    t.matmul(bank[4][:, 0:384], later[:], pS[:], start=True, stop=False)
                    t.matmul(bank[4][:, P:NP], ones[:], pS[:, NP:NP + P], start=False, stop=True).then_inc(S["p_cs"], 1)
                    t.matmul(bank[3][:], later[:], sS[:, 0:PAGES, :].rearrange("p a c -> p (a c)"), start=True, stop=False)
                    t.matmul(bank[3][:], ones[0:ST, :], sS[0:ST, PAGES:PAGES + 1, :].to_broadcast([ST, PAGES, HQ]), start=False, stop=False)
                    pe.wait_ge(S["s_r"], j + 1)
                    t.matmul(bank[3][:], ones[:], sR[:, 0:PAGES, :].rearrange("p a c -> p (a c)"), start=False, stop=True).then_inc(S["s_cs"], 1)

                def outputs():
                    pe.wait_ge(S["p_w"], j + 1)
                    pe.wait_ge(S["s_w"], j + 1)
                    t.matmul(bank[4][:, 0:NP], vh[:, 0, :], pe_[:, 0:NP], start=True, stop=False)
                    t.matmul(bank[4][:, P:NP], vh[:, 1, :], pe_[:, NP:NP + P], start=False, stop=True).then_inc(S["p_pv"], 1)
                    if front:
                        pe.wait_ge(S["zn_copied"], i + 1)
                    pe.wait_ge(S["vnew_landed"], j * 16 + 16)
                    for p in range(PAGES):
                        pe.wait_ge(vpage_landed[p], j * 16 + 16)
                    alone(pe)
                    for h in range(HEADS):
                        o = bank[5 + h // 4][0:ST, (h % 4) * HD:(h % 4 + 1) * HD]
                        for p in range(PAGES):
                            t.matmul(o, se[:, p, h * ST:(h + 1) * ST], vpage[p][:, h * HD:(h + 1) * HD], start=(p == 0), stop=False)
                        last = t.matmul(o, se[0:ST, PAGES, h * ST:(h + 1) * ST], vnew[:, h * HD:(h + 1) * HD], start=False, stop=True)
                    last.then_inc(S["pv_rows"], 1)

                def turn_outputs():
                    pe.wait_ge(S["o_act"], j + 1)
                    pe.wait_ge(S["o_dve"], j + 1)
                    pe.wait_ge(S["att_p"], j + 2)
                    alone(pe)
                    for h in range(HEADS):
                        last = t.transpose(bank[4][:, 512 - HQ + h * ST:512 - HQ + (h + 1) * ST], o_rows[:, h * HD:(h + 1) * HD], ident[0:ST, 0:ST])
                    last.then_inc(S["s_pv"], 1)

                for p in range(PAGES):
                    if front:
                        flip(p)
                    if back and p == 0:
                        head_scores()
                    if front and p == 0:
                        new_scores()
                    if front and p:
                        score(p - 1)
                    if back and p == 4:
                        sums()
                    if front and p == 5:
                        turn_scores(0)
                    if back and p == 7:
                        outputs()
                if front:
                    score(PAGES - 1)
                    turn_scores(4)
                    pe.wait_ge(S["zn_copied"], i + 1)
                    alone(pe)
                    t.transpose(bank[3][0:ST, 0:HQ], zn_rows[:], ident[0:HQ, 0:HQ]).then_inc(S["z_turned"], 1)
                if back:
                    turn_outputs()

            attend(0, back=False)
            with pe.Fori(1, SB) as i:
                attend(i)
            attend(SB, front=False)

            pe.wait_ge(S["att_s"], SB + 1)
            with pe.Fori(0, BATCHES) as i:
                pe.wait_ge(S["ug_ready"], i + 1)
                alone(pe)
                for gg in range(GB):
                    last = t.transpose(bank[4][:, gg * CT:(gg + 1) * CT], Ug[:, gg, :], ident[0:CT, 0:CT])
                last.then_inc(S["ug_flipped"], 1)
                pe.wait_ge(S["u_ready"], i + 1)
                pe.wait_ge(S["w2_ready"], i + 1)
                pe.wait_ge(S["g_read"], i + 1)
                for b, w in ((5, W1), (6, W2)):
                    for gg in range(GB):
                        last = t.matmul(bank[b][:, gg * CT:(gg + 1) * CT], w[:, gg, :],
                                        U[:, ds(i * GB + gg, 1), :].rearrange("p o c -> p (o c)"), start=True, stop=True)
                last.then_inc(S["g_done"], 1)
            pe.wait_ge(S["h0_landed"], 48)
            pe.wait_ge(S["g_read"], BATCHES + 1)
            turn(state_turns())
            pe.wait_ge(S["scanned"], 1)
            turn(final_state_turns())
            pe.wait_ge(S["flips_read"], turned[0])
            with pe.Fori(0, BATCHES) as i:
                pe.wait_ge(S["us_ready"], i + 1)
                pe.wait_ge(S["kt_landed"], i * (16 * CHUNK) + 16 * CHUNK)
                pe.wait_ge(S["pt_landed"], i * 16 + 16)
                pe.wait_ge(S["y_read"], i + 1)
                for gg in range(GB):
                    o = bank[4 + gg // 4][0:CT, (gg % 4) * P:(gg % 4 + 1) * P]
                    t.matmul(o.rearrange("c (s n) -> c s n", n=GC), Us[:, gg, :], Kt[:, :, gg * GC:(gg + 1) * GC], start=True, stop=False)
                    last = t.matmul(o, Hs[:, gg, :], Pt[:, gg, :], start=False, stop=True)
                last.then_inc(S["y_done"], 1)
            pe.wait_ge(S["y_read"], BATCHES + 1)
            pe.wait_ge(S["ytk_landed"], 32)
            for c in range(KA):
                if c >= 4:
                    pe.wait_ge(S["y_pre"], c - 3)
                for tt in range(3):
                    rows = min(P, T - tt * P)
                    last = t.transpose(bank[4 + c % 4][:, tt * P:tt * P + rows], ytk[0:rows, tt, c * P:(c + 1) * P], ident[0:rows, 0:rows])
                last.then_inc(S["ytk_turned"], 1)

            pe.wait_ge(S["y_ready"], KA)
            passes(pe, "glu", None, 0, lambda i, _: [products(i, GLU, cc, KA, ygH, ygL) for cc in range(4)])
            pe.wait_ge(S["s_ready"], KA)
            operands = [(KD, hH, hL), (KA, attH, attL), (KD, hH, hL), (KA, sH, sL)]
            passes(pe, "merge", None, 0, lambda i, _: [products(i, MERGE, cc, *operands[cc]) for cc in range(4)])
            pe.wait_ge(S["m_ready"], KD)
            passes(pe, "out", None, 0, lambda i, _: [products(i, OUT, cc, KD, mH, mL) for cc in range(4)])

            def layer_norm(nth):
                pe.wait_ge(S["x_pre"], KD * (nth + 1) + 1)
                for k in range(KD):
                    last = t.matmul(bank[2][:, 0:T], mean_of[:], xT[:, k, :], start=(k == 0), stop=(k == KD - 1))
                last.then_inc(S["mean_done"], 1)
                for k in range(KD):
                    pe.wait_ge(S["squared"], KD * nth + k + 1)
                    last = t.matmul(bank[3][:, 0:T], mean_of[:], centred_sq[:, k, :], start=(k == 0), stop=(k == KD - 1))
                last.then_inc(S["var_done"], 1)

            pe.wait_ge(S["conv_landed"], 16)
            turn(conv_state_turns())
            layer_norm(0)
            pe.wait_ge(S["h2_ready"], KD)
            down = 0
            for q, nj in enumerate(QUARTERS):
                n0 = first_of[f"up{q}"]
                passes(pe, f"up{q}", None, 0, lambda i, _, n0=n0: [products(i, n0, cc, KD, hH, hL) for cc in range(4)])
                down += nj
                pe.wait_ge(S["f_ready"], down + 1)
                n0 = first_of[f"down{q}"]
                passes(pe, f"down{q}", None, 0, lambda i, _, n0=n0, nj=nj: [products(i, n0, cc, nj, fH, fL) for cc in range(4)])
            pe.wait_ge(S["own_pool"], rows_copied[0])
            turn(rows_out_turns())
            layer_norm(1)
            pe.wait_ge(S["normed"], KD)
            turn(y_turns())

        @block.scalar
        def _(act):
            a = nc.scalar
            own = Own(act, S["own_act"])
            act.sem_inc(S["ada_copied"], 1)
            act.sem_inc(S["z_copied"], 1)
            act.sem_inc(S["w_read"], 1)
            act.sem_inc(S["kt_act"], 1)
            act.sem_inc(S["y_read"], 1)
            for s in acc_free:
                act.sem_inc(s, 1)
            act.dma_start(xrows[:, 0:2, :], x_prompt[0].rearrange("(t p) d -> p t d", p=P)).then_inc(S["x_landed"], 16)
            act.dma_start(xrows[0:SB * ST, 2, :], x_sample.rearrange("b t d -> (b t) d")).then_inc(S["x_landed"], 16)
            act.wait_ge(S["c_landed"], 32)
            a.activation(csil[:], crows[:], ACT.Sigmoid).then_inc(S["prep_act"], 1)
            for v in range(2):
                act.dma_start(a_raw[:, 0, v * GS:(v + 1) * GS], ssm_a_re[0]).then_inc(S["ssm_landed"], 16)
                act.dma_start(a_raw[:, 1, v * GS:(v + 1) * GS], ssm_a_im[0]).then_inc(S["ssm_landed"], 16)
            for v, (b, c) in enumerate(((ssm_b_re, ssm_c_re), (ssm_b_im, ssm_c_im), (ssm_b_re, ssm_c_re))):
                act.dma_start(b_raw[:, v, :], b[0].rearrange("g p n -> g (p n)")).then_inc(S["ssm_landed"], 16)
                act.dma_start(c_raw[:, :, v, :], c[0]).then_inc(S["ssm_landed"], 16)
            act.dma_start(log_dt[:], ssm_log_dt.to_broadcast([P, GROUPS])).then_inc(S["ssm_landed"], 16)
            act.dma_start(bias_h[:], sb_bias.to_broadcast([P, HEADS])).then_inc(S["bias_landed"], 16)

            def split_high(n, cc, K, n4, buf=None):
                act.wait_ge(ring_landed[cc], n4 * 16 + 16)
                act.wait_ge(S["chunk_done"], n + 1 if buf is None else n)
                a.activation(wH[cc % 2 if buf is None else buf][:, 0:K, :], ring[cc][:, 0:K, :], ACT.Copy).then_inc(S["hi_done"], 1)

            def split_ahead(i, n0, cc, next_ks, own_ks):
                c = cc + 2
                if c < 4:
                    split_high(i * 4 + (n0 + c), c, own_ks[c], i + n0 // 4)
                elif next_ks:
                    split_high(i * 4 + (n0 + c), c - 4, next_ks[c - 4], i + (n0 // 4 + 1))

            def start_stream(n0, ks):
                for c in range(2):
                    split_high(n0 + c, c, ks[c], n0 // 4)

            def wait_product(i, n0, cc):
                act.wait_ge(S["chunk_done"], i * 4 + (n0 + cc + 3))

            def copy_rows(n, block_no):
                act.wait_ge(S["chunk_done"], n + 3)
                act.wait_ge(S["ada_turned"], block_no + 1)
                a.activation(ada_rows[:], bank[2][0:2 * NC, :], ACT.Copy).then_inc(S["ada_copied"], 1)

            def ada_pass(i, last=False):
                for u in range(UNITS):
                    if u == UNITS - 1:
                        copy_rows(i * UNITS + u, i)
                    c = u + 2
                    if not (last and c >= UNITS):
                        split_high(i * UNITS + c, c % UNITS, KD, i + c // UNITS)

            act.wait_ge(S["flips_read"], 4)
            start_stream(ADA1, [KD] * 2)
            with act.Fori(0, 2) as i:
                ada_pass(i)
            act.wait_ge(S["angle_ready"], 1)
            a.activation(small64[:, 6, :], small64[:, 4, :], ACT.Sin).then_inc(S["prep_act"], 1)
            a.activation(small64[:, 7, :], small64[:, 4, :], ACT.Sin, scale=0.5).then_inc(S["prep_act"], 1)
            with act.Fori(2, UNITS) as i:
                ada_pass(i)

            def ssm_pass(i, last=False):
                ada_pass(i, last)
                for e in range(2):
                    b = i * 2 + (e - 2 * UNITS)
                    act.wait_ge(S["w_flipped"], b + 2)
                    act.wait_ge(S["w_saved"], b + 1)
                    a.activation(w1s[:, 0:4, :].rearrange("p g m -> p (g m)"), bank[4][:], ACT.Copy)
                    a.activation(w1s[:, 4:8, :].rearrange("p g m -> p (g m)"), bank[5][:], ACT.Copy)
                    a.activation(o_s[:], bank[6][:, 0:P], ACT.Copy).then_inc(S["w_read"], 1)

            with act.Fori(UNITS, 2 * UNITS - 1) as i:
                ssm_pass(i)
            ssm_pass(2 * UNITS - 1, last=True)

            for x in range(2):
                split_high(PROJ + x, x, KD, PROJ // RING)
            for name in ("w1_stored", "taps_stored", "p_stored"):
                act.wait_ge(S[name], 16 * BATCHES)
            act.wait_ge(S["zeros_stored"], 16)
            split_high(PROJ + 2, 2, KD, PROJ // RING, 2)

            def proj_pass(i, last=False):
                for x, (kind, m) in enumerate(items):
                    n = i * ITEMS + (PROJ + x)
                    if kind == "chunk":
                        act.wait_ge(S["chunk_done"], n + 3)
                        a.activation(projT[:, ds(i * 4 + m, 1), :].rearrange("p o t -> p (o t)"),
                                     bank[m % 2][:, 0:T], ACT.Copy).then_inc(acc_free[m % 2], 1)
                    elif m % UNITS == UNITS - 1:
                        copy_rows(n, i * 2 + (2 * UNITS + m // UNITS))
                    y = x + 3
                    if not (last and y >= ITEMS):
                        split_high(n + 3, y % RING, KD, i * (ITEMS // RING) + (PROJ // RING + y // RING), y % 3)

            with act.Fori(0, KA - 1) as i:
                proj_pass(i)
            proj_pass(KA - 1, last=True)

            act.wait_ge(S["flips_read"], 4 + 8 + KD + 18)

            def attend(i, front=True, back=True):
                j = i - 1

                def read_page(p):
                    act.wait_ge(S["k_flipped"], i * PAGES + (p + KSLOTS + 1))
                    act.wait_ge(S["scored"], i * PAGES + (p + 1))
                    a.activation(kTp[p % 2][:, 4:8, :].rearrange("p h k -> p (h k)"), bank[1][:], ACT.Copy).then_inc(S["kt_act"], 1)

                def copy_scores(first):
                    act.wait_ge(S["scored"], i * PAGES + (first + 6))
                    act.wait_ge(S["z_turned"], i + 1)
                    a.activation(z_rows[:, first:first + 4, :].rearrange("p a k -> p (a k)"), bank[7][0:HQ, :], ACT.Copy).then_inc(S["z_copied"], 1)

                for p in range(PAGES):
                    if front:
                        read_page(p)
                    if front and p == 0:
                        act.wait_ge(S["zn_done"], i + 2)
                        act.wait_ge(S["z_turned"], i + 1)
                        a.activation(zn_rows[:], bank[6][0:HQ, 0:ST], ACT.Copy).then_inc(S["zn_copied"], 1)
                    if front and p == 4:
                        copy_scores(0)
                    if back and p == 1:
                        act.wait_ge(S["s_e_in"], j + 2)
                        own.mark(a.activation(se[:], se[:], ACT.Exp))
                        act.wait_ge(S["p_exp_in"], j + 1)
                        own.step(a.activation(pe_[:], pe_[:], ACT.Exp))
                        a.activation(pe_[:], pe_[:], ACT.Ln, bias=1.0).then_inc(S["p_ln"], 1)
                        a.activation(se[:], se[:], ACT.Ln, bias=1.0).then_inc(S["s_ln"], 1)
                    if back and p == 5:
                        act.wait_ge(S["p_arg"], j + 1)
                        a.activation(pe_[:], pe_[:], ACT.Exp).then_inc(S["p_w"], 1)
                        act.wait_ge(S["s_arg"], j + 1)
                        a.activation(se[:], se[:], ACT.Exp).then_inc(S["s_w"], 1)
                if back:
                    act.wait_ge(S["pv_rows"], j + 2)
                    a.activation(o_rows[:, 0:512], bank[5][0:ST, :], ACT.Copy).then_inc(S["o_act"], 1)
                if front:
                    copy_scores(4)

            attend(0, back=False)
            with act.Fori(1, SB) as i:
                own.begin(i, 2, first=1)
                attend(i)
                own.end(SB - 1)
            attend(SB, front=False)

            with act.Fori(0, BATCHES) as i:
                act.wait_ge(S["ug_flipped"], i + 2)
                a.activation(U[:, ds(i * GB, GB), :].rearrange("p g c -> p (g c)"), bank[4][:, 0:GB * CT], ACT.Copy).then_inc(S["u_ready"], 1)
            with act.Fori(0, BATCHES) as i:
                act.wait_ge(S["y_done"], i + 2)
                act.wait_ge(S["y_saved"], i + 1)
                for half in range(2):
                    for g4 in range(4):
                        last = a.activation(Yt[:, :, half * 4 + g4, :],
                                            bank[4 + half][0:CT, g4 * P:(g4 + 1) * P].rearrange("c (s n) -> c s n", n=GC), ACT.Copy)
                last.then_inc(S["y_read"], 1)
            for c in range(KA):
                act.wait_ge(S["y_pre"], c + 1)
                if c >= 2:
                    act.wait_ge(S["y_ready"], c - 1)
                a.activation(ygl[c % 2][:], ypre[c % 2][:], ACT.Gelu_apprx_tanh).then_inc(S["y_gelu"], 1)

            start_stream(GLU, ks_of["glu"])

            def glu_pass(i, next_ks):
                for cc in range(4):
                    wait_product(i, GLU, cc)
                    m = i * 4 + cc
                    if m >= 2:
                        act.wait_ge(S["s_ready"], m - 1)
                    a.activation(gate[cc % 2][:], bank[cc % 2][:, 0:T], ACT.Sigmoid,
                                 bias=par[:, P + 120 + m:P + 121 + m]).then_inc(acc_free[cc % 2], 1)
                    split_ahead(i, GLU, cc, next_ks, ks_of["glu"])

            glu_pass(0, ks_of["glu"])
            glu_pass(1, ks_of["merge"])

            def merge_pass(i, next_ks):
                for cc in range(4):
                    if cc % 2 == 0:
                        wait_product(i, MERGE, cc)
                        act.wait_ge(acc_free[1], i * 2 + (nth_pair(MERGE) + cc // 2))
                        a.activation(gate[cc // 2][:], bank[0][:, 0:T], ACT.Sigmoid).then_inc(acc_free[0], 1)
                    split_ahead(i, MERGE, cc, next_ks, ks_of["merge"])

            act.wait_ge(S["s_ready"], KA)
            passes(act, "merge", None, 0, merge_pass)
            passes(act, "out", None, 0, lambda i, ks: [split_ahead(i, OUT, cc, ks, ks_of["out"]) for cc in range(4)])

            def layer_norm(nth, g0, b0):
                for k in range(KD):
                    act.wait_ge(S["centred"], KD * nth + k + 1)
                    a.activation(centred_sq[:, k, :], xT[:, k, :], ACT.Square).then_inc(S["squared"], 1)
                act.wait_ge(S["var_ready"], nth + 1)
                a.activation(sd[:], var[:], ACT.Sqrt).then_inc(S["sd_ready"], 1)

            layer_norm(0, 96, 112)
            conv = 0
            for q, nj in enumerate(QUARTERS):
                n0 = first_of[f"up{q}"]

                def up_pass(i, next_ks, n0=n0, conv=conv, q=q):
                    for cc in range(4):
                        wait_product(i, n0, cc)
                        act.wait_ge(S["halo"], i * 4 + (conv + cc + 1))
                        b = bank[cc % 2]
                        a.activation(ext[cc][:, 2:2 + NP], b[:, 0:NP], ACT.Copy).then_inc(S["conv_ev"], 1)
                        tail = ext[cc][:, NP + 2:EXT].rearrange("p (b t) -> p b t", b=SB)
                        a.activation(tail[:, :, 2:2 + ST], samples(b), ACT.Copy).then_inc(acc_free[cc % 2], 1)
                        split_ahead(i, n0, cc, next_ks, ks_of["up0"])
                        if cc % 2:
                            act.wait_ge(S["ext_read"], i * 4 + (conv + cc + 5))
                            a.activation(cvG[:, 0:EXT - 2], cvG[:, 0:EXT - 2], ACT.Gelu_apprx_tanh).then_inc(S["gelu_done"], 1)

                passes(act, f"up{q}", None, 0, up_pass)
                conv += 2 * nj
                n0 = first_of[f"down{q}"]
                passes(act, f"down{q}", None, 0,
                       lambda i, ks, n0=n0, q=q: [split_ahead(i, n0, cc, ks, ks_of[f"down{q}"]) for cc in range(4)])
            layer_norm(1, P + 88, P + 104)


        @block.vector
        def _(dve):
            v = nc.vector
            own = Own(dve, S["own_dve"])
            for name in ("ada_mod", "kt_dve", "s_e_in", "att_p", "att_s", "g_read", "x_pre", "f_ready"):
                dve.sem_inc(S[name], 1)
            dve.sem_inc(S["split_done"], RING)
            dve.sem_inc(S["ext_read"], 4)
            MUL, ADD, SUB = ALU.mult, ALU.add, ALU.subtract
            flips = [0]

            def read_turns(turns):
                for sources, rows, dst in turns:
                    dve.wait_ge(S["flipped"], flips[0] + 1)
                    src = bank[4 + flips[0] % 4][0:rows, 0:width(sources)]
                    if len(dst.shape) == 3:
                        src = src.rearrange("p (a b) -> p a b", a=dst.shape[1])
                    v.tensor_copy(dst, src).then_inc(S["flips_read"], 1)
                    flips[0] += 1

            dve.wait_ge(S["prep_act"], 1)
            v.tensor_tensor(csil[:], csil[:], crows[:], MUL).then_inc(S["silu_ready"], 1)
            setup = list(setup_turns())
            read_turns(setup[0:1])
            dve.wait_ge(S["consts_ready"], 1)
            dve.wait_ge(S["flips_read"], 1)
            own.mark(v.tensor_tensor(add_up[:], ident[0:2 * NC, 0:NC], ident[0:2 * NC, NC:2 * NC], ADD))
            own.step(v.tensor_copy(cHL[:, :, 0:NC], cT[:]))
            v.tensor_tensor(cHL[:, :, NC:2 * NC], cT[:], cHL[:, :, 0:NC].bitcast(F32), SUB).then_inc(S["c_split"], 1)
            read_turns(setup[1:12])
            dve.wait_ge(S["flips_read"], flips[0])

            def split_low(n, cc, K, buf=None):
                buf = cc % 2 if buf is None else buf
                dve.wait_ge(S["hi_done"], n + 1)
                v.tensor_tensor(wL[buf][:, 0:K, :], ring[cc][:, 0:K, :], wH[buf][:, 0:K, :].bitcast(F32), SUB)\
                    .then_inc(S["split_done"], 1)

            def ada_out(b):
                dve.wait_ge(S["ada_turned"], b + 2)
                n = BLOCK // P
                v.tensor_tensor(mod[:, ds(b * n, n), :], bank[3][:, 0:n * NC].rearrange("p (m c) -> p m c", c=NC),
                                par[:, ds(b * n, n)].unsqueeze(2).to_broadcast([P, n, NC]), ADD).then_inc(S["ada_mod"], 1)

            pieces = []
            for n in range(UNITS * UNITS + 2):
                pieces.append(lambda n=n: split_low(n, n % UNITS, KD))
                if n % UNITS == 1 and n > UNITS:
                    pieces.append(lambda b=n // UNITS - 1: ada_out(b))

            def piece(count=1):
                for _ in range(min(count, len(pieces))):
                    pieces.pop(0)()

            piece(2)
            steps = [0]

            def step(ins):
                own.mark(ins)
                steps[0] += 1
                if steps[0] % 5 == 0:
                    piece()
                own.settle()

            def s64(n):
                return small64[:, n, :]

            aR, aI, dt, expo, ang, mag, sn, shf, kk, rden, lb1, t0, t1_, fr, fi = (s64(n) for n in range(15))

            def exponential(out, x):
                step(v.tensor_scalar(kk, x, 1.0 / math.log(2.0), None, MUL))
                step(v.tensor_scalar(kk, kk, ROUND, None, ADD))
                step(v.tensor_scalar(kk, kk, ROUND, None, SUB))
                step(v.tensor_scalar(kk, kk, 127.0, -126.0, ALU.min, ALU.max))
                for c in LOG_2:
                    step(v.scalar_tensor_tensor(out=x, in0=kk, scalar=-c, in1=x, op0=MUL, op1=ADD))
                step(v.tensor_scalar(x, x, -1.0, 1.0, ALU.max, ALU.min))
                step(v.tensor_scalar(kk, kk, 127.0, 2.0 ** 23, ADD, MUL))
                step(v.tensor_copy(two_n[:], kk))
                step(v.tensor_scalar(out, x, 1.0 / math.factorial(8), 1.0 / math.factorial(7), MUL, ADD))
                for n in range(6, -1, -1):
                    step(v.tensor_tensor(out, out, x, MUL))
                    step(v.tensor_scalar(out, out, 1.0 / math.factorial(n), None, ADD))
                step(v.tensor_tensor(out, out, two_n[:].bitcast(F32), MUL))

            exponential(dt, log_dt[:])
            own.mark(v.tensor_tensor(expo, aR, dt, MUL))
            step(v.tensor_tensor(ang, aI, dt, MUL))
            step(v.tensor_scalar(kk, ang, 1.0 / (2.0 * math.pi), None, MUL))
            step(v.tensor_scalar(kk, kk, ROUND, None, ADD))
            step(v.tensor_scalar(kk, kk, ROUND, None, SUB))
            for c in TWO_PI:
                step(v.scalar_tensor_tensor(out=ang, in0=kk, scalar=-c, in1=ang, op0=MUL, op1=ADD))
            v.tensor_scalar(ang, ang, PI_IN, -PI_IN, ALU.min, ALU.max).then_inc(S["angle_ready"], 1)
            exponential(mag, expo)
            piece(len(pieces) - 10)
            dve.wait_ge(S["prep_act"], 3)
            pR, pI = pows
            own.mark(v.memset(pR[:, :, 0], 1.0))
            own.mark(v.memset(pI[:, :, 0], 0.0))
            step(v.tensor_tensor(pI[:, :, 1], mag, sn, MUL))
            step(v.tensor_tensor(t0, shf, shf, MUL))
            step(v.tensor_scalar(t0, t0, -2.0, 1.0, MUL, ADD))
            step(v.tensor_tensor(pR[:, :, 1], mag, t0, MUL))
            scratch = [VT[:].rearrange("p g m -> p (g m)")[:, 0:4 * GROUPS], VT[:].rearrange("p g m -> p (g m)")[:, 4 * GROUPS:8 * GROUPS]]
            for n in (1, 2, 4):
                x, y = (z[:, 0:n * GROUPS].rearrange("p (g j) -> p g j", j=n) for z in scratch)

                def top(t):
                    return t[:, :, n:n + 1].to_broadcast([P, GROUPS, n])

                own.mark(v.tensor_tensor(x, pR[:, :, 1:n + 1], top(pR), MUL))
                step(v.tensor_tensor(y, pI[:, :, 1:n + 1], top(pI), MUL))
                step(v.tensor_tensor(pR[:, :, n + 1:2 * n + 1], x, y, SUB))
                own.mark(v.tensor_tensor(x, pR[:, :, 1:n + 1], top(pI), MUL))
                step(v.tensor_tensor(y, pI[:, :, 1:n + 1], top(pR), MUL))
                step(v.tensor_tensor(pI[:, :, n + 1:2 * n + 1], x, y, ADD))
            for s in range(CHUNK):
                own.mark(v.tensor_copy(revs[0][:, :, s], pR[:, :, CHUNK - 1 - s]))
                own.mark(v.tensor_copy(revs[1][:, :, s], pI[:, :, CHUNK - 1 - s]))
            own.mark(v.tensor_copy(lam8[:, 0, :], pR[:, :, CHUNK]))
            own.mark(v.tensor_copy(lam8[:, 1, :], pI[:, :, CHUNK]))
            own.mark(v.tensor_scalar(lam8[:, 2, :], pI[:, :, CHUNK], -1.0, None, MUL))
            own.mark(v.tensor_scalar(lb1, pR[:, :, 1], -1.0, None, ADD))
            own.mark(v.tensor_tensor(t0, aR, aR, MUL))
            step(v.tensor_tensor(t1_, aI, aI, MUL))
            step(v.tensor_tensor(t0, t0, t1_, ADD))
            step(v.reciprocal(rden, t0))
            own.mark(v.tensor_tensor(t0, lb1, aR, MUL))
            step(v.tensor_tensor(t1_, pI[:, :, 1], aI, MUL))
            step(v.tensor_tensor(t0, t0, t1_, ADD))
            step(v.tensor_tensor(fr, t0, rden, MUL))
            own.mark(v.tensor_tensor(t0, pI[:, :, 1], aR, MUL))
            step(v.tensor_tensor(t1_, lb1, aI, MUL))
            step(v.tensor_tensor(t0, t0, t1_, SUB))
            step(v.tensor_tensor(fi, t0, rden, MUL))
            own.mark(v.tensor_scalar(b2[:], b2[:], sign[:, 1:2], None, MUL))
            own.mark(v.tensor_scalar(c1[:], c1[:], sign[:, 0:1], None, MUL))
            step(v.tensor_scalar(c2[:], c2[:], -1.0, None, MUL))

            def over_n(z):
                return z.unsqueeze(2).to_broadcast([P, GROUPS, GC])

            own.mark(v.tensor_tensor(bb1[:], b1[:], over_n(fr), MUL))
            step(v.tensor_tensor(bt[:], b2[:], over_n(fi), MUL))
            step(v.tensor_tensor(bb1[:], bb1[:], bt[:], ADD))
            own.mark(v.tensor_tensor(bb2[:], b2[:], over_n(fr), MUL))
            step(v.tensor_tensor(bt[:], b1[:], over_n(fi), MUL))
            v.tensor_tensor(bb2[:], bb2[:], bt[:], SUB).then_inc(S["prep_dve"], 1)
            dve.wait_ge(S["prep_dve"], 1)

            piece(len(pieces))
            read_turns(setup[12:])

            def state_weights(b):
                gs = ds(b * GB, GB)

                def blocks(z):
                    return z[:].rearrange("p g (s n) -> p g s n", n=GC)

                dve.wait_ge(S["w_flipped"], b + 1)
                for z, power, rows in ((V, revs[0], bb1), (VT, revs[1], bb2)):
                    ins = v.tensor_tensor(blocks(z), power[:, gs, :].unsqueeze(3).to_broadcast([P, GB, CHUNK, GC]),
                                          rows[:, gs, :].unsqueeze(2).to_broadcast([P, GB, CHUNK, GC]), MUL)
                    own.mark(ins)
                own.settle()
                v.tensor_tensor(V[:], V[:], VT[:], ADD).then_inc(S["v_ready"], 1)
                dve.wait_ge(S["v_ready"], b + 1)

            def ssm_pass(i, last=False):
                for u in range(UNITS):
                    c = u + 2
                    if not (last and c >= UNITS):
                        split_low(i * UNITS + c, c % UNITS, KD)
                    if u == 1:
                        state_weights(i * 2 - 2 * UNITS)
                state_weights(i * 2 + (1 - 2 * UNITS))
                ada_out(i)

            with dve.Fori(UNITS, 2 * UNITS - 1) as i:
                own.begin(i, 4, first=UNITS)
                ssm_pass(i)
                own.end(UNITS - 1)
            ssm_pass(2 * UNITS - 1, last=True)

            def modulate(k, shift, scale, high, low, ready, tmp):
                own.mark(v.tensor_scalar(tmp[:, 0:NP], xT[:, k, 0:NP], mod[:, scale + k, 0:1], mod[:, shift + k, 0:1], MUL, ADD))
                own.step(v.tensor_tensor(samples(tmp), samples(xT[:, k, :]), per_sample(mod[:, scale + k, 1:NC]), MUL))
                own.step(v.tensor_tensor(samples(tmp), samples(tmp), per_sample(mod[:, shift + k, 1:NC]), ADD))
                own.step(v.tensor_copy(high[:, k, :], tmp))
                v.tensor_tensor(low[:, k, :], tmp, high[:, k, :].bitcast(F32), SUB).then_inc(ready, 1)

            SH1, SC1, G1, SH2, SC2, G2 = (m * KD for m in range(MODS))
            dve.wait_ge(S["ada_mod"], 1 + 2 * UNITS)
            own.step(v.tensor_scalar(mod[:, SC1:SC1 + KD, :], mod[:, SC1:SC1 + KD, :], 1.0, None, ADD))
            for k in range(KD):
                modulate(k, SH1, SC1, hH, hL, S["h_ready"], small64[:].rearrange("p a b -> p (a b)")[:, (k % 2) * T:(k % 2 + 1) * T])

            def split_ahead(i, n0, cc, next_ks, own_ks):
                c = cc + 2
                if c < 4:
                    split_low(i * 4 + (n0 + c), c, own_ks[c])
                elif next_ks:
                    split_low(i * 4 + (n0 + c), c - 4, next_ks[c - 4])

            def start_stream(n0, ks):
                for c in range(2):
                    split_low(n0 + c, c, ks[c])

            for x in range(3):
                split_low(PROJ + x, x, KD, x)

            def proj_pass(i, last=False):
                for x, (kind, m) in enumerate(items):
                    y = x + 3
                    if not (last and y >= ITEMS):
                        split_low(i * ITEMS + (PROJ + y), y % RING, KD, y % 3)
                    if kind == "chunk" and m % 2:
                        ada_out(i * 2 + (2 * UNITS + m // 2))

            with dve.Fori(0, KA - 1) as i:
                proj_pass(i)
            proj_pass(KA - 1, last=True)
            dve.wait_ge(S["ada_mod"], 1 + MODS * UNITS)
            own.mark(v.tensor_scalar(mod[:, G1:G1 + KD, :], mod[:, G1:G1 + KD, :], 1.0, None, ADD))
            own.step(v.tensor_scalar(mod[:, SC2:, :], mod[:, SC2:, :], 1.0, None, ADD))
            f = flips[0]
            turns = list(proj_turns())
            read_turns(turns[0:12])
            dve.wait_ge(S["u_stored"], 32)
            read_turns(turns[12:])

            dve.wait_ge(S["k_stored"], 32)
            dve.wait_ge(S["bias_landed"], 16)
            dve.wait_ge(S["bias_spread"], 1)
            new = sS[0:ST, PAGES, :]

            def attend(i, front=True, back=True):
                j = i - 1

                def read_page(p):
                    dve.wait_ge(S["k_flipped"], i * PAGES + (p + KSLOTS + 1))
                    dve.wait_ge(S["scored"], i * PAGES + (p + 1))
                    v.tensor_copy(kTp[p % 2][:, 0:4, :].rearrange("p h k -> p (h k)"), bank[0][:]).then_inc(S["kt_dve"], 1)

                def scores():
                    dve.wait_ge(S["z_turned"], j + 2)
                    own.mark(v.scalar_tensor_tensor(out=sz[:, 0:PAGES, :], in0=bank[2][:].rearrange("p (a c) -> p a c", a=PAGES), scalar=SCALE,
                                                    in1=bias_q[:].unsqueeze(1).to_broadcast([P, PAGES, HQ]), op0=MUL, op1=ADD))
                    own.step(v.scalar_tensor_tensor(out=sz[0:ST, PAGES, :], in0=bank[3][0:ST, 0:HQ], scalar=SCALE, in1=bias_q[0:ST, :], op0=MUL, op1=ADD))
                    v.scalar_tensor_tensor(out=se[:], in0=sz[:], scalar=-1.0, in1=sz[:], op0=MUL, op1=ALU.min).then_inc(S["s_e_in"], 1)

                def head_scores():
                    dve.wait_ge(S["pz_done"], j + 1)
                    own.step(v.tensor_scalar(pz[:], bank[4][:, 0:384], SCALE, bias_h[:, ds(j, 1)], MUL, ADD))
                    v.scalar_tensor_tensor(out=pe_[:], in0=pz[:], scalar=-1.0, in1=pz[:], op0=MUL, op1=ALU.min).then_inc(S["p_exp_in"], 1)

                def softplus():
                    dve.wait_ge(S["s_ln"], j + 1)
                    own.mark(v.scalar_tensor_tensor(out=sS[:], in0=sz[:], scalar=0.0, in1=se[:], op0=ALU.max, op1=ADD))
                    dve.wait_ge(S["p_ln"], j + 1)
                    own.step(v.scalar_tensor_tensor(out=pS[:], in0=pz[:], scalar=0.0, in1=pe_[:], op0=ALU.max, op1=ADD))
                    v.scalar_tensor_tensor(out=new, in0=mask_new[:], scalar=1.0, in1=new, op0=ADD, op1=MUL).then_inc(S["s_s"], 1)
                    v.scalar_tensor_tensor(out=pS[:], in0=masks[:], scalar=1.0, in1=pS[:], op0=ADD, op1=MUL).then_inc(S["p_s"], 1)

                def log_weights():
                    dve.wait_ge(S["p_cs"], j + 1)
                    own.step(v.tensor_tensor(pz[:], pz[:], bank[4][:, 0:384], SUB))
                    v.scalar_tensor_tensor(out=pe_[:], in0=masks[:], scalar=1e30, in1=pz[:], op0=MUL, op1=ADD).then_inc(S["p_arg"], 1)
                    dve.wait_ge(S["s_cs"], j + 1)
                    own.mark(v.tensor_tensor(se[:, 0:PAGES, :], sz[:, 0:PAGES, :], bank[3][:].rearrange("p (a c) -> p a c", a=PAGES), SUB))
                    own.step(v.tensor_tensor(sz[0:ST, PAGES, :], sz[0:ST, PAGES, :], bank[4][0:ST, 384:384 + HQ], SUB))
                    v.scalar_tensor_tensor(out=se[0:ST, PAGES, :], in0=mask_new[:], scalar=1e30, in1=sz[0:ST, PAGES, :], op0=MUL, op1=ADD)\
                        .then_inc(S["s_arg"], 1)

                def outputs():
                    dve.wait_ge(S["p_pv"], j + 2)
                    o = bank[4][:, 0:NP].unsqueeze(1)
                    own.step(v.tensor_copy(attH[:, ds(j, 1), 0:NP], o))
                    v.tensor_tensor(attL[:, ds(j, 1), 0:NP], o, attH[:, ds(j, 1), 0:NP].bitcast(F32), SUB).then_inc(S["att_p"], 1)
                    dve.wait_ge(S["pv_rows"], j + 2)
                    v.tensor_copy(o_rows[:, 512:], bank[6][0:ST, :]).then_inc(S["o_dve"], 1)
                    dve.wait_ge(S["s_pv"], j + 2)
                    o = bank[4][:, 512 - HQ:].rearrange("p (h q) -> p h q", q=ST)
                    cols = ds(j * ST + NP, ST)
                    own.step(v.tensor_copy(attH[:, :, cols], o))
                    v.tensor_tensor(attL[:, :, cols], o, attH[:, :, cols].bitcast(F32), SUB).then_inc(S["att_s"], 1)

                steps = {0: scores, 3: softplus, 5: log_weights} if back else {}
                for p in range(PAGES):
                    if p in steps:
                        steps[p]()
                    if front:
                        read_page(p)
                    if back and p == 0:
                        head_scores()
                if back:
                    outputs()

            attend(0, back=False)
            with dve.Fori(1, SB) as i:
                own.begin(i, 10, first=1)
                attend(i)
                own.end(SB - 1)
            attend(SB, front=False)

            with dve.Fori(0, BATCHES) as i:
                dve.wait_ge(S["w1_landed"], i * 16 + 16)
                own.begin(i, 2)
                own.mark(v.tensor_scalar(W2[:, :, 0:GS], W1[:, :, GS:P], -1.0, None, MUL))
                v.tensor_copy(W2[:, :, GS:P], W1[:, :, 0:GS]).then_inc(S["w2_ready"], 1)
                dve.wait_ge(S["g_done"], i + 2)
                own.mark(v.tensor_copy(G[:, 0, ds(i * GB, GB), :], bank[5][:, 0:GB * CT].rearrange("p (g c) -> p g c", g=GB)))
                v.tensor_copy(G[:, 1, ds(i * GB, GB), :], bank[6][:, 0:GB * CT].rearrange("p (g c) -> p g c", g=GB)).then_inc(S["g_read"], 1)
                own.end(BATCHES)
            dve.wait_ge(S["g_read"], BATCHES + 1)
            own.step(v.memset(Z[:, :, :, 0], 0.0))
            read_turns(state_turns())
            dve.wait_ge(S["flips_read"], flips[0])
            own.step(v.tensor_scalar(h0[:, 1], h0[:, 1], sign[:, 1:2], None, MUL))
            l_re, l_im, l_neg = (lam8[:, n, :] for n in range(3))
            with dve.Fori(0, CP) as c:
                own.begin(c, 5)

                def state(n, half):
                    return Z[:, half, :, ds(c + n, 1)].rearrange("p g o -> p (g o)")

                for half in range(2):
                    own.mark(v.tensor_tensor(t1[:, half, :], state(0, half), l_re, MUL))
                    ins = v.tensor_tensor(t2[:, half, :], state(0, 1 - half), l_neg if half else l_im, MUL)
                    own.mark(ins)
                own.settle()
                own.step(v.tensor_tensor(t1[:], t1[:], t2[:], ADD))
                v.tensor_tensor(Z[:, :, :, ds(c + 1, 1)].rearrange("p v g o -> p v (g o)"), t1[:],
                                G[:, :, :, ds(c, 1)].rearrange("p v g o -> p v (g o)"), ADD).then_inc(S["state_step"], 1)
                dve.wait_ge(S["state_step"], c + 1)
                own.end(CP)

            def over_b(z):
                return z.unsqueeze(2).to_broadcast([P, GROUPS, SB])

            own.mark(v.tensor_copy(Z[:, 0, :, CP + 1:], h0[:, 0]))
            own.mark(v.tensor_tensor(zf[:], h0[:, 0], over_b(l_re), MUL))
            own.step(v.tensor_tensor(u1[:], h0[:, 1], over_b(l_im), MUL))
            own.step(v.tensor_tensor(zf[:], zf[:], u1[:], ADD))
            v.tensor_tensor(zf[:], zf[:], G[:, 0, :, CP:], ADD).then_inc(S["scanned"], 1)
            read_turns(final_state_turns())
            for c in range(KA):
                dve.wait_ge(S["ytk_turned"], c + 1)
                if c >= 2:
                    dve.wait_ge(S["y_gelu"], c - 1)
                v.scalar_tensor_tensor(out=ypre[c % 2][:], in0=projT[:, c, :], scalar=cw[:, 3 * 2 * JF + c:3 * 2 * JF + c + 1],
                                       in1=bank[4 + c % 4][:, 0:T], op0=MUL, op1=ADD).then_inc(S["y_pre"], 1)
                if c >= 1:
                    dve.wait_ge(S["y_gelu"], c)
                    own.step(v.tensor_copy(ygH[:, c - 1, :], ygl[(c - 1) % 2][:]))
                    v.tensor_tensor(ygL[:, c - 1, :], ygl[(c - 1) % 2][:], ygH[:, c - 1, :].bitcast(F32), SUB).then_inc(S["y_ready"], 1)
            c = KA
            dve.wait_ge(S["y_gelu"], c)
            own.step(v.tensor_copy(ygH[:, c - 1, :], ygl[(c - 1) % 2][:]))
            v.tensor_tensor(ygL[:, c - 1, :], ygl[(c - 1) % 2][:], ygH[:, c - 1, :].bitcast(F32), SUB).then_inc(S["y_ready"], 1)

            start_stream(GLU, ks_of["glu"])
            for m in range(KA):
                i, cc = m // 4, m % 4
                dve.wait_ge(S["y_ready"], KA)
                dve.wait_ge(acc_free[cc % 2], nth_pair(GLU + m) + 2)
                dve.wait_ge(S["s_ready"], m)
                own.step(v.tensor_tensor(part[0][:], ygH[:, m, :].bitcast(F32), ygL[:, m, :].bitcast(F32), ADD))
                own.step(v.tensor_tensor(part[0][:], part[0][:], gate[cc % 2][:], MUL))
                own.step(v.tensor_copy(sH[:, m, :], part[0][:]))
                v.tensor_tensor(sL[:, m, :], part[0][:], sH[:, m, :].bitcast(F32), SUB).then_inc(S["s_ready"], 1)
                split_ahead(i, GLU, cc, ks_of["glu"] if i == 0 else ks_of["merge"], ks_of["glu"])

            def merge_pass(i, next_ks):
                for cc in range(4):
                    if cc % 2:
                        h = cc // 2
                        dve.wait_ge(acc_free[0], i * 2 + (nth_pair(MERGE) + h + 2))
                        dve.wait_ge(S["chunk_done"], i * 4 + (MERGE + cc + 3))
                        v.tensor_tensor(part[h][:], bank[1][:, 0:T], gate[h][:], MUL).then_inc(acc_free[1], 1)
                    if cc == 3:
                        dve.wait_ge(acc_free[1], i * 2 + (nth_pair(MERGE) + 3))
                        v.tensor_tensor(merged[:, ds(i, 1), :].rearrange("p o t -> p (o t)"), part[0][:], part[1][:], ADD).then_inc(S["merged_ready"], 1)
                    split_ahead(i, MERGE, cc, next_ks, ks_of["merge"])

            passes(dve, "merge", None, 0, merge_pass)
            dve.wait_ge(S["merged_ready"], KD)
            dve.wait_ge(S["chunk_done"], OUT + 2)
            for k in range(KD):
                own.step(v.tensor_copy(mH[:, k, :], merged[:, k, :]))
                v.tensor_tensor(mL[:, k, :], merged[:, k, :], mH[:, k, :].bitcast(F32), SUB).then_inc(S["m_ready"], 1)

            def residual(src, m, gain, ready, free=None):
                r = res[0]
                col = mod[:, ds(m + gain, 1), :].rearrange("p o c -> p (o c)")
                own.mark(v.tensor_scalar(r[:, 0:NP], src[:, 0:NP], col[:, 0:1], None, MUL))
                ins = v.tensor_tensor(samples(r[:]), samples(src), per_sample(col[:, 1:NC]), MUL)
                if free:
                    ins.then_inc(free[0], 1)
                    own.settle()
                    dve.wait_ge(free[0], free[1])
                else:
                    own.step(ins)
                x = xT[:, ds(m, 1), :].rearrange("p o t -> p (o t)")
                v.scalar_tensor_tensor(out=x, in0=x, scalar=ALPHA, in1=r[:], op0=MUL, op1=ADD).then_inc(ready, 1)

            def out_pass(i, next_ks):
                for cc in range(4):
                    dve.wait_ge(S["chunk_done"], i * 4 + (OUT + cc + 3))
                    dve.wait_ge(S["x_pre"], i * 4 + (cc + 1))
                    residual(bank[cc % 2][:, 0:T], i * 4 + cc, G1, S["x_pre"], (acc_free[cc % 2], i * 2 + (nth_pair(OUT) + cc // 2 + 2)))
                    split_ahead(i, OUT, cc, next_ks, ks_of["out"])

            passes(dve, "out", own, 4, out_pass)

            def layer_norm(nth, g0, b0):
                dve.wait_ge(S["mean_done"], nth + 1)
                own.step(v.tensor_copy(mu[:], bank[2][:, 0:T]))
                for k in range(KD):
                    v.tensor_tensor(xT[:, k, :], xT[:, k, :], mu[:], SUB).then_inc(S["centred"], 1)
                dve.wait_ge(S["var_done"], nth + 1)
                v.tensor_scalar(var[:], bank[3][:, 0:T], EPS, None, ADD).then_inc(S["var_ready"], 1)
                dve.wait_ge(S["sd_ready"], nth + 1)
                own.step(v.reciprocal(rstd[:], sd[:]))
                own.step(v.tensor_tensor(newton[:], rstd[:], rstd[:], MUL))
                own.step(v.tensor_tensor(newton[:], newton[:], var[:], MUL))
                own.step(v.tensor_scalar(newton[:], newton[:], -0.5, 1.5, MUL, ADD))
                own.step(v.tensor_tensor(rstd[:], rstd[:], newton[:], MUL))
                for k in range(KD):
                    own.step(v.tensor_tensor(xT[:, k, :], xT[:, k, :], rstd[:], MUL))
                    ins = v.tensor_scalar(xT[:, k, :], xT[:, k, :], par[:, g0 + k:g0 + k + 1], par[:, b0 + k:b0 + k + 1], MUL, ADD)
                    if nth:
                        ins.then_inc(S["normed"], 1)
                    else:
                        own.step(ins)
                        modulate(k, SH2, SC2, hH, hL, S["h2_ready"], res[k % 2][:])

            dve.wait_ge(S["state_stored"], 64)
            read_turns(conv_state_turns())
            layer_norm(0, 96, 112)

            done, pairs = 0, 0
            j0 = 0
            for q, nj in enumerate(QUARTERS):
                n0 = first_of[f"up{q}"]

                def up_pass(i, next_ks):
                    for cc in range(4):
                        split_ahead(i, n0, cc, next_ks, ks_of["up0"])
                        n = i * 4 + (done + cc)
                        ch = i * 2 + (j0 + cc // 2 + (cc % 2) * JF)
                        dst = cvG if cc % 2 else cvV
                        dve.wait_ge(S["halo"], n + 1)
                        dve.wait_ge(S["conv_ev"], n + 1)
                        dve.wait_ge(acc_free[cc % 2], i * 2 + (nth_pair(n0) + cc // 2 + 2))
                        e = ext[cc]
                        own.step(v.tensor_scalar(dst[:, 0:EXT - 2], e[:, 0:EXT - 2], cw[:, ds(ch, 1)], par[:, ds(ch + P, 1)], MUL, ADD))
                        own.step(v.scalar_tensor_tensor(out=dst[:, 0:EXT - 2], in0=e[:, 1:EXT - 1], scalar=cw[:, ds(ch + 2 * JF, 1)], in1=dst[:, 0:EXT - 2], op0=MUL, op1=ADD))
                        v.scalar_tensor_tensor(out=dst[:, 0:EXT - 2], in0=e[:, 2:EXT], scalar=cw[:, ds(ch + 4 * JF, 1)],
                                               in1=dst[:, 0:EXT - 2], op0=MUL, op1=ADD).then_inc(S["ext_read"], 1)
                        dve.wait_ge(S["ext_read"], n + 5)
                        if cc % 2:
                            j = i * 2 + cc // 2
                            dve.wait_ge(S["gelu_done"], i * 2 + (pairs + cc // 2 + 1))
                            dve.wait_ge(S["f_ready"], i * 2 + (pairs + cc // 2 + 1))
                            own.mark(v.tensor_tensor(prod[:, 0:NP], cvV[:, 0:NP], cvG[:, 0:NP], MUL))
                            own.step(v.tensor_tensor(samples(prod[:]), late(cvV), late(cvG), MUL))
                            own.step(v.tensor_copy(fH[:, ds(j, 1), :], prod[:].unsqueeze(1)))
                            v.tensor_tensor(fL[:, ds(j, 1), :], prod[:].unsqueeze(1), fH[:, ds(j, 1), :].bitcast(F32), SUB).then_inc(S["f_ready"], 1)

                passes(dve, f"up{q}", own, 14, up_pass)
                done += 2 * nj
                pairs += nj
                n0 = first_of[f"down{q}"]

                def down_pass(i, next_ks):
                    for cc in range(4):
                        dve.wait_ge(S["chunk_done"], i * 4 + (n0 + cc + 3))
                        y = yacc[:, ds(i * 4 + cc, 1), :].rearrange("p o t -> p (o t)")
                        acc = bank[cc % 2][:, 0:T]
                        ins = v.tensor_tensor(y, y, acc, ADD) if q else v.tensor_copy(y, acc)
                        ins.then_inc(acc_free[cc % 2], 1)
                        split_ahead(i, n0, cc, next_ks, ks_of[f"down{q}"])

                passes(dve, f"down{q}", None, 0, down_pass)
                j0 += nj
            for s in acc_free:
                dve.wait_ge(s, nth_pair(FFN + sum(2 * nj + KD for nj in QUARTERS)) + 1)
            for m in range(KD):
                residual(yacc[:, m, :], m, G2, S["x_pre"])
                dve.wait_ge(S["x_pre"], KD + m + 2)
            read_turns(rows_out_turns())
            layer_norm(1, P + 88, P + 104)
            read_turns(y_turns())


_INS = ["x_prompt", "x_sample", "cache_k", "cache_v", "state_ssm_re", "state_ssm_im", "state_conv", "page_table",
        "c_prompt", "c_sample", "w_ada", "b_ada", "w_in", "w_att_br", "w_ssm_br", "w_out", "sb_bias",
        "ssm_a_re", "ssm_a_im", "ssm_log_dt", "ssm_b_re", "ssm_b_im", "ssm_c_re", "ssm_c_im", "ssm_d",
        "w_glu", "b_glu", "ln1_g", "ln1_b", "w_up", "conv_w", "conv_b", "w_down", "ln2_g", "ln2_b"]
_OUTS = [(1, NP, D), (SB, ST, D), (1, 1, NP, HEADS, HD), (1, 1, NP, HEADS, HD), (1, 1, GROUPS, GS), (1, 1, GROUPS, GS),
         (1, 1, 2, 2 * FF), (1, SB, ST, HEADS, HD), (1, SB, ST, HEADS, HD), (1, SB, GROUPS, GS), (1, SB, GROUPS, GS),
         (1, SB, 2, 2 * FF)]


def kernel(**inputs):
    import numpy as np
    import concourse.bacc as bacc
    from concourse.bass_utils import run_bass_kernel_spmd

    nc = bacc.Bacc("TRN2", target_bir_lowering=False, num_devices=1)
    arrays, args = {}, []
    for name in _INS:
        a = np.ascontiguousarray(inputs[name])
        arrays[f"in_{name}"] = a
        args.append(nc.dram_tensor(f"in_{name}", a.shape, mybir.dt.from_np(a.dtype), kind="ExternalInput").ap())
    for i, shape in enumerate(_OUTS):
        args.append(nc.dram_tensor(f"out_{i}", shape, F32, kind="ExternalOutput").ap())
    hybrid_step(nc, *args)
    r = run_bass_kernel_spmd(nc, [arrays], core_ids=[0])
    return tuple(r.results[0][f"out_{i}"] for i in range(len(_OUTS)))
```

```python
import math

import concourse.bass as bass
from concourse import mybir

P = 128
F32 = mybir.dt.float32
F32R = mybir.dt.float32r
I32 = mybir.dt.int32
ALU = mybir.AluOpType
ACT = mybir.ActivationFunctionType
ds = bass.ds

D = 2048
NP = 256
SB, ST = 8, 8
T = NP + SB * ST
HEADS, HD = 8, 128
AW = HEADS * HD
SW = D - AW
GROUPS, GC, GS = 64, 16, 64
FF = 5632
PAGE, PAGES = 128, 8
KD = D // P
KA = AW // P
JF = FF // P
MODS = 6
NC = 1 + SB
CHUNK = 8
CP = NP // CHUNK
CT = CP + SB
GB = P // GC
BATCHES = GROUPS // GB
POOL_GROUPS = 3
ALPHA = 2.0 ** 0.25
EPS = 1e-5
SCALE = HD ** -0.5
EXT = 2 + NP + SB * (2 + ST)
QUARTERS = [12, 12, 10, 10]

TWO_PI = (6.28125, 0.0019350051879882812, 2.0 * math.pi - 6.28125 - 0.0019350051879882812)
ROUND = 1.5 * 2.0 ** 23
PI_IN = 3.1415925
LOG_2 = (0.693359375, math.log(2.0) - 0.693359375)

RING = 4
BLOCK = 512
KSLOTS = 3


class Own:

    def __init__(self, eng, sem):
        self.eng, self.sem, self.count, self.index = eng, sem, 0, None

    def begin(self, index, per_pass, first=0):
        self.index, self.per_pass, self.k, self.first = index, per_pass, 0, first

    def end(self, passes):
        assert self.k == self.per_pass, (self.k, self.per_pass)
        self.count, self.index = self.count + passes * self.per_pass, None

    def mark(self, instruction):
        instruction.then_inc(self.sem, 1)
        if self.index is None:
            self.count += 1
        else:
            self.k += 1

    def settle(self):
        at = self.count if self.index is None else self.index * self.per_pass + (self.count - self.first * self.per_pass + self.k)
        self.eng.wait_ge(self.sem, at)

    def step(self, instruction):
        self.mark(instruction)
        self.settle()


def hybrid_step(nc, x_prompt, x_sample, cache_k, cache_v, state_ssm_re, state_ssm_im, state_conv, page_table,
                c_prompt, c_sample, w_ada, b_ada, w_in, w_att_br, w_ssm_br, w_out, sb_bias,
                ssm_a_re, ssm_a_im, ssm_log_dt, ssm_b_re, ssm_b_im, ssm_c_re, ssm_c_im, ssm_d,
                w_glu, b_glu, ln1_g, ln1_b, w_up, conv_w, conv_b, w_down, ln2_g, ln2_b,
                y_prompt, y_sample, k_prompt, v_prompt, ssm_re_prompt, ssm_im_prompt, conv_prompt,
                k_sample, v_sample, ssm_re_sample, ssm_im_sample, conv_sample):
    n_phys = cache_k.shape[1]
    S = {}

    def sem(name):
        S[name] = nc.alloc_semaphore(name)
        return S[name]

    base = (nc.sbuf_base + 127) // 128 * 128

    def at(name, shape, offset, dtype=F32):
        return nc.alloc_sbuf_tensor_at(name, shape, dtype, offset=base + offset)

    CH = T * 4
    small, r_x, r_h = 0, 16384, 16384 + KD * CH
    r_ring = r_h + 2 * KD * CH
    r_split = r_ring + RING * KD * P * 4
    r_u = r_split + 4 * KD * P * 4
    r_q, r_k, r_v = r_u + KA * CH, r_u + 2 * KA * CH, r_u + 3 * KA * CH
    r_vtok = r_v + KA * CH
    r_attl = r_vtok + 3 * AW * 4
    r_tail = r_attl + KA * CH

    mod = at("mod", [P, MODS * KD, NC], small)
    par = at("par", [P, 256], small + 3456)
    cw = at("cw", [P, 3 * 2 * JF + KA], small + 4480)
    ident = at("ident", [P, P], small + 5568)
    mean_of = at("mean_of", [P, P], small + 6080)
    later = at("later", [P, P], small + 6592)
    ones = at("ones", [P, P], small + 7104)
    r_small2 = small + 7616
    masks = at("masks", [P, 384], small + 13312)
    lam8 = at("lam8", [P, 3, GROUPS], small + 14848)
    bias_h = at("bias_h", [P, HEADS], small + 15616)
    sign = at("sign", [P, 2], small + 15648)
    pages = at("pages", [1, SB * PAGES], small + 15680, I32)
    mask_new = at("mask_new", [ST, HEADS * ST], small + 15936)

    xT = at("xT", [P, KD, T], r_x)
    hH, hL = (at(n, [P, KD, T], r_h + i * KD * CH, F32R) for i, n in enumerate(("hH", "hL")))
    ring = [at(f"ring{i}", [P, KD, P], r_ring + i * KD * P * 4) for i in range(RING)]
    wH = [at(f"wH{i}", [P, KD, P], r_split + 2 * i * KD * P * 4, F32R) for i in range(2)]
    wL = [at(f"wL{i}", [P, KD, P], r_split + (2 * i + 1) * KD * P * 4, F32R) for i in range(2)]
    wH.append(at("wH2", [P, KD, P], r_vtok, F32R))
    wL.append(at("wL2", [P, KD, P], r_vtok + KD * P * 4, F32R))
    projT = at("projT", [P, 4 * KA, T], r_u)

    xrows = at("xrows", [P, 3, D], r_h)
    crows = at("crows", [NC, D], r_h + 24576)
    csil = at("csil", [NC, D], r_h + 32768)
    b_raw = at("b_raw", [GROUPS, 3, GS * GC], r_u + 8704)
    c_raw = at("c_raw", [GROUPS, GC, 3, GS], r_u + 8704 + 12288)
    zeros = at("zeros", [112, AW], r_u + 8704 + 24576 + 512)
    r_tail2 = r_vtok + 16384
    pr = at("pr", [P, 2, P], r_tail2)
    prw = at("prw", [2 * JF, 3, P], r_tail2 + 1024)
    prd = at("prd", [KA, P], r_tail2 + 2560)
    a_raw = at("a_raw", [GROUPS, 2, P], r_tail2 + 3072)
    log_dt = at("log_dt", [P, GROUPS], r_tail2 + 4096)
    small64 = at("small64", [P, 20, GROUPS], r_tail2 + 4352)
    two_n = at("two_n", [P, GROUPS], r_tail2 + 4352 + 5120 + 576, I32)
    cT = at("cT", [P, KD, NC], r_tail2 + 4352 + 5120)
    cHL = at("cHL", [P, KD, 2 * NC], r_small2, F32R)
    ada_rows = at("ada_rows", [2 * NC, BLOCK], r_small2 + 1152)
    add_up = at("add_up", [2 * NC, NC], r_small2 + 3200)
    pows = [at(f"pow{n}", [P, GROUPS, CHUNK + 1], r_u + i * 2304) for i, n in enumerate(("R", "I"))]
    revs = [at(f"rev{n}", [P, GROUPS, CHUNK], r_u + 4608 + i * 2048) for i, n in enumerate(("R", "I"))]
    b1, b2, c1, c2 = (at(n, [P, GROUPS, GC], r_vtok + i * 4096) for i, n in enumerate(("b1", "b2", "c1", "c2")))
    bb1, bb2, bt = (at(n, [P, GROUPS, GC], r_h + 24576 + i * 4096) for i, n in enumerate(("bb1", "bb2", "bt")))
    V, VT, PT, PX, P_, w1s = (at(n, [P, GB, P], r_u + 8704 + i * 4096)
                              for i, n in enumerate(("V", "VT", "PT", "PX", "Pm", "w1s")))
    o_s = at("o_s", [P, P], r_u + 8704 + 6 * 4096)

    vtok = at("vtok", [P, 3, AW], r_vtok)
    stage = at("stage", [P, 3, AW], r_attl)
    kstage = at("kstage", [P, 3, AW], r_ring)

    vpage = [at(f"vpage{i}", [P, AW], r_ring + i * 4096) for i in range(PAGES)]
    kpage = [at(f"kpage{i}", [P, AW], o) for i, o in enumerate((r_split, r_split + 4096, r_vtok + 2 * AW * 4))]
    kTp = [at(f"kTp{i}", [P, HEADS, PAGE], r_split + 8192 + i * 4096) for i in range(2)]
    HQ = HEADS * ST
    sz, se, sS, sR = (at(n, [P, PAGES + 1, HQ], r_split + 16384 + i * 2304) for i, n in enumerate(("sz", "se", "sS", "sR")))
    pz, pe_, pS = (at(n, [P, 384], r_split + 25600 + i * 1536) for i, n in enumerate(("pz", "pe_", "pS")))
    q_block = at("q_block", [P, HEADS * (HQ + ST)], r_split + 30208)
    z_rows = at("z_rows", [HQ, PAGES, PAGE], r_tail)
    zn_rows = at("zn_rows", [HQ, ST], r_small2 + 5120)
    o_rows = at("o_rows", [ST, AW], r_split + 16384 + 2 * 2304)
    kh = at("kh", [P, NP], r_small2 + 4096)
    vh = at("vh", [P, 2, HD], r_tail + 4096)
    bias_q = at("bias_q", [P, HQ], r_split + 32512)
    vnew = at("vnew", [ST, AW], r_small2)
    attH, attL = at("attH", [P, KA, T], r_v, F32R), at("attL", [P, KA, T], r_attl, F32R)

    U = at("U", [P, GROUPS, CT], r_q)
    G = at("G", [P, 2, GROUPS, CT], r_ring)
    Z = at("Z", [P, 2, GROUPS, CT + 1], r_ring + 20480)
    r_ssm = r_ring + 20480 + 20992
    W1 = [at(f"W1_{i}", [P, GB, P], r_ssm + i * 4096) for i in range(2)]
    Uraw = [at(f"Uraw{i}", [CT, CHUNK, P], o) for i, o in enumerate((r_ssm + 8192, r_k + 6144))]
    Ug = [at(f"Ug{i}", [CT, GB, P], o) for i, o in enumerate((r_ssm + 12288, r_tail))]
    r_out = (r_ssm, r_ring)
    Kt, Pt = ([at(f"{n}{i}", [P, CHUNK, P], o + 4096 * k) for i, o in enumerate(r_out)] for k, n in enumerate(("Kt", "Pt")))
    Yt = [at(f"Yt{i}", [CT, CHUNK, GB, GC], o + 8192) for i, o in enumerate(r_out)]
    Us, Hs = ([at(f"{n}{i}", [P, GB, CT], o + 12288 + 1280 * k) for i, o in enumerate(r_out)] for k, n in enumerate(("Us", "Hs")))
    wide1 = at("wide1", [P, GROUPS, CP // 2], r_k + 6144)
    wide2 = at("wide2", [P, GROUPS, CP // 2], r_tail)
    lam16 = at("lam16", [P, 3, GROUPS], r_tail + 4096)
    swap = at("swap", [P, P], r_vtok + 9216)
    h0raw = at("h0raw", [GROUPS, SB, 3, GS], r_k)
    h0 = at("h0", [P, 2, GROUPS, SB], r_vtok)
    t1 = at("t1", [P, 2, GROUPS], r_vtok + 4096)
    t2 = at("t2", [P, 2, GROUPS], r_vtok + 4096 + 512)
    u1 = at("u1", [P, GROUPS, SB], r_vtok + 5120)
    zf = at("zf", [P, GROUPS, SB], r_vtok + 7168)
    fin = at("fin", [GROUPS, NC, P], r_small2)
    ytk = at("ytk", [P, 3, SW], r_ring)
    ypre = [at(f"ypre{i}", [P, T], r_vtok + i * CH) for i in range(2)]
    ygl = [at(f"ygl{i}", [P, T], r_vtok + (2 + i) * CH) for i in range(2)]

    ygH, ygL = at("ygH", [P, KA, T], r_q, F32R), at("ygL", [P, KA, T], r_k, F32R)
    sH, sL = at("sH", [P, KA, T], r_u, F32R), at("sL", [P, KA, T], r_vtok, F32R)
    merged = at("merged", [P, KD, T], r_q)
    gate = [at(f"gate{i}", [P, T], r_tail + i * CH) for i in range(2)]
    part = [at(f"part{i}", [P, T], r_tail + (2 + i) * CH) for i in range(2)]
    mH, mL = (at(n, [P, KD, T], r_h + i * KD * CH, F32R) for i, n in enumerate(("mH", "mL")))

    centred_sq = at("centred_sq", [P, KD, T], r_u)
    mu, var, sd, rstd, newton = (at(n, [P, T], r_u + (KD + i) * CH) for i, n in enumerate(("mu", "var", "sd", "rstd", "newton")))
    res = [at(f"res{i}", [P, T], r_u + (KD + 5 + i) * CH) for i in range(2)]

    conv_raw = at("conv_raw", [2 * JF, SB * 2, P], r_u + (KD + 7) * CH)
    conv_st = at("conv_st", [P, SB * 2, 2 * JF], r_small2)
    fH, fL = (at(n, [P, QUARTERS[0], T], r_u + i * QUARTERS[0] * CH, F32R) for i, n in enumerate(("fH", "fL")))
    yacc = at("yacc", [P, KD, T], r_u + 24 * CH)
    r_f, EB = r_u + 40 * CH, (EXT * 4 + 31) // 32 * 32
    ext = [at(f"ext{i}", [P, EXT], r_f + i * EB) for i in range(4)]
    cvV, cvG = (at(n, [P, EXT], r_f + (4 + i) * EB) for i, n in enumerate(("cvV", "cvG")))
    prod = at("prod", [P, T], r_f + 6 * EB)
    rows_out = at("rows_out", [P, NC * 2, 2 * JF], r_f + 6 * EB + CH)
    rows_t = at("rows_t", [2 * JF, NC * 2, P], r_h)
    ytok = at("ytok", [P, 3, D], r_ring)

    bank = [nc.alloc_psum_tensor(f"bank{i}", [P, 512], F32) for i in range(8)]

    u_tok = nc.dram_tensor("u_tok", (T, SW), F32).ap()
    y_tok = nc.dram_tensor("y_tok", (T, SW), F32).ap()
    w1_d = nc.dram_tensor("w1_d", (BATCHES, P, GB * P), F32).ap()
    p_d = nc.dram_tensor("p_d", (BATCHES, P, GB * P), F32).ap()
    taps_d = nc.dram_tensor("taps_d", (P + 112, SW), F32).ap()

    for name in ("c_landed x_landed params_landed ssm_landed pages_landed silu_ready ident_ready consts_ready "
                 "flipped flips_read ada_copied ada_turned ada_mod prep_act prep_dve v_ready w_flipped w_read "
                 "w1_stored taps_stored p_stored zeros_stored h_ready hi_done split_done chunk_done half_hi half_split half_done front_hi front_split own_act "
                 "own_dve own_pool ytk_turned u_stored v_stored k_stored "
                 "head_staged pz_done state_step bias_landed carried p_exp_in p_ln p_s p_cs p_arg p_w p_pv att_p q_staged z_copied zn_copied z_turned pv_rows o_act o_dve vnew_landed "
                 "k_flipped kt_dve kt_act scored s_e_in s_ln s_s s_r s_cs s_arg s_w s_pv att_s zn_done "
                 "ug_ready ug_dve ug_flipped g_swapped swap_ready u_ready g_done g_read h0_landed scanned "
                 "us_ready y_done y_read state_stored ytk_landed y_pre y_gelu y_ready "
                 "s_ready merged_ready m_ready x_pre mean_done centred squared var_done var_ready "
                 "sd_ready rstd_ready scaled gained modulated h2_hi normed h2_ready conv_landed halo conv_ev gelu_done f_ready ext_read "
                 "rows_stored y_out angle_ready c_split bias_spread").split():
        sem(name)
    ring_landed = [sem(f"ring_landed{i}") for i in range(RING)]
    uraw_landed, w1_landed, kt_landed, pt_landed, y_stored = ([sem(f"{n}{i}") for i in range(2)] for n in (
        "uraw_landed", "w1_landed", "kt_landed", "pt_landed", "y_stored"))
    kpage_landed = [sem(f"kpage_landed{i}") for i in range(KSLOTS)]
    vpage_landed = [sem(f"vpage_landed{i}") for i in range(PAGES)]
    acc_free = [sem(f"acc_free{i}") for i in range(2)]

    UNITS = D // BLOCK
    ADA1, PROJ = 0, 2 * UNITS * UNITS
    UNITS_LEFT = MODS * UNITS * UNITS - PROJ
    GLU = PROJ + 4 * KA + UNITS_LEFT
    MERGE, OUT = GLU + KA, GLU + KA + 4 * KD
    FFN = OUT + KD
    stages = [("glu", GLU, KA // 4, [KA] * 4), ("merge", MERGE, KD, [KD, KA, KD, KA]),
              ("out", OUT, KD // 4, [KD] * 4)]
    def nth_pair(n):
        return (n - (GLU - 4 * KA)) // 2

    items = [("unit", 0), ("unit", 1), ("chunk", 0), ("unit", 2), ("unit", 3), ("chunk", 1),
             ("unit", 4), ("unit", 5), ("chunk", 2), ("unit", 6), ("unit", 7), ("chunk", 3)]
    ITEMS = len(items)

    def front_of(x):
        return KD // 2 if items[x % ITEMS][0] == "chunk" else 0

    n0, j0 = FFN, 0
    for q, nj in enumerate(QUARTERS):
        stages.append((f"up{q}", n0, nj // 2, [KD] * 4))
        stages.append((f"down{q}", n0 + 2 * nj, KD // 4, [nj] * 4))
        n0, j0 = n0 + 2 * nj + KD, j0 + nj
    ks_of = {s[0]: s[3] for s in stages}
    first_of = {s[0]: s[1] for s in stages}
    passes_of = {s[0]: s[2] for s in stages}
    next_of = {a[0]: b[0] for a, b in zip(stages, stages[1:])}

    w_in_d = w_in[0].rearrange("(k p) c -> p k c", p=P)
    w_ada_d = w_ada[0].rearrange("(u k p) c -> u p k c", p=P, u=UNITS)
    w_att_d = w_att_br[0].rearrange("(k p) c -> p k c", p=P)
    w_ssm_d = w_ssm_br[0].rearrange("(k p) c -> p k c", p=P)
    w_glu_d = w_glu[0].rearrange("(k p) c -> p k c", p=P)
    w_out_d = w_out[0].rearrange("(k p) c -> p k c", p=P)
    w_up_d = w_up[0].rearrange("(k p) c -> p k c", p=P)
    w_down_d = w_down[0].rearrange("(k p) c -> p k c", p=P)

    def wide(t):
        return t[:].rearrange("p k c -> p (k c)").rearrange("p (k c) -> p k c", c=BLOCK)

    def last_in_slot(p):
        return p - KSLOTS if p >= KSLOTS else max(range(p, PAGES, KSLOTS)) - PAGES

    pieces_of_merge = [(0, 0, True), (0, KA, False), (1, 0, False), (2, 0, True), (2, KA, False), (3, 0, False)]

    def piece_buffers(x):
        h, k = ((0, 0), (0, KA), (1, 0))[x % 3]
        return wH[h][:, k:k + KA, :], wL[h][:, k:k + KA, :]

    def alone(eng):
        eng.sem_inc(S["carried"], 1)

    def passes(eng, stage, own, per_pass, body):
        n = passes_of[stage]
        with eng.Fori(0, n - 1) as i:
            if own:
                own.begin(i, per_pass)
            body(i, ks_of[stage])
            if own:
                own.end(n - 1)
        body(n - 1, ks_of[next_of[stage]] if stage in next_of else None)

    def samples(ap):
        return ap[:, NP:T].rearrange("p (b t) -> p b t", b=SB)

    def late(t):
        return t[:, NP + 2:EXT].rearrange("p (b t) -> p b t", b=SB)[:, :, 0:ST]

    def per_sample(ap):
        return ap.unsqueeze(2).to_broadcast([P, SB, ST])

    def setup_turns():
        yield [(csil[0:NC, k * P:(k + 1) * P], NC) for k in range(KD)], P, cT[:].rearrange("p k c -> p (k c)")
        yield [(pr[:, i, :], P) for i in range(2)], P, par[:]
        yield [(prw[:, i, :], 2 * JF) for i in range(3)] + [(prd[:], KA)], P, cw[:]
        yield [(a_raw[:, i, :], GROUPS) for i in range(2)], P, small64[:, 0:2, :]
        for dst, v in ((b1, 0), (b2, 1)):
            for half in range(2):
                src = b_raw[:].rearrange("g v (p n) -> g (v p) n", n=GC)
                yield ([(src[:, v * GS:v * GS + P, 8 * half + n], GROUPS) for n in range(8)], P,
                       dst[:].rearrange("p g n -> p n g")[:, 8 * half:8 * half + 8, :])
        for dst, v in ((c1, 0), (c2, 1)):
            for half in range(2):
                src = c_raw[:].rearrange("g n v p -> g n (v p)")
                yield ([(src[:, 8 * half + n, v * GS:v * GS + P], GROUPS) for n in range(8)], P,
                       dst[:].rearrange("p g n -> p n g")[:, 8 * half:8 * half + 8, :])
        for k in range(KD):
            yield ([(xrows[0:min(P, T - t * P), t, k * P:(k + 1) * P], min(P, T - t * P)) for t in range(3)], P, xT[:, k, :])

    def proj_turns():
        for first, dst in ((0, stage), (3 * KA, vtok), (2 * KA, kstage)):
            for half in range(2):
                for t in range(3):
                    rows = min(P, T - t * P)
                    yield ([(projT[:, first + 4 * half + c, t * P:t * P + rows], P) for c in range(4)], rows,
                           dst[0:rows, t, half * 512:half * 512 + 512])

    def state_turns():
        for v in range(2):
            yield ([(h0raw[:].rearrange("g b v p -> g b (v p)")[:, b, v * GS:v * GS + P], GROUPS) for b in range(SB)], P,
                   h0[:, v, :, :].rearrange("p g b -> p b g"))

    def final_state_turns():
        sources = [Z[:, 0, :, CP]] + [zf[:, :, b] for b in range(SB)]
        for first in (0, 4, 8):
            part_ = sources[first:first + 4]
            yield [(s, P) for s in part_], GROUPS, fin[:, first:first + len(part_), :]

    def conv_state_turns():
        for first in range(0, SB * 2, 4):
            yield ([(conv_raw[:, first + r, :], 2 * JF) for r in range(4)], P, conv_st[:, first:first + 4, :])

    def rows_out_turns():
        for first in range(0, NC * 2, 4):
            n = min(4, NC * 2 - first)
            yield [(rows_out[:, first + r, :], P) for r in range(n)], 2 * JF, rows_t[:, first:first + n, :]

    def y_turns():
        for quarter in range(4):
            for t in range(3):
                rows = min(P, T - t * P)
                yield ([(xT[:, 4 * quarter + c, t * P:t * P + rows], P) for c in range(4)], rows,
                       ytok[0:rows, t, quarter * 512:(quarter + 1) * 512])

    def width(sources):
        return sum(w for _, w in sources)

    rows_copied = []
    block = nc.Block()
    with block:

        @block.sync
        def _(sp):
            sp.dma_start(crows[0:1, :], c_prompt).then_inc(S["c_landed"], 16)
            sp.dma_start(crows[1:NC, :], c_sample).then_inc(S["c_landed"], 16)

            def load(n, s, K, src):
                sp.wait_ge(S["split_done"], n + 1)
                alone(sp)
                sp.dma_start(ring[s][:, 0:K, :], src).then_inc(ring_landed[s], 16)

            def load_unit(n, s, block_no, unit):
                sp.wait_ge(S["split_done"], n + 1)
                alone(sp)
                sp.dma_start(wide(ring[s]), w_ada_d[unit][:, :, ds(block_no * BLOCK, BLOCK)]).then_inc(ring_landed[s], 16)

            lp = S["params_landed"]
            for a, b in ((0, b_ada), (96, ln1_g), (112, ln1_b)):
                n = b.shape[1] // P
                sp.dma_start(pr[a:a + n, 0, :], b[0].rearrange("(r c) -> r c", c=P)).then_inc(lp, 16)
            for a, b in ((0, conv_b), (88, ln2_g), (104, ln2_b), (120, b_glu)):
                n = b.shape[1] // P
                sp.dma_start(pr[a:a + n, 1, :], b[0].rearrange("(r c) -> r c", c=P)).then_inc(lp, 16)
            sp.dma_start(prw[:], conv_w[0].rearrange("i (r c) -> r i c", c=P)).then_inc(lp, 16)
            sp.dma_start(prd[:], ssm_d[0].rearrange("(r c) -> r c", c=P)).then_inc(lp, 16)
            with sp.Fori(0, 2 * UNITS) as i:
                for u in range(UNITS):
                    load_unit(i * UNITS + u, u, i, u)

            def proj_pass(i, column):
                for x, (kind, m) in enumerate(items):
                    if kind == "unit":
                        load_unit(i * ITEMS + (PROJ + x), x % RING, i * 2 + (2 * UNITS + m // UNITS), m % UNITS)
                    else:
                        load(i * ITEMS + (PROJ + x), x % RING, KD, w_in_d[:, :, ds(column + m * P, P)])

            with sp.Fori(0, 2) as i:
                proj_pass(i, i * (4 * P) + 3 * AW)
            with sp.Fori(2, 8) as i:
                proj_pass(i, i * (4 * P) - 2 * 4 * P)

            sp.dma_start(pages[:], page_table.rearrange("b n -> (b n)").unsqueeze(0)).then_inc(S["pages_landed"], 16)
            sp.wait_ge(S["pages_landed"], 16)
            sp.wait_ge(S["chunk_done"], 2 + GLU)
            ck = cache_k[0].rearrange("n t h d -> n t (h d)")
            cv = cache_v[0].rearrange("n t h d -> n t (h d)")
            vs = v_sample[0].rearrange("b t h d -> b t (h d)")

            def page(i, p):
                return ds(sp.value_load(pages[0:1, ds(i * PAGES + p, 1)], min_val=0, max_val=n_phys - 1), 1)

            def attend(i, front=True, back=True):
                j = i - 1
                for p in range(PAGES):
                    if front:
                        here = page(i, p)
                        if not back and p == 2:
                            sp.wait_ge(S["v_stored"], 32)
                        sp.wait_ge(S["k_flipped"], i * PAGES + (last_in_slot(p) + 1 + KSLOTS))
                        sp.dma_start(kpage[p % KSLOTS][:], ck[here].rearrange("n t c -> (n t) c")).then_inc(kpage_landed[p % KSLOTS], 16)
                    if back and p == PAGES // 2 - 1:
                        sp.wait_ge(S["pv_rows"], j + 1)
                        sp.dma_start(vnew[:], vs[ds(j, 1)].rearrange("b t c -> (b t) c")).then_inc(S["vnew_landed"], 16)
                    if back and p >= PAGES // 2:
                        for n in (2 * p - PAGES, 2 * p - PAGES + 1):
                            sp.dma_start(vpage[n][:], cv[page(j, n)].rearrange("n t c -> (n t) c")).then_inc(vpage_landed[n], 16)

            attend(0, back=False)
            sp.wait_ge(S["k_stored"], 32)
            with sp.Fori(1, SB) as i:
                attend(i)
            attend(SB, front=False)

            sp.wait_ge(S["s_pv"], SB + 1)
            sp.wait_ge(S["att_p"], HEADS + 1)
            sp.wait_ge(S["u_stored"], 32)
            sp.wait_ge(S["w1_stored"], 16 * BATCHES)
            sp.dma_start(h0raw[:, :, 0, :], state_ssm_re[0].rearrange("b g p -> g b p")).then_inc(S["h0_landed"], 16)
            sp.dma_start(h0raw[:, :, 2, :], state_ssm_re[0].rearrange("b g p -> g b p")).then_inc(S["h0_landed"], 16)
            sp.dma_start(h0raw[:, :, 1, :], state_ssm_im[0].rearrange("b g p -> g b p")).then_inc(S["h0_landed"], 16)
            u_chunks = u_tok.rearrange("(c s) d -> c s d", s=CHUNK)

            def load_rows(b, e):
                sp.wait_ge(S["ug_ready"], b + 1)
                sp.wait_ge(S["ug_dve"], b + 1)
                sp.dma_start(Uraw[e][:], u_chunks[:, :, ds(b * P, P)]).then_inc(uraw_landed[e], 16)

            def load_weights(b, e):
                sp.wait_ge(S["g_done"], b + 1)
                sp.dma_start(W1[e][:], w1_d[ds(b, 1)].rearrange("o p (g m) -> (o p) g m", m=P)).then_inc(w1_landed[e], 16)

            for e in range(2):
                load_rows(e, e)
            with sp.Fori(0, BATCHES // 2 - 1) as i:
                for e in range(2):
                    load_weights(i * 2 + e, e)
                    load_rows(i * 2 + (e + 2), e)
            for e in range(2):
                load_weights(BATCHES - 2 + e, e)

            sp.wait_ge(S["g_done"], BATCHES + 2)
            sp.wait_ge(S["taps_stored"], 16 * BATCHES)
            sp.wait_ge(S["p_stored"], 16 * BATCHES)

            def load_out(b, e):
                sp.wait_ge(S["y_done"], b + 1)
                for s in range(CHUNK):
                    a = (CHUNK - 1 - s) * GC
                    sp.dma_start(Kt[e][:, s, :], taps_d[a:a + P, ds(b * P, P)]).then_inc(kt_landed[e], 16)
                sp.dma_start(Pt[e][:], p_d[ds(b, 1)].rearrange("o p (g m) -> (o p) g m", m=P)).then_inc(pt_landed[e], 16)

            load_out(0, 0)
            sp.wait_ge(S["scanned"], 1)
            load_out(1, 1)
            with sp.Fori(1, BATCHES // 2) as i:
                for e in range(2):
                    load_out(i * 2 + e, e)
            for e in range(2):
                sp.wait_ge(y_stored[e], 8 * BATCHES)
            yt = y_tok[0:NP].rearrange("(t p) d -> p t d", p=P)
            sp.dma_start(ytk[:, 0:2, :], yt).then_inc(S["ytk_landed"], 16)
            sp.dma_start(ytk[0:SB * ST, 2, :], y_tok[NP:T]).then_inc(S["ytk_landed"], 16)

            sp.wait_ge(S["y_pre"], KA)
            with sp.Fori(0, KA // 4) as i:
                for cc in range(4):
                    load(i * 4 + (GLU + cc), cc, KA, w_glu_d[:, :, ds((i * 4 + cc) * P, P)])
            with sp.Fori(0, KD) as i:
                load(i * 4 + MERGE, 0, KD, w_in_d[:, :, ds(i * P + 3 * AW + SW, P)])
                load(i * 4 + (MERGE + 1), 1, KA, w_att_d[:, :, ds(i * P, P)])
                load(i * 4 + (MERGE + 2), 2, KD, w_in_d[:, :, ds(i * P + 3 * AW + SW + D, P)])
                load(i * 4 + (MERGE + 3), 3, KA, w_ssm_d[:, :, ds(i * P, P)])
            with sp.Fori(0, KD // 4) as i:
                for cc in range(4):
                    load(i * 4 + (OUT + cc), cc, KD, w_out_d[:, :, ds((i * 4 + cc) * P, P)])
            sp.wait_ge(S["m_ready"], KD)
            sp.dma_start(conv_raw[:], state_conv[0].rearrange("b i (r c) -> r (b i) c", c=P)).then_inc(S["conv_landed"], 16)
            j0 = 0
            for q, nj in enumerate(QUARTERS):
                n0 = first_of[f"up{q}"]
                with sp.Fori(0, nj // 2) as i:
                    for cc in range(4):
                        column = (j0 + cc // 2) * P + (cc % 2) * FF
                        load(i * 4 + (n0 + cc), cc, KD, w_up_d[:, :, ds(i * (2 * P) + column, P)])
                n0 = first_of[f"down{q}"]
                with sp.Fori(0, KD // 4) as i:
                    for cc in range(4):
                        load(i * 4 + (n0 + cc), cc, nj, w_down_d[:, j0:j0 + nj, ds((i * 4 + cc) * P, P)])
                j0 += nj

            sp.wait_ge(S["flips_read"], 60)
            for o, r in ((conv_prompt[0], 0), (conv_sample[0], 2)):
                n = o.shape[0] * 2
                sp.dma_start(o.rearrange("b i (r c) -> r (b i) c", c=P), rows_t[:, r:r + n, :]).then_inc(S["rows_stored"], 16)
            for n in range(4):
                sp.wait_ge(S["flips_read"], 63 + 3 * n)
                c = slice(n * 512, n * 512 + 512)
                sp.dma_start(y_prompt[0].rearrange("(t p) d -> p t d", p=P)[:, :, c], ytok[:, 0:2, c]).then_inc(S["y_out"], 16)
                sp.dma_start(y_sample.rearrange("b t d -> (b t) d")[:, c], ytok[0:SB * ST, 2, c]).then_inc(S["y_out"], 16)
            sp.wait_ge(S["rows_stored"], 32)
            sp.wait_ge(S["y_out"], 128)

        @block.gpsimd
        def _(pool):
            g = nc.gpsimd
            pool.sem_inc(S["ug_ready"], 2)
            own = Own(pool, S["own_pool"])
            own.mark(g.memset(zeros[:], 0.0))
            own.mark(g.memset(ident[:], 0.0))
            own.mark(g.memset(later[:], 1.0))
            own.mark(g.memset(mean_of[:], 1.0 / D))
            own.mark(g.memset(masks[:], 0.0))
            own.mark(g.memset(mask_new[:], 0.0))
            own.mark(g.memset(sign[:], 1.0))
            own.step(g.memset(ones[:], 1.0))
            g.affine_select(out=ident[:], in_=ident[:], compare_op=ALU.not_equal, fill=1.0, base=0,
                            pattern=[[-1, P]], channel_multiplier=1).then_inc(S["ident_ready"], 1)
            own.mark(g.affine_select(out=later[:], in_=later[:], compare_op=ALU.is_ge, fill=0.0, base=0,
                                     pattern=[[-1, P]], channel_multiplier=1))
            for first in (0, 256):
                own.mark(g.affine_select(out=masks[:, first:first + P], in_=masks[:, first:first + P], compare_op=ALU.is_gt,
                                         fill=-1.0, base=0, pattern=[[1, P]], channel_multiplier=-1))
            mn = mask_new[:].rearrange("k (h q) -> k h q", h=HEADS)
            own.mark(g.affine_select(out=mn, in_=mn, compare_op=ALU.is_gt, fill=-1.0, base=0,
                                     pattern=[[0, HEADS], [1, ST]], channel_multiplier=-1))
            own.step(g.affine_select(out=sign[:, 0:1], in_=sign[:, 0:1], compare_op=ALU.is_gt, fill=-1.0, base=GS,
                                     pattern=[[0, 1]], channel_multiplier=-1))
            g.tensor_scalar(sign[:, 1:2], sign[:, 0:1], -1.0, None, ALU.mult).then_inc(S["consts_ready"], 1)
            pool.dma_start(taps_d[P:P + 112], zeros[:]).then_inc(S["zeros_stored"], 16)

            pool.wait_ge(S["prep_dve"], 1)

            def out_of_state(i, first=False):
                gs = ds(i * GB, GB)

                def power(t):
                    return t[:, gs, 1:CHUNK + 1].unsqueeze(3).to_broadcast([P, GB, CHUNK, GC])

                def rows(t):
                    return t[:, gs, :].unsqueeze(2).to_broadcast([P, GB, CHUNK, GC])

                def blocks(t):
                    return t[:].rearrange("p g (s n) -> p g s n", n=GC)

                own.mark(g.tensor_tensor(blocks(PT), power(pows[0]), rows(c1), ALU.mult))
                own.step(g.tensor_tensor(blocks(PX), power(pows[1]), rows(c2), ALU.mult))
                if not first:
                    pool.wait_ge(S["p_stored"], i * 16)
                own.step(g.tensor_tensor(P_[:], PT[:], PX[:], ALU.add))
                pool.dma_start(p_d[ds(i, 1)].rearrange("o p c -> (o p) c"), P_[:].rearrange("p g m -> p (g m)")).then_inc(S["p_stored"], 16)

            out_of_state(0, first=True)
            with pool.Fori(1, BATCHES) as i:
                own.begin(i, 3, first=1)
                out_of_state(i)
                own.end(BATCHES - 1)

            pool.wait_ge(S["chunk_done"], 2 + GLU)
            own.mark(g.memset(sR[:], 0.0))
            own.mark(g.memset(sz[:], 0.0))
            own.mark(g.memset(se[:], 0.0))
            own.mark(g.memset(q_block[:], 0.0))
            own.step(g.memset(sS[:], 0.0))
            pool.wait_ge(S["bias_landed"], 16)
            for q in range(ST):
                last = g.tensor_copy(bias_q[:].rearrange("p (h q) -> p h q", q=ST)[:, :, q], bias_h[:])
            last.then_inc(S["bias_spread"], 1)

            f = 4 + 8 + KD

            def store_rows(prompt, sample, src, name):
                pool.dma_start(prompt.rearrange("(t p) c -> p t c", p=P), src[:, 0:2, :]).then_inc(S[name], 16)
                pool.dma_start(sample, src[0:SB * ST, 2, :]).then_inc(S[name], 16)

            pool.wait_ge(S["flips_read"], f + 6)
            store_rows(u_tok[0:NP], u_tok[NP:T], stage, "u_stored")
            pool.wait_ge(S["flips_read"], f + 12)
            store_rows(v_prompt[0, 0].rearrange("t h d -> t (h d)"), v_sample[0].rearrange("b t h d -> (b t) (h d)"), vtok, "v_stored")
            pool.wait_ge(S["flips_read"], f + 18)
            store_rows(k_prompt[0, 0].rearrange("t h d -> t (h d)"), k_sample[0].rearrange("b t h d -> (b t) (h d)"), kstage, "k_stored")


            def attend(i, front=True, back=True):
                j = i - 1
                if front:
                    pool.wait_ge(S["scored"], i * PAGES + 2)
                    g.tensor_copy(q_block[:].rearrange("p (h c) -> p h c", h=HEADS)[:, :, 0:ST],
                                  projT[:, KA:2 * KA, ds(i * ST + NP, ST)]).then_inc(S["q_staged"], 1)
                if back:
                    pool.wait_ge(S["p_pv"], j + 1)
                    own.step(g.tensor_copy(kh[:].unsqueeze(1), projT[:, ds(j + 2 * KA, 1), 0:NP]))
                    g.tensor_copy(vh[:], vtok[:, 0:2, ds(j * HD, HD)]).then_inc(S["head_staged"], 1)
                if back:
                    pool.wait_ge(S["s_s"], j + 1)
                    alone(pool)
                    own.step(g.tensor_copy(sR[:, PAGES - 2, :], sS[:, PAGES - 1, :]))
                    for p in range(PAGES - 3, -1, -1):
                        ins = g.tensor_tensor(sR[:, p, :], sR[:, p + 1, :], sS[:, p + 1, :], ALU.add)
                        if p:
                            own.step(ins)
                        else:
                            ins.then_inc(S["s_r"], 1)

            attend(0, back=False)
            with pool.Fori(1, SB) as i:
                own.begin(i, 7, first=1)
                attend(i)
                own.end(SB - 1)
            attend(SB, front=False)

            pool.wait_ge(S["s_pv"], SB + 1)
            own.step(g.memset(swap[:], 0.0))
            own.step(g.affine_select(out=swap[:], in_=swap[:], compare_op=ALU.not_equal, fill=-1.0, base=-GS,
                                     pattern=[[-1, P]], channel_multiplier=1))
            g.affine_select(out=swap[:], in_=swap[:], compare_op=ALU.not_equal, fill=1.0, base=GS,
                            pattern=[[-1, P]], channel_multiplier=1).then_inc(S["swap_ready"], 1)
            with pool.Fori(0, BATCHES // 2) as i:
                for e in range(2):
                    pool.wait_ge(uraw_landed[e], i * 16 + 16)
                    pool.wait_ge(S["ug_flipped"], i * 2 + (e + 1))
                    alone(pool)
                    for gg in range(POOL_GROUPS):
                        last = g.tensor_copy(Ug[e][:, gg, :].rearrange("c (s n) -> c s n", n=GC), Uraw[e][:, :, gg * GC:(gg + 1) * GC])
                    last.then_inc(S["ug_ready"], 1)
            pool.wait_ge(S["scanned"], 1)
            y_chunks = y_tok.rearrange("(c s) d -> c s d", s=CHUNK)

            def stage_in(b, e):
                pool.wait_ge(S["y_done"], b + 1)
                alone(pool)
                g.tensor_copy(Us[e][:], U[:, ds(b * GB, GB), :])
                g.tensor_copy(Hs[e][:, :, 0:CP], Z[:, 0, ds(b * GB, GB), 0:CP])
                g.tensor_copy(Hs[e][:, :, CP:CT], Z[:, 0, ds(b * GB, GB), CP + 1:CT + 1]).then_inc(S["us_ready"], 1)

            def store_out(b, e):
                pool.wait_ge(S["y_read"], b + 3)
                alone(pool)
                pool.dma_start(y_chunks[:, :, ds(b * P, P)], Yt[e][:].rearrange("c s g n -> c s (g n)")).then_inc(y_stored[e], 16)

            def out_pair(i, last=False):
                stage_in(i * 2 + 1, 1)
                store_out(i * 2, 0)
                if not last:
                    stage_in(i * 2 + 2, 0)
                store_out(i * 2 + 1, 1)

            stage_in(0, 0)
            with pool.Fori(0, BATCHES // 2 - 1) as i:
                out_pair(i)
            out_pair(BATCHES // 2 - 1, last=True)
            pool.wait_ge(S["flips_read"], f + 18 + 2 + 3)
            for o, r, b in ((ssm_re_prompt, 0, 0), (ssm_im_prompt, 1, 0), (ssm_re_sample, 0, 1), (ssm_im_sample, 1, 1)):
                n = SB if b else 1
                pool.dma_start(o[0].rearrange("b g p -> g b p"), fin[:, b:b + n, r * GS:(r + 1) * GS]).then_inc(S["state_stored"], 16)

            def layer_norm(nth):
                pool.wait_ge(S["rstd_ready"], nth + 1)
                for k in range(KD):
                    g.tensor_tensor(xT[:, k, :], xT[:, k, :], rstd[:], ALU.mult).then_inc(S["scaled"], 1)

            layer_norm(0)

            pool.wait_ge(S["flips_read"], f + 18 + 2 + 3 + 4)
            pool.wait_ge(S["h2_ready"], KD)
            for e in ext:
                own.mark(g.memset(e[:, 0:2], 0.0))
            own.settle()
            j0 = 0
            done = 0
            for q, nj in enumerate(QUARTERS):
                with pool.Fori(0, nj // 2) as i:
                    own.begin(i, 8)
                    for cc in range(4):
                        block_no = i * 2 + (j0 + cc // 2 + (cc % 2) * JF)
                        tail = ext[cc][:, NP + 2:EXT].rearrange("p (b t) -> p b t", b=SB)
                        n = i * 4 + (done + cc)
                        pool.wait_ge(S["ext_read"], n + 1)
                        own.settle()
                        g.tensor_copy(tail[:, :, 0:2], conv_st[:, :, ds(block_no, 1)].rearrange("p (b i) o -> p b (i o)", b=SB)).then_inc(S["halo"], 1)
                        pool.wait_ge(S["conv_ev"], n + 1)
                        own.mark(g.tensor_copy(rows_out[:, 0:2, ds(block_no, 1)], ext[cc][:, NP:NP + 2].unsqueeze(2)))
                        pool.wait_ge(acc_free[cc % 2], i * 2 + (nth_pair(first_of[f"up{q}"]) + cc // 2 + 2))
                        own.mark(g.tensor_copy(rows_out[:, 2:2 + 2 * SB, ds(block_no, 1)].rearrange("p (b i) o -> p b (i o)", b=SB), tail[:, :, ST:ST + 2]))
                    own.end(nj // 2)
                j0 += nj
                done += 2 * nj
            own.settle()
            rows_copied.append(own.count)
            layer_norm(1)
            for name, n in (("u_stored", 32), ("v_stored", 32), ("k_stored", 32), ("state_stored", 64),
                            ("w1_stored", 16 * BATCHES), ("taps_stored", 16 * BATCHES),
                            ("p_stored", 16 * BATCHES)):
                pool.wait_ge(S[name], n)
            for e in range(2):
                pool.wait_ge(y_stored[e], 8 * BATCHES)

        @block.tensor
        def _(pe):
            t = nc.tensor
            turned = [0]

            def turn(turns, ready=None):
                for n, (sources, rows, _) in enumerate(turns):
                    if ready and n in ready:
                        ready[n]()
                    if turned[0] >= 4:
                        pe.wait_ge(S["flips_read"], turned[0] - 3)
                    b, c = bank[4 + turned[0] % 4], 0
                    for src, w in sources:
                        k = src.shape[0]
                        last = t.transpose(b[0:rows, c:c + w], src, ident[0:k, 0:k])
                        c += w
                    last.then_inc(S["flipped"], 1)
                    turned[0] += 1

            pe.sem_inc(S["ada_turned"], 1)
            pe.sem_inc(S["chunk_done"], 2)
            pe.sem_inc(S["k_flipped"], KSLOTS)
            for name in ("scored", "g_done", "y_done", "ug_flipped"):
                pe.sem_inc(S[name], 2)
            for name in ( "p_pv", "zn_done", "s_pv", "w_flipped", "z_turned", "pv_rows"):
                pe.sem_inc(S[name], 1)

            pe.wait_ge(S["ident_ready"], 1)
            setup = list(setup_turns())
            turn(setup[:1], {0: lambda: pe.wait_ge(S["silu_ready"], 1)})

            def ada_unit(n, buf, block_no, unit):
                pe.wait_ge(S["split_done"], n + (1 + RING))
                if unit == 0:
                    pe.wait_ge(S["ada_copied"], block_no + 1)
                    alone(pe)
                rows = bank[2][0:2 * NC, :]
                for k in range(BLOCK // P):
                    c = cHL[:, unit * (BLOCK // P) + k, :]
                    t.matmul(rows, c, wide(wH[buf])[:, k, :], start=(unit == 0 and k == 0), stop=False)
                    last = t.matmul(rows, c, wide(wL[buf])[:, k, :], start=False, stop=(unit == UNITS - 1 and k == BLOCK // P - 1))
                last.then_inc(S["chunk_done"], 1)

            def ada_turn(block_no):
                pe.wait_ge(S["ada_copied"], block_no + 2)
                pe.wait_ge(S["ada_mod"], block_no + 1)
                for c in range(BLOCK // P):
                    last = t.matmul(bank[3][:, c * NC:(c + 1) * NC], ada_rows[:, c * P:(c + 1) * P], add_up[:], start=True, stop=True)
                last.then_inc(S["ada_turned"], 1)

            pe.wait_ge(S["c_split"], 1)
            for u in range(UNITS):
                ada_unit(u, u % 2, 0, u)
            ada_turn(0)
            turn(setup[1:12], {0: lambda: pe.wait_ge(S["params_landed"], 9 * 16), 2: lambda: pe.wait_ge(S["ssm_landed"], 11 * 16)})
            with pe.Fori(1, UNITS) as i:
                for u in range(UNITS):
                    ada_unit(i * UNITS + u, u % 2, i, u)
                ada_turn(i)
            turn(setup[12:], {0: lambda: pe.wait_ge(S["x_landed"], 32)})
            with pe.Fori(UNITS, 2 * UNITS) as i:
                for u in range(UNITS):
                    ada_unit(i * UNITS + u, u % 2, i, u)
                    if u % 2:
                        b = i * 2 + (u // 2 - 2 * UNITS)
                        pe.wait_ge(S["v_ready"], b + 1)
                        pe.wait_ge(S["w_read"], b + 1)
                        for gg in range(GB):
                            t.transpose(bank[4 + gg // 4][:, (gg % 4) * P:(gg % 4 + 1) * P], V[:, gg, :], ident[:])
                        for gg in range(GB):
                            last = t.matmul(bank[6][:, gg * GC:(gg + 1) * GC], V[:, gg, :],
                                            c1[:, ds(b * GB + gg, 1), :].rearrange("p o n -> p (o n)"), start=True, stop=True)
                        last.then_inc(S["w_flipped"], 1)
                ada_turn(i)

            def product(n, cc, K, half_n, high, low, buf=None, ready=None, nth_front=None):
                if nth_front is None:
                    pe.wait_ge(S["split_done"], n + (1 + RING))
                else:
                    pe.wait_ge(S["front_split"], nth_front + 1)
                pe.wait_ge(acc_free[cc % 2], half_n + 1)
                acc = bank[cc % 2][:, 0:T]
                buf = cc % 2 if buf is None else buf
                a, b = wH[buf], wL[buf]
                for k in range(K):
                    if nth_front is not None and k == K // 2:
                        pe.wait_ge(S["split_done"], n + (1 + RING))
                    if ready:
                        pe.wait_ge(ready[0], ready[1] + k + 1)
                    t.matmul(acc, a[:, k, :], high[:, k, :], start=(k == 0), stop=False)
                    t.matmul(acc, a[:, k, :], low[:, k, :], start=False, stop=False)
                    last = t.matmul(acc, b[:, k, :], high[:, k, :], start=False, stop=(k == K - 1))
                last.then_inc(S["chunk_done"], 1)

            def products(i, n0, cc, K, high, low, ready=None):
                product(i * 4 + (n0 + cc), cc, K, i * 2 + (nth_pair(n0) + cc // 2), high, low, None, ready)

            with pe.Fori(0, KA) as i:
                for x, (kind, m) in enumerate(items):
                    n = i * ITEMS + (PROJ + x)
                    if kind == "unit":
                        ada_unit(n, x % 3, i * 2 + (2 * UNITS + m // UNITS), m % UNITS)
                    else:
                        product(n, m, KD, i * 2 + m // 2, hH, hL, x % 3, (S["h_ready"], 0) if m == 0 else None, i * 4 + m)
                        if m % 2:
                            ada_turn(i * 2 + (2 * UNITS + m // 2))

            for a_ in acc_free:
                pe.wait_ge(a_, nth_pair(GLU) + 1)
            turn(proj_turns())

            pe.wait_ge(S["consts_ready"], 1)
            pe.wait_ge(S["flips_read"], turned[0])

            def attend(i, front=True, back=True):
                j = i - 1

                def flip(p):
                    pe.wait_ge(kpage_landed[p % KSLOTS], i * (16 * len(range(p % KSLOTS, PAGES, KSLOTS))) + 16 * (p // KSLOTS + 1))
                    pe.wait_ge(S["kt_dve"], i * PAGES + (p + 1))
                    pe.wait_ge(S["kt_act"], i * PAGES + (p + 1))
                    for h in range(HEADS):
                        last = t.transpose(bank[h // 4][:, (h % 4) * P:(h % 4 + 1) * P], kpage[p % KSLOTS][:, h * HD:(h + 1) * HD], ident[:])
                    last.then_inc(S["k_flipped"], 1)

                def score(p):
                    pe.wait_ge(S["kt_dve"], i * PAGES + (p + 2))
                    pe.wait_ge(S["kt_act"], i * PAGES + (p + 2))
                    if p % 4 == 0:
                        pe.wait_ge(S["z_copied"], i * 2 + (p // 4 + 1))
                    for h in range(HEADS):
                        last = t.matmul(bank[7][0:HQ, (p % 4) * PAGE:(p % 4 + 1) * PAGE], q_block[:, h * HQ:(h + 1) * HQ],
                                        kTp[p % 2][:, h, :], start=(h == 0), stop=(h == HEADS - 1))
                    last.then_inc(S["scored"], 1)

                def new_scores():
                    pe.wait_ge(S["q_staged"], i + 1)
                    alone(pe)
                    for h in range(HEADS):
                        last = t.matmul(bank[6][0:HQ, 0:ST], q_block[:, h * HQ:(h + 1) * HQ],
                                        projT[:, 2 * KA + h, ds(i * ST + NP, ST)], start=(h == 0), stop=(h == HEADS - 1))
                    last.then_inc(S["zn_done"], 1)

                def turn_scores(first):
                    pe.wait_ge(S["z_copied"], i * 2 + (first // 4 + 2))
                    if first == 0:
                        pe.wait_ge(S["s_e_in"], i + 1)
                    alone(pe)
                    for p in range(first, first + 4):
                        t.transpose(bank[2][:, p * HQ:(p + 1) * HQ], z_rows[:, p, :], ident[0:HQ, 0:HQ])

                def head_scores():
                    pe.wait_ge(S["head_staged"], j + 1)
                    pe.wait_ge(S["att_p"], j + 1)
                    pe.wait_ge(S["att_s"], j + 1)
                    q = projT[:, ds(j + KA, 1), :].rearrange("p o t -> p (o t)")
                    t.matmul(bank[4][:, 0:NP], kh[:, 0:P], q[:, 0:NP], start=True, stop=True)
                    t.matmul(bank[4][:, NP:NP + P], kh[:, P:NP], q[:, P:NP], start=True, stop=True).then_inc(S["pz_done"], 1)

                def sums():
                    pe.wait_ge(S["s_s"], j + 1)
                    pe.wait_ge(S["p_s"], j + 1)
                    alone(pe)
                    t.matmul(bank[4][0:ST, 384:384 + HQ], later[0:ST, 0:ST], sS[0:ST, PAGES, :], start=True, stop=True)
                    t.matmul(bank[4][:, 0:384], later[:], pS[:], start=True, stop=False)
                    t.matmul(bank[4][:, P:NP], ones[:], pS[:, NP:NP + P], start=False, stop=True).then_inc(S["p_cs"], 1)
                    t.matmul(bank[3][:], later[:], sS[:, 0:PAGES, :].rearrange("p a c -> p (a c)"), start=True, stop=False)
                    t.matmul(bank[3][:], ones[0:ST, :], sS[0:ST, PAGES:PAGES + 1, :].to_broadcast([ST, PAGES, HQ]), start=False, stop=False)
                    pe.wait_ge(S["s_r"], j + 1)
                    t.matmul(bank[3][:], ones[:], sR[:, 0:PAGES, :].rearrange("p a c -> p (a c)"), start=False, stop=True).then_inc(S["s_cs"], 1)

                def outputs():
                    pe.wait_ge(S["p_w"], j + 1)
                    pe.wait_ge(S["s_w"], j + 1)
                    t.matmul(bank[4][:, 0:NP], vh[:, 0, :], pe_[:, 0:NP], start=True, stop=False)
                    t.matmul(bank[4][:, P:NP], vh[:, 1, :], pe_[:, NP:NP + P], start=False, stop=True).then_inc(S["p_pv"], 1)
                    if front:
                        pe.wait_ge(S["zn_copied"], i + 1)
                    pe.wait_ge(S["vnew_landed"], j * 16 + 16)
                    for p in range(PAGES):
                        pe.wait_ge(vpage_landed[p], j * 16 + 16)
                    alone(pe)
                    for h in range(HEADS):
                        o = bank[5 + h // 4][0:ST, (h % 4) * HD:(h % 4 + 1) * HD]
                        for p in range(PAGES):
                            t.matmul(o, se[:, p, h * ST:(h + 1) * ST], vpage[p][:, h * HD:(h + 1) * HD], start=(p == 0), stop=False)
                        last = t.matmul(o, se[0:ST, PAGES, h * ST:(h + 1) * ST], vnew[:, h * HD:(h + 1) * HD], start=False, stop=True)
                    last.then_inc(S["pv_rows"], 1)

                def turn_outputs():
                    pe.wait_ge(S["o_act"], j + 1)
                    pe.wait_ge(S["o_dve"], j + 1)
                    pe.wait_ge(S["att_p"], j + 2)
                    alone(pe)
                    for h in range(HEADS):
                        last = t.transpose(bank[4][:, 512 - HQ + h * ST:512 - HQ + (h + 1) * ST], o_rows[:, h * HD:(h + 1) * HD], ident[0:ST, 0:ST])
                    last.then_inc(S["s_pv"], 1)

                for p in range(PAGES):
                    if front:
                        flip(p)
                    if back and p == 0:
                        head_scores()
                    if front and p == 0:
                        new_scores()
                    if front and p:
                        score(p - 1)
                    if back and p == 4:
                        sums()
                    if front and p == 5:
                        turn_scores(0)
                    if back and p == 7:
                        outputs()
                if front:
                    score(PAGES - 1)
                    turn_scores(4)
                    pe.wait_ge(S["zn_copied"], i + 1)
                    alone(pe)
                    t.transpose(bank[3][0:ST, 0:HQ], zn_rows[:], ident[0:HQ, 0:HQ]).then_inc(S["z_turned"], 1)
                if back:
                    turn_outputs()

            attend(0, back=False)
            with pe.Fori(1, SB) as i:
                attend(i)
            attend(SB, front=False)

            pe.wait_ge(S["att_s"], SB + 1)

            def flip_in(b, e):
                pe.wait_ge(S["ug_ready"], b + 3)
                pe.wait_ge(S["ug_dve"], b + 3)
                alone(pe)
                for gg in range(GB):
                    last = t.transpose(bank[4][:, gg * CT:(gg + 1) * CT], Ug[e][:, gg, :], ident[0:CT, 0:CT])
                last.then_inc(S["ug_flipped"], 1)

            def into_state(i, b, e, last=False):
                pe.wait_ge(S["u_ready"], b + 1)
                if not last:
                    flip_in(b + 1, 1 - e)
                pe.wait_ge(w1_landed[e], i * 16 + 16)
                pe.wait_ge(S["g_read"], b + 1)
                for gg in range(GB):
                    last = t.matmul(bank[5 + e][:, gg * CT:(gg + 1) * CT], W1[e][:, gg, :],
                                    U[:, ds(b * GB + gg, 1), :].rearrange("p o c -> p (o c)"), start=True, stop=True)
                last.then_inc(S["g_done"], 1)

            flip_in(0, 0)
            with pe.Fori(0, BATCHES // 2 - 1) as i:
                for e in range(2):
                    into_state(i, i * 2 + e, e)
            into_state(BATCHES // 2 - 1, BATCHES - 2, 0)
            into_state(BATCHES // 2 - 1, BATCHES - 1, 1, last=True)
            pe.wait_ge(S["swap_ready"], 1)
            pe.wait_ge(S["g_read"], BATCHES + 2)
            for n in range(GROUPS * CT // 512):
                if n >= 2:
                    pe.wait_ge(S["g_swapped"], n - 1)
                t.matmul(bank[n % 2][:], swap[:], G[:, 0].rearrange("p g c -> p (g c)")[:, n * 512:(n + 1) * 512],
                         start=True, stop=True).then_inc(S["g_done"], 1)
            pe.wait_ge(S["h0_landed"], 48)
            turn(state_turns())
            pe.wait_ge(S["scanned"], 1)
            turn(final_state_turns())
            pe.wait_ge(S["flips_read"], turned[0])
            with pe.Fori(0, BATCHES // 2) as i:
                for e in range(2):
                    b = i * 2 + e
                    pe.wait_ge(S["us_ready"], b + 1)
                    pe.wait_ge(kt_landed[e], i * (16 * CHUNK) + 16 * CHUNK)
                    pe.wait_ge(pt_landed[e], i * 16 + 16)
                    pe.wait_ge(S["y_read"], b + 1)
                    for gg in range(GB):
                        o = bank[4 + 2 * e + gg // 4][0:CT, (gg % 4) * P:(gg % 4 + 1) * P]
                        t.matmul(o.rearrange("c (s n) -> c s n", n=GC), Us[e][:, gg, :], Kt[e][:, :, gg * GC:(gg + 1) * GC], start=True, stop=False)
                        last = t.matmul(o, Hs[e][:, gg, :], Pt[e][:, gg, :], start=False, stop=True)
                    last.then_inc(S["y_done"], 1)
            pe.wait_ge(S["y_read"], BATCHES + 2)
            pe.wait_ge(S["ytk_landed"], 32)
            for c in range(KA):
                if c >= 4:
                    pe.wait_ge(S["y_pre"], c - 3)
                for tt in range(3):
                    rows = min(P, T - tt * P)
                    last = t.transpose(bank[4 + c % 4][:, tt * P:tt * P + rows], ytk[0:rows, tt, c * P:(c + 1) * P], ident[0:rows, 0:rows])
                last.then_inc(S["ytk_turned"], 1)

            pe.wait_ge(S["y_ready"], KA)
            passes(pe, "glu", None, 0, lambda i, _: [products(i, GLU, cc, KA, ygH, ygL) for cc in range(4)])
            pe.wait_ge(S["s_ready"], KA)
            operands = [(hH, hL), (attH, attL), (hH, hL), (sH, sL)]
            pe.sem_inc(S["half_done"], 1)
            with pe.Fori(0, KD) as i:
                for x, (cc, k0, more) in enumerate(pieces_of_merge):
                    (a, b), (high, low) = piece_buffers(x), operands[cc]
                    if more:
                        pe.wait_ge(S["half_split"], i * 2 + (cc // 2 + 1))
                    else:
                        pe.wait_ge(S["split_done"], i * 4 + (MERGE + cc + 1 + RING))
                    if k0 == 0:
                        pe.wait_ge(acc_free[cc % 2], i * 2 + (nth_pair(MERGE) + cc // 2 + 1))
                    acc = bank[cc % 2][:, 0:T]
                    for k in range(KA):
                        t.matmul(acc, a[:, k, :], high[:, k0 + k, :], start=(k0 == 0 and k == 0), stop=False)
                        t.matmul(acc, a[:, k, :], low[:, k0 + k, :], start=False, stop=False)
                        last = t.matmul(acc, b[:, k, :], high[:, k0 + k, :], start=False, stop=(not more and k == KA - 1))
                    last.then_inc(S["half_done" if more else "chunk_done"], 1)
            passes(pe, "out", None, 0, lambda i, _: [products(i, OUT, cc, KD, mH, mL, (S["m_ready"], 0) if cc == 0 else None) for cc in range(4)])

            def layer_norm(nth):
                for k in range(KD):
                    pe.wait_ge(S["x_pre"], KD * nth + k + 2)
                    last = t.matmul(bank[2][:, 0:T], mean_of[:], xT[:, k, :], start=(k == 0), stop=(k == KD - 1))
                last.then_inc(S["mean_done"], 1)
                for k in range(KD):
                    pe.wait_ge(S["squared"], KD * nth + k + 1)
                    last = t.matmul(bank[3][:, 0:T], mean_of[:], centred_sq[:, k, :], start=(k == 0), stop=(k == KD - 1))
                last.then_inc(S["var_done"], 1)

            pe.wait_ge(S["conv_landed"], 16)
            turn(conv_state_turns())
            layer_norm(0)
            down = 0
            for q, nj in enumerate(QUARTERS):
                n0 = first_of[f"up{q}"]
                passes(pe, f"up{q}", None, 0, lambda i, _, n0=n0: [products(i, n0, cc, KD, hH, hL, (S["h2_ready"], 0) if cc == 0 and n0 == FFN else None) for cc in range(4)])
                n0 = first_of[f"down{q}"]
                passes(pe, f"down{q}", None, 0, lambda i, _, n0=n0, nj=nj, d=down: [products(i, n0, cc, nj, fH, fL, (S["f_ready"], d + 1) if cc == 0 else None)
                                                                              for cc in range(4)])
                down += nj
            pe.wait_ge(S["own_pool"], rows_copied[0])
            turn(rows_out_turns())
            layer_norm(1)
            turn(y_turns(), {3 * n: lambda n=n: pe.wait_ge(S["normed"], 4 * (n + 1)) for n in range(4)})

        @block.scalar
        def _(act):
            a = nc.scalar
            own = Own(act, S["own_act"])
            act.sem_inc(S["ada_copied"], 1)
            act.sem_inc(S["z_copied"], 1)
            act.sem_inc(S["w_read"], 1)
            act.sem_inc(S["kt_act"], 1)
            act.sem_inc(S["y_read"], 2)
            for s in acc_free:
                act.sem_inc(s, 1)
            act.wait_ge(S["c_landed"], 32)
            a.activation(csil[:], crows[:], ACT.Sigmoid).then_inc(S["prep_act"], 1)
            for v in range(2):
                act.dma_start(a_raw[:, 0, v * GS:(v + 1) * GS], ssm_a_re[0]).then_inc(S["ssm_landed"], 16)
                act.dma_start(a_raw[:, 1, v * GS:(v + 1) * GS], ssm_a_im[0]).then_inc(S["ssm_landed"], 16)
            for v, (b, c) in enumerate(((ssm_b_re, ssm_c_re), (ssm_b_im, ssm_c_im), (ssm_b_re, ssm_c_re))):
                act.dma_start(b_raw[:, v, :], b[0].rearrange("g p n -> g (p n)")).then_inc(S["ssm_landed"], 16)
                act.dma_start(c_raw[:, :, v, :], c[0]).then_inc(S["ssm_landed"], 16)
            act.dma_start(log_dt[:], ssm_log_dt.to_broadcast([P, GROUPS])).then_inc(S["ssm_landed"], 16)
            act.dma_start(bias_h[:], sb_bias.to_broadcast([P, HEADS])).then_inc(S["bias_landed"], 16)
            act.dma_start(xrows[:, 0:2, :], x_prompt[0].rearrange("(t p) d -> p t d", p=P)).then_inc(S["x_landed"], 16)
            act.dma_start(xrows[0:SB * ST, 2, :], x_sample.rearrange("b t d -> (b t) d")).then_inc(S["x_landed"], 16)

            def split_high(n, cc, K, n4, buf=None, front=0):
                act.wait_ge(ring_landed[cc], n4 * 16 + 16)
                act.wait_ge(S["chunk_done"], n + 1 if buf is None else n)
                high = wH[cc % 2 if buf is None else buf]
                if front:
                    a.activation(high[:, 0:front, :], ring[cc][:, 0:front, :], ACT.Copy).then_inc(S["front_hi"], 1)
                a.activation(high[:, front:K, :], ring[cc][:, front:K, :], ACT.Copy).then_inc(S["hi_done"], 1)

            def split_ahead(i, n0, cc, next_ks, own_ks):
                c = cc + 2
                if c < 4:
                    split_high(i * 4 + (n0 + c), c, own_ks[c], i + n0 // 4)
                elif next_ks:
                    split_high(i * 4 + (n0 + c), c - 4, next_ks[c - 4], i + (n0 // 4 + 1))

            def start_stream(n0, ks):
                for c in range(2):
                    split_high(n0 + c, c, ks[c], n0 // 4)

            def wait_product(i, n0, cc):
                act.wait_ge(S["chunk_done"], i * 4 + (n0 + cc + 3))

            def copy_rows(n, block_no):
                act.wait_ge(S["chunk_done"], n + 3)
                act.wait_ge(S["ada_turned"], block_no + 1)
                a.activation(ada_rows[:], bank[2][0:2 * NC, :], ACT.Copy).then_inc(S["ada_copied"], 1)

            def ada_pass(i, last=False):
                for u in range(UNITS):
                    if u == UNITS - 1:
                        copy_rows(i * UNITS + u, i)
                    c = u + 2
                    if not (last and c >= UNITS):
                        split_high(i * UNITS + c, c % UNITS, KD, i + c // UNITS)

            start_stream(ADA1, [KD] * 2)
            with act.Fori(0, 2) as i:
                ada_pass(i)
            act.wait_ge(S["angle_ready"], 1)
            a.activation(small64[:, 6, :], small64[:, 4, :], ACT.Sin).then_inc(S["prep_act"], 1)
            a.activation(small64[:, 7, :], small64[:, 4, :], ACT.Sin, scale=0.5).then_inc(S["prep_act"], 1)
            with act.Fori(2, UNITS) as i:
                ada_pass(i)

            def ssm_pass(i, first=False, last=False):
                for u in range(UNITS):
                    if u == UNITS - 1:
                        copy_rows(i * UNITS + u, i)
                    c = u + 2
                    if not (last and c >= UNITS):
                        split_high(i * UNITS + c, c % UNITS, KD, i + c // UNITS)
                    if u % 2 == 0:
                        continue
                    b = i * 2 + (u // 2 - 2 * UNITS)
                    act.wait_ge(S["w_flipped"], b + 2)
                    if not (first and u == 1):
                        act.wait_ge(S["w1_stored"], b * 16)
                        act.wait_ge(S["taps_stored"], b * 16)
                    a.activation(w1s[:, 0:4, :].rearrange("p g m -> p (g m)"), bank[4][:], ACT.Copy)
                    a.activation(w1s[:, 4:8, :].rearrange("p g m -> p (g m)"), bank[5][:], ACT.Copy)
                    a.activation(o_s[:], bank[6][:, 0:P], ACT.Copy).then_inc(S["w_read"], 1)
                    act.wait_ge(S["w_read"], b + 2)
                    alone(act)
                    act.dma_start(w1_d[ds(b, 1)].rearrange("o p c -> (o p) c"), w1s[:].rearrange("p g m -> p (g m)")).then_inc(S["w1_stored"], 16)
                    act.dma_start(taps_d[0:P, ds(b * P, P)], o_s[:]).then_inc(S["taps_stored"], 16)

            ssm_pass(UNITS, first=True)
            with act.Fori(UNITS + 1, 2 * UNITS - 1) as i:
                ssm_pass(i)
            ssm_pass(2 * UNITS - 1, last=True)

            for x in range(2):
                split_high(PROJ + x, x, KD, PROJ // RING)
            for name in ("w1_stored", "taps_stored", "p_stored"):
                act.wait_ge(S[name], 16 * BATCHES)
            act.wait_ge(S["zeros_stored"], 16)
            split_high(PROJ + 2, 2, KD, PROJ // RING, 2, KD // 2)

            def proj_pass(i, last=False):
                for x, (kind, m) in enumerate(items):
                    n = i * ITEMS + (PROJ + x)
                    if kind == "chunk":
                        act.wait_ge(S["chunk_done"], n + 3)
                        a.activation(projT[:, ds(i * 4 + m, 1), :].rearrange("p o t -> p (o t)"),
                                     bank[m % 2][:, 0:T], ACT.Copy).then_inc(acc_free[m % 2], 1)
                    elif m % UNITS == UNITS - 1:
                        copy_rows(n, i * 2 + (2 * UNITS + m // UNITS))
                    y = x + 3
                    if not (last and y >= ITEMS):
                        split_high(n + 3, y % RING, KD, i * (ITEMS // RING) + (PROJ // RING + y // RING), y % 3, front_of(y))

            with act.Fori(0, KA - 1) as i:
                proj_pass(i)
            proj_pass(KA - 1, last=True)

            act.wait_ge(S["flips_read"], 4 + 8 + KD + 18)

            def attend(i, front=True, back=True):
                j = i - 1

                def read_page(p):
                    act.wait_ge(S["k_flipped"], i * PAGES + (p + KSLOTS + 1))
                    act.wait_ge(S["scored"], i * PAGES + (p + 1))
                    a.activation(kTp[p % 2][:, 4:8, :].rearrange("p h k -> p (h k)"), bank[1][:], ACT.Copy).then_inc(S["kt_act"], 1)

                def copy_scores(first):
                    act.wait_ge(S["scored"], i * PAGES + (first + 6))
                    act.wait_ge(S["z_turned"], i + 1)
                    a.activation(z_rows[:, first:first + 4, :].rearrange("p a k -> p (a k)"), bank[7][0:HQ, :], ACT.Copy).then_inc(S["z_copied"], 1)

                for p in range(PAGES):
                    if front:
                        read_page(p)
                    if front and p == 0:
                        act.wait_ge(S["zn_done"], i + 2)
                        act.wait_ge(S["z_turned"], i + 1)
                        a.activation(zn_rows[:], bank[6][0:HQ, 0:ST], ACT.Copy).then_inc(S["zn_copied"], 1)
                    if front and p == 4:
                        copy_scores(0)
                    if back and p == 1:
                        act.wait_ge(S["s_e_in"], j + 2)
                        own.mark(a.activation(se[:], se[:], ACT.Exp))
                        act.wait_ge(S["p_exp_in"], j + 1)
                        own.step(a.activation(pe_[:], pe_[:], ACT.Exp))
                        a.activation(pe_[:], pe_[:], ACT.Ln, bias=1.0).then_inc(S["p_ln"], 1)
                        a.activation(se[:], se[:], ACT.Ln, bias=1.0).then_inc(S["s_ln"], 1)
                    if back and p == 5:
                        act.wait_ge(S["p_arg"], j + 1)
                        a.activation(pe_[:], pe_[:], ACT.Exp).then_inc(S["p_w"], 1)
                        act.wait_ge(S["s_arg"], j + 1)
                        a.activation(se[:], se[:], ACT.Exp).then_inc(S["s_w"], 1)
                if back:
                    act.wait_ge(S["pv_rows"], j + 2)
                    a.activation(o_rows[:, 0:512], bank[5][0:ST, :], ACT.Copy).then_inc(S["o_act"], 1)
                if front:
                    copy_scores(4)

            attend(0, back=False)
            with act.Fori(1, SB) as i:
                own.begin(i, 2, first=1)
                attend(i)
                own.end(SB - 1)
            attend(SB, front=False)

            with act.Fori(0, BATCHES) as i:
                act.wait_ge(S["ug_flipped"], i + 3)
                a.activation(U[:, ds(i * GB, GB), :].rearrange("p g c -> p (g c)"), bank[4][:, 0:GB * CT], ACT.Copy).then_inc(S["u_ready"], 1)

            def read_y(i, e):
                act.wait_ge(S["y_done"], i * 2 + (e + 3))
                if not (isinstance(i, int) and i == 0):
                    act.wait_ge(y_stored[e], i * 16)
                alone(act)
                for g8 in range(GB):
                    last = a.activation(Yt[e][:, :, g8, :], bank[4 + 2 * e + g8 // 4][0:CT, (g8 % 4) * P:(g8 % 4 + 1) * P]
                                        .rearrange("c (s n) -> c s n", n=GC), ACT.Copy)
                last.then_inc(S["y_read"], 1)

            for e in range(2):
                read_y(0, e)
            with act.Fori(1, BATCHES // 2) as i:
                for e in range(2):
                    read_y(i, e)
            for c in range(KA):
                act.wait_ge(S["y_pre"], c + 1)
                if c >= 2:
                    act.wait_ge(S["y_ready"], c - 1)
                a.activation(ygl[c % 2][:], ypre[c % 2][:], ACT.Gelu_apprx_tanh).then_inc(S["y_gelu"], 1)

            start_stream(GLU, ks_of["glu"])

            def glu_pass(i, next_ks):
                for cc in range(4):
                    wait_product(i, GLU, cc)
                    m = i * 4 + cc
                    if m >= 2:
                        act.wait_ge(S["s_ready"], m - 1)
                    a.activation(gate[cc % 2][:], bank[cc % 2][:, 0:T], ACT.Sigmoid,
                                 bias=par[:, P + 120 + m:P + 121 + m]).then_inc(acc_free[cc % 2], 1)
                    split_ahead(i, GLU, cc, next_ks, ks_of["glu"])

            glu_pass(0, ks_of["glu"])
            glu_pass(1, None)

            def high_piece(i, x):
                i, x = i + x // 6, x % 6
                cc, k0, more = pieces_of_merge[x]
                act.wait_ge(ring_landed[cc], i * 16 + (MERGE // 4 * 16 + 16))
                if more:
                    act.wait_ge(S["half_done"], i * 2 + (cc // 2 + 1))
                else:
                    act.wait_ge(S["chunk_done"], i * 4 + (MERGE + cc + 1))
                a.activation(piece_buffers(x)[0], ring[cc][:, k0:k0 + KA, :], ACT.Copy).then_inc(S["half_hi" if more else "hi_done"], 1)

            act.wait_ge(S["chunk_done"], MERGE + 1)
            for x in range(3):
                high_piece(0, x)

            def merge_pass(i, next_ks):
                for x, (cc, _, more) in enumerate(pieces_of_merge):
                    if cc % 2 == 0 and not more:
                        wait_product(i, MERGE, cc)
                        act.wait_ge(acc_free[1], i * 2 + (nth_pair(MERGE) + cc // 2))
                        a.activation(gate[cc // 2][:], bank[0][:, 0:T], ACT.Sigmoid).then_inc(acc_free[0], 1)
                    if x < 3 or next_ks:
                        high_piece(i, x + 3)
                    elif x > 3:
                        split_high(OUT + x - 4, x - 4, KD, OUT // RING)

            act.wait_ge(S["s_ready"], KA)
            with act.Fori(0, KD - 1) as i:
                merge_pass(i, True)
            merge_pass(KD - 1, False)
            passes(act, "out", None, 0, lambda i, ks: [split_ahead(i, OUT, cc, ks, ks_of["out"]) for cc in range(4)])

            def layer_norm(nth, g0, b0):
                for k in range(KD):
                    act.wait_ge(S["centred"], KD * nth + k + 1)
                    a.activation(centred_sq[:, k, :], xT[:, k, :], ACT.Square).then_inc(S["squared"], 1)
                act.wait_ge(S["var_ready"], nth + 1)
                a.activation(sd[:], var[:], ACT.Sqrt).then_inc(S["sd_ready"], 1)

            def gain(k, nth, g0, b0, ready):
                act.wait_ge(S["scaled"], KD * nth + k + 1)
                a.activation(xT[:, k, :], xT[:, k, :], ACT.Identity, scale=par[:, g0 + k:g0 + k + 1],
                             bias=par[:, b0 + k:b0 + k + 1]).then_inc(ready, 1)

            layer_norm(0, 96, 112)
            for k in range(KD + 1):
                if k < KD:
                    gain(k, 0, 96, 112, S["gained"])
                if k >= 1:
                    act.wait_ge(S["modulated"], k)
                    a.activation(hH[:, k - 1, :], res[(k - 1) % 2][:], ACT.Copy).then_inc(S["h2_hi"], 1)
            conv = 0
            for q, nj in enumerate(QUARTERS):
                n0 = first_of[f"up{q}"]

                def up_pass(i, next_ks, n0=n0, conv=conv, q=q):
                    for cc in range(4):
                        wait_product(i, n0, cc)
                        act.wait_ge(S["halo"], i * 4 + (conv + cc + 1))
                        b = bank[cc % 2]
                        a.activation(ext[cc][:, 2:2 + NP], b[:, 0:NP], ACT.Copy).then_inc(S["conv_ev"], 1)
                        tail = ext[cc][:, NP + 2:EXT].rearrange("p (b t) -> p b t", b=SB)
                        a.activation(tail[:, :, 2:2 + ST], samples(b), ACT.Copy).then_inc(acc_free[cc % 2], 1)
                        split_ahead(i, n0, cc, next_ks, ks_of["up0"])
                        if cc % 2:
                            act.wait_ge(S["ext_read"], i * 4 + (conv + cc + 5))
                            a.activation(cvG[:, 0:EXT - 2], cvG[:, 0:EXT - 2], ACT.Gelu_apprx_tanh).then_inc(S["gelu_done"], 1)

                passes(act, f"up{q}", None, 0, up_pass)
                conv += 2 * nj
                n0 = first_of[f"down{q}"]
                passes(act, f"down{q}", None, 0,
                       lambda i, ks, n0=n0, q=q: [split_ahead(i, n0, cc, ks, ks_of[f"down{q}"]) for cc in range(4)])
            layer_norm(1, P + 88, P + 104)
            for k in range(KD):
                gain(k, 1, P + 88, P + 104, S["normed"])

        @block.vector
        def _(dve):
            v = nc.vector
            own = Own(dve, S["own_dve"])
            for name in ("ada_mod", "kt_dve", "s_e_in", "att_p", "att_s", "x_pre", "f_ready"):
                dve.sem_inc(S[name], 1)
            dve.sem_inc(S["split_done"], RING)
            dve.sem_inc(S["g_read"], 2)
            dve.sem_inc(S["ug_dve"], 2)
            dve.sem_inc(S["ext_read"], 4)
            MUL, ADD, SUB = ALU.mult, ALU.add, ALU.subtract
            flips = [0]

            def read_turns(turns):
                for sources, rows, dst in turns:
                    dve.wait_ge(S["flipped"], flips[0] + 1)
                    src = bank[4 + flips[0] % 4][0:rows, 0:width(sources)]
                    if len(dst.shape) == 3:
                        src = src.rearrange("p (a b) -> p a b", a=dst.shape[1])
                    v.tensor_copy(dst, src).then_inc(S["flips_read"], 1)
                    flips[0] += 1

            dve.wait_ge(S["prep_act"], 1)
            v.tensor_tensor(csil[:], csil[:], crows[:], MUL).then_inc(S["silu_ready"], 1)
            setup = list(setup_turns())
            read_turns(setup[0:1])
            dve.wait_ge(S["consts_ready"], 1)
            dve.wait_ge(S["flips_read"], 1)
            own.mark(v.tensor_tensor(add_up[:], ident[0:2 * NC, 0:NC], ident[0:2 * NC, NC:2 * NC], ADD))
            own.step(v.tensor_copy(cHL[:, :, 0:NC], cT[:]))
            v.tensor_tensor(cHL[:, :, NC:2 * NC], cT[:], cHL[:, :, 0:NC].bitcast(F32), SUB).then_inc(S["c_split"], 1)
            def split_low(n, cc, K, buf=None, front=0, nth_front=None):
                buf = cc % 2 if buf is None else buf
                if front:
                    dve.wait_ge(S["front_hi"], nth_front + 1)
                    v.tensor_tensor(wL[buf][:, 0:front, :], ring[cc][:, 0:front, :], wH[buf][:, 0:front, :].bitcast(F32), SUB)\
                        .then_inc(S["front_split"], 1)
                dve.wait_ge(S["hi_done"], n + 1)
                v.tensor_tensor(wL[buf][:, front:K, :], ring[cc][:, front:K, :], wH[buf][:, front:K, :].bitcast(F32), SUB)\
                    .then_inc(S["split_done"], 1)

            def ada_out(b):
                dve.wait_ge(S["ada_turned"], b + 2)
                n = BLOCK // P
                v.tensor_tensor(mod[:, ds(b * n, n), :], bank[3][:, 0:n * NC].rearrange("p (m c) -> p m c", c=NC),
                                par[:, ds(b * n, n)].unsqueeze(2).to_broadcast([P, n, NC]), ADD).then_inc(S["ada_mod"], 1)

            pieces = []
            for n in range(UNITS * UNITS + 2):
                pieces.append(lambda n=n: split_low(n, n % UNITS, KD))
                if n % UNITS == 1 and n > UNITS:
                    pieces.append(lambda b=n // UNITS - 1: ada_out(b))

            def piece(count=1):
                for _ in range(min(count, len(pieces))):
                    pieces.pop(0)()

            piece(UNITS + 2)
            read_turns(setup[1:12])
            dve.wait_ge(S["flips_read"], flips[0])
            steps = [0]

            def step(ins):
                own.mark(ins)
                steps[0] += 1
                if steps[0] % 8 == 0:
                    piece()
                own.settle()

            def s64(n):
                return small64[:, n, :]

            aR, aI, dt, expo, ang, mag, sn, shf, kk, rden, lb1, t0, t1_, fr, fi = (s64(n) for n in range(15))

            def exponential(out, x):
                step(v.tensor_scalar(kk, x, 1.0 / math.log(2.0), None, MUL))
                step(v.tensor_scalar(kk, kk, ROUND, None, ADD))
                step(v.tensor_scalar(kk, kk, ROUND, None, SUB))
                step(v.tensor_scalar(kk, kk, 127.0, -126.0, ALU.min, ALU.max))
                for c in LOG_2:
                    step(v.scalar_tensor_tensor(out=x, in0=kk, scalar=-c, in1=x, op0=MUL, op1=ADD))
                step(v.tensor_scalar(x, x, -1.0, 1.0, ALU.max, ALU.min))
                step(v.tensor_scalar(kk, kk, 127.0, 2.0 ** 23, ADD, MUL))
                step(v.tensor_copy(two_n[:], kk))
                step(v.tensor_scalar(out, x, 1.0 / math.factorial(8), 1.0 / math.factorial(7), MUL, ADD))
                for n in range(6, -1, -1):
                    step(v.tensor_tensor(out, out, x, MUL))
                    step(v.tensor_scalar(out, out, 1.0 / math.factorial(n), None, ADD))
                step(v.tensor_tensor(out, out, two_n[:].bitcast(F32), MUL))

            exponential(dt, log_dt[:])
            own.mark(v.tensor_tensor(expo, aR, dt, MUL))
            step(v.tensor_tensor(ang, aI, dt, MUL))
            step(v.tensor_scalar(kk, ang, 1.0 / (2.0 * math.pi), None, MUL))
            step(v.tensor_scalar(kk, kk, ROUND, None, ADD))
            step(v.tensor_scalar(kk, kk, ROUND, None, SUB))
            for c in TWO_PI:
                step(v.scalar_tensor_tensor(out=ang, in0=kk, scalar=-c, in1=ang, op0=MUL, op1=ADD))
            v.tensor_scalar(ang, ang, PI_IN, -PI_IN, ALU.min, ALU.max).then_inc(S["angle_ready"], 1)
            exponential(mag, expo)
            piece(len(pieces) - 10)
            dve.wait_ge(S["prep_act"], 3)
            pR, pI = pows
            own.mark(v.memset(pR[:, :, 0], 1.0))
            own.mark(v.memset(pI[:, :, 0], 0.0))
            step(v.tensor_tensor(pI[:, :, 1], mag, sn, MUL))
            step(v.tensor_tensor(t0, shf, shf, MUL))
            step(v.tensor_scalar(t0, t0, -2.0, 1.0, MUL, ADD))
            step(v.tensor_tensor(pR[:, :, 1], mag, t0, MUL))
            scratch = [VT[:].rearrange("p g m -> p (g m)")[:, 0:4 * GROUPS], VT[:].rearrange("p g m -> p (g m)")[:, 4 * GROUPS:8 * GROUPS]]
            for n in (1, 2, 4):
                x, y = (z[:, 0:n * GROUPS].rearrange("p (g j) -> p g j", j=n) for z in scratch)

                def top(t):
                    return t[:, :, n:n + 1].to_broadcast([P, GROUPS, n])

                own.mark(v.tensor_tensor(x, pR[:, :, 1:n + 1], top(pR), MUL))
                step(v.tensor_tensor(y, pI[:, :, 1:n + 1], top(pI), MUL))
                step(v.tensor_tensor(pR[:, :, n + 1:2 * n + 1], x, y, SUB))
                own.mark(v.tensor_tensor(x, pR[:, :, 1:n + 1], top(pI), MUL))
                step(v.tensor_tensor(y, pI[:, :, 1:n + 1], top(pR), MUL))
                step(v.tensor_tensor(pI[:, :, n + 1:2 * n + 1], x, y, ADD))
            for s in range(CHUNK):
                own.mark(v.tensor_copy(revs[0][:, :, s], pR[:, :, CHUNK - 1 - s]))
                own.mark(v.tensor_copy(revs[1][:, :, s], pI[:, :, CHUNK - 1 - s]))
            own.mark(v.tensor_copy(lam8[:, 0, :], pR[:, :, CHUNK]))
            own.mark(v.tensor_copy(lam8[:, 1, :], pI[:, :, CHUNK]))
            own.mark(v.tensor_scalar(lam8[:, 2, :], pI[:, :, CHUNK], -1.0, None, MUL))
            own.mark(v.tensor_scalar(lb1, pR[:, :, 1], -1.0, None, ADD))
            own.mark(v.tensor_tensor(t0, aR, aR, MUL))
            step(v.tensor_tensor(t1_, aI, aI, MUL))
            step(v.tensor_tensor(t0, t0, t1_, ADD))
            step(v.reciprocal(rden, t0))
            own.mark(v.tensor_tensor(t0, lb1, aR, MUL))
            step(v.tensor_tensor(t1_, pI[:, :, 1], aI, MUL))
            step(v.tensor_tensor(t0, t0, t1_, ADD))
            step(v.tensor_tensor(fr, t0, rden, MUL))
            own.mark(v.tensor_tensor(t0, pI[:, :, 1], aR, MUL))
            step(v.tensor_tensor(t1_, lb1, aI, MUL))
            step(v.tensor_tensor(t0, t0, t1_, SUB))
            step(v.tensor_tensor(fi, t0, rden, MUL))
            own.mark(v.tensor_scalar(b2[:], b2[:], sign[:, 1:2], None, MUL))
            own.mark(v.tensor_scalar(c1[:], c1[:], sign[:, 0:1], None, MUL))
            step(v.tensor_scalar(c2[:], c2[:], -1.0, None, MUL))

            def over_n(z):
                return z.unsqueeze(2).to_broadcast([P, GROUPS, GC])

            own.mark(v.tensor_tensor(bb1[:], b1[:], over_n(fr), MUL))
            step(v.tensor_tensor(bt[:], b2[:], over_n(fi), MUL))
            step(v.tensor_tensor(bb1[:], bb1[:], bt[:], ADD))
            own.mark(v.tensor_tensor(bb2[:], b2[:], over_n(fr), MUL))
            step(v.tensor_tensor(bt[:], b1[:], over_n(fi), MUL))
            v.tensor_tensor(bb2[:], bb2[:], bt[:], SUB).then_inc(S["prep_dve"], 1)
            dve.wait_ge(S["prep_dve"], 1)

            piece(len(pieces))
            read_turns(setup[12:])

            def state_weights(b):
                gs = ds(b * GB, GB)

                def blocks(z):
                    return z[:].rearrange("p g (s n) -> p g s n", n=GC)

                dve.wait_ge(S["w_flipped"], b + 1)
                for z, power, rows in ((V, revs[0], bb1), (VT, revs[1], bb2)):
                    ins = v.tensor_tensor(blocks(z), power[:, gs, :].unsqueeze(3).to_broadcast([P, GB, CHUNK, GC]),
                                          rows[:, gs, :].unsqueeze(2).to_broadcast([P, GB, CHUNK, GC]), MUL)
                    own.mark(ins)
                own.settle()
                v.tensor_tensor(V[:], V[:], VT[:], ADD).then_inc(S["v_ready"], 1)
                dve.wait_ge(S["v_ready"], b + 1)

            def ssm_pass(i, last=False):
                for u in range(UNITS):
                    c = u + 2
                    if not (last and c >= UNITS):
                        split_low(i * UNITS + c, c % UNITS, KD)
                    if u % 2 and not (last and u == UNITS - 1):
                        state_weights(i * 2 + (u // 2 + 1 - 2 * UNITS))
                ada_out(i)

            state_weights(0)
            with dve.Fori(UNITS, 2 * UNITS - 1) as i:
                own.begin(i, 4, first=UNITS)
                ssm_pass(i)
                own.end(UNITS - 1)
            ssm_pass(2 * UNITS - 1, last=True)

            def modulate(k, shift, scale, high, low, ready, tmp):
                own.mark(v.tensor_scalar(tmp[:, 0:NP], xT[:, k, 0:NP], mod[:, scale + k, 0:1], mod[:, shift + k, 0:1], MUL, ADD))
                own.step(v.tensor_tensor(samples(tmp), samples(xT[:, k, :]), per_sample(mod[:, scale + k, 1:NC]), MUL))
                own.step(v.tensor_tensor(samples(tmp), samples(tmp), per_sample(mod[:, shift + k, 1:NC]), ADD))
                own.step(v.tensor_copy(high[:, k, :], tmp))
                v.tensor_tensor(low[:, k, :], tmp, high[:, k, :].bitcast(F32), SUB).then_inc(ready, 1)

            SH1, SC1, G1, SH2, SC2, G2 = (m * KD for m in range(MODS))
            dve.wait_ge(S["ada_mod"], 1 + 2 * UNITS)
            own.step(v.tensor_scalar(mod[:, SC1:SC1 + KD, :], mod[:, SC1:SC1 + KD, :], 1.0, None, ADD))
            for k in range(KD):
                modulate(k, SH1, SC1, hH, hL, S["h_ready"], small64[:].rearrange("p a b -> p (a b)")[:, (k % 2) * T:(k % 2 + 1) * T])

            def split_ahead(i, n0, cc, next_ks, own_ks):
                c = cc + 2
                if c < 4:
                    split_low(i * 4 + (n0 + c), c, own_ks[c])
                elif next_ks:
                    split_low(i * 4 + (n0 + c), c - 4, next_ks[c - 4])

            def start_stream(n0, ks):
                for c in range(2):
                    split_low(n0 + c, c, ks[c])

            for x in range(3):
                split_low(PROJ + x, x, KD, x, front_of(x), 0)

            def proj_pass(i, last=False):
                for x, (kind, m) in enumerate(items):
                    y = x + 3
                    if not (last and y >= ITEMS):
                        split_low(i * ITEMS + (PROJ + y), y % RING, KD, y % 3, front_of(y), i * 4 + y // 3)
                    if kind == "chunk" and m % 2:
                        ada_out(i * 2 + (2 * UNITS + m // 2))

            with dve.Fori(0, KA - 1) as i:
                proj_pass(i)
            proj_pass(KA - 1, last=True)
            dve.wait_ge(S["ada_mod"], 1 + MODS * UNITS)
            own.mark(v.tensor_scalar(mod[:, G1:G1 + KD, :], mod[:, G1:G1 + KD, :], 1.0, None, ADD))
            own.step(v.tensor_scalar(mod[:, SC2:, :], mod[:, SC2:, :], 1.0, None, ADD))
            f = flips[0]
            read_turns(proj_turns())

            dve.wait_ge(S["u_stored"], 32)
            dve.wait_ge(S["bias_landed"], 16)
            dve.wait_ge(S["bias_spread"], 1)
            new = sS[0:ST, PAGES, :]

            def attend(i, front=True, back=True):
                j = i - 1

                def read_page(p):
                    dve.wait_ge(S["k_flipped"], i * PAGES + (p + KSLOTS + 1))
                    dve.wait_ge(S["scored"], i * PAGES + (p + 1))
                    v.tensor_copy(kTp[p % 2][:, 0:4, :].rearrange("p h k -> p (h k)"), bank[0][:]).then_inc(S["kt_dve"], 1)

                def scores():
                    dve.wait_ge(S["z_turned"], j + 2)
                    own.mark(v.scalar_tensor_tensor(out=sz[:, 0:PAGES, :], in0=bank[2][:].rearrange("p (a c) -> p a c", a=PAGES), scalar=SCALE,
                                                    in1=bias_q[:].unsqueeze(1).to_broadcast([P, PAGES, HQ]), op0=MUL, op1=ADD))
                    own.step(v.scalar_tensor_tensor(out=sz[0:ST, PAGES, :], in0=bank[3][0:ST, 0:HQ], scalar=SCALE, in1=bias_q[0:ST, :], op0=MUL, op1=ADD))
                    v.scalar_tensor_tensor(out=se[:], in0=sz[:], scalar=-1.0, in1=sz[:], op0=MUL, op1=ALU.min).then_inc(S["s_e_in"], 1)

                def head_scores():
                    dve.wait_ge(S["pz_done"], j + 1)
                    own.step(v.tensor_scalar(pz[:], bank[4][:, 0:384], SCALE, bias_h[:, ds(j, 1)], MUL, ADD))
                    v.scalar_tensor_tensor(out=pe_[:], in0=pz[:], scalar=-1.0, in1=pz[:], op0=MUL, op1=ALU.min).then_inc(S["p_exp_in"], 1)

                def softplus():
                    dve.wait_ge(S["s_ln"], j + 1)
                    own.mark(v.scalar_tensor_tensor(out=sS[:], in0=sz[:], scalar=0.0, in1=se[:], op0=ALU.max, op1=ADD))
                    dve.wait_ge(S["p_ln"], j + 1)
                    own.step(v.scalar_tensor_tensor(out=pS[:], in0=pz[:], scalar=0.0, in1=pe_[:], op0=ALU.max, op1=ADD))
                    v.scalar_tensor_tensor(out=new, in0=mask_new[:], scalar=1.0, in1=new, op0=ADD, op1=MUL).then_inc(S["s_s"], 1)
                    v.scalar_tensor_tensor(out=pS[:], in0=masks[:], scalar=1.0, in1=pS[:], op0=ADD, op1=MUL).then_inc(S["p_s"], 1)

                def log_weights():
                    dve.wait_ge(S["p_cs"], j + 1)
                    own.step(v.tensor_tensor(pz[:], pz[:], bank[4][:, 0:384], SUB))
                    v.scalar_tensor_tensor(out=pe_[:], in0=masks[:], scalar=1e30, in1=pz[:], op0=MUL, op1=ADD).then_inc(S["p_arg"], 1)
                    dve.wait_ge(S["s_cs"], j + 1)
                    own.mark(v.tensor_tensor(se[:, 0:PAGES, :], sz[:, 0:PAGES, :], bank[3][:].rearrange("p (a c) -> p a c", a=PAGES), SUB))
                    own.step(v.tensor_tensor(sz[0:ST, PAGES, :], sz[0:ST, PAGES, :], bank[4][0:ST, 384:384 + HQ], SUB))
                    v.scalar_tensor_tensor(out=se[0:ST, PAGES, :], in0=mask_new[:], scalar=1e30, in1=sz[0:ST, PAGES, :], op0=MUL, op1=ADD)\
                        .then_inc(S["s_arg"], 1)

                def outputs():
                    dve.wait_ge(S["p_pv"], j + 2)
                    o = bank[4][:, 0:NP].unsqueeze(1)
                    own.step(v.tensor_copy(attH[:, ds(j, 1), 0:NP], o))
                    v.tensor_tensor(attL[:, ds(j, 1), 0:NP], o, attH[:, ds(j, 1), 0:NP].bitcast(F32), SUB).then_inc(S["att_p"], 1)
                    dve.wait_ge(S["pv_rows"], j + 2)
                    v.tensor_copy(o_rows[:, 512:], bank[6][0:ST, :]).then_inc(S["o_dve"], 1)
                    dve.wait_ge(S["s_pv"], j + 2)
                    o = bank[4][:, 512 - HQ:].rearrange("p (h q) -> p h q", q=ST)
                    cols = ds(j * ST + NP, ST)
                    own.step(v.tensor_copy(attH[:, :, cols], o))
                    v.tensor_tensor(attL[:, :, cols], o, attH[:, :, cols].bitcast(F32), SUB).then_inc(S["att_s"], 1)

                steps = {0: scores, 3: softplus, 5: log_weights} if back else {}
                for p in range(PAGES):
                    if p in steps:
                        steps[p]()
                    if front:
                        read_page(p)
                    if back and p == 0:
                        head_scores()
                if back:
                    outputs()

            attend(0, back=False)
            with dve.Fori(1, SB) as i:
                own.begin(i, 10, first=1)
                attend(i)
                own.end(SB - 1)
            attend(SB, front=False)

            def gather(i, e):
                dve.wait_ge(uraw_landed[e], i * 16 + 16)
                dve.wait_ge(S["ug_flipped"], i * 2 + (e + 1))
                for gg in range(POOL_GROUPS, GB):
                    last = v.tensor_copy(Ug[e][:, gg, :].rearrange("c (s n) -> c s n", n=GC), Uraw[e][:, :, gg * GC:(gg + 1) * GC])
                last.then_inc(S["ug_dve"], 1)

            def read_in(i, more=True):
                for e in range(2):
                    if more:
                        gather(i + 1, e)
                    dve.wait_ge(S["g_done"], i * 2 + (e + 3))
                    v.tensor_copy(G[:, 0, ds(i * (2 * GB) + e * GB, GB), :], bank[5 + e][:, 0:GB * CT].rearrange("p (g c) -> p g c", g=GB)).then_inc(S["g_read"], 1)

            for e in range(2):
                gather(0, e)
            with dve.Fori(0, BATCHES // 2 - 1) as i:
                read_in(i)
            read_in(BATCHES // 2 - 1, more=False)
            for n in range(GROUPS * CT // 512):
                dve.wait_ge(S["g_done"], BATCHES + n + 3)
                v.tensor_copy(G[:, 1].rearrange("p g c -> p (g c)")[:, n * 512:(n + 1) * 512], bank[n % 2][:]).then_inc(S["g_swapped"], 1)
            dve.wait_ge(S["g_swapped"], GROUPS * CT // 512)
            own.step(v.memset(Z[:, :, :, 0], 0.0))
            read_turns(state_turns())
            dve.wait_ge(S["flips_read"], flips[0])
            own.step(v.tensor_scalar(h0[:, 1], h0[:, 1], sign[:, 1:2], None, MUL))
            l_re, l_im, l_neg = (lam8[:, n, :] for n in range(3))
            even = slice(0, CP, 2)

            def times_lam8(z, half):
                def over(l):
                    return l.unsqueeze(2).to_broadcast([P, GROUPS, CP // 2])

                own.mark(v.tensor_tensor(wide1[:], z[half], over(l_re), MUL))
                own.step(v.tensor_tensor(wide2[:], z[1 - half], over(l_neg if half else l_im), MUL))
                own.step(v.tensor_tensor(wide1[:], wide1[:], wide2[:], ADD))

            own.mark(v.tensor_tensor(lam16[:, 0, :], l_re, l_re, MUL))
            own.mark(v.tensor_tensor(lam16[:, 2, :], l_im, l_im, MUL))
            own.step(v.tensor_tensor(lam16[:, 1, :], l_re, l_im, MUL))
            own.mark(v.tensor_tensor(lam16[:, 0, :], lam16[:, 0, :], lam16[:, 2, :], SUB))
            own.step(v.tensor_scalar(lam16[:, 1, :], lam16[:, 1, :], 2.0, None, MUL))
            own.step(v.tensor_scalar(lam16[:, 2, :], lam16[:, 1, :], -1.0, None, MUL))
            for half in range(2):
                times_lam8([G[:, h, :, even] for h in range(2)], half)
                odd = G[:, half, :, 1:CP:2]
                own.step(v.tensor_tensor(odd, odd, wide1[:], ADD))
            with dve.Fori(0, CP // 8) as c:
                own.begin(c, 4 * 4)
                for n in range(4):
                    def state(half):
                        return Z[:, half, :, ds(c * 8 + 2 * n, 1)].rearrange("p g o -> p (g o)")

                    own.mark(v.tensor_tensor(t1[:], Z[:, :, :, ds(c * 8 + 2 * n, 1)].rearrange("p v g o -> p v (g o)"),
                                             lam16[:, 0, :].unsqueeze(1).to_broadcast([P, 2, GROUPS]), MUL))
                    for half in range(2):
                        own.mark(v.tensor_tensor(t2[:, half, :], state(1 - half), lam16[:, 1 + half, :], MUL))
                    own.settle()
                    own.step(v.tensor_tensor(t1[:], t1[:], t2[:], ADD))
                    v.tensor_tensor(Z[:, :, :, ds(c * 8 + (2 * n + 2), 1)].rearrange("p v g o -> p v (g o)"), t1[:],
                                    G[:, :, :, ds(c * 8 + (2 * n + 1), 1)].rearrange("p v g o -> p v (g o)"), ADD).then_inc(S["state_step"], 1)
                    dve.wait_ge(S["state_step"], c * 4 + (n + 1))
                own.end(CP // 8)
            times_lam8([Z[:, h, :, even] for h in range(2)], 0)
            own.step(v.tensor_tensor(Z[:, 0, :, 1:CP:2], G[:, 0, :, even], wide1[:], ADD))

            def over_b(z):
                return z.unsqueeze(2).to_broadcast([P, GROUPS, SB])

            own.mark(v.tensor_copy(Z[:, 0, :, CP + 1:], h0[:, 0]))
            own.mark(v.tensor_tensor(zf[:], h0[:, 0], over_b(l_re), MUL))
            own.step(v.tensor_tensor(u1[:], h0[:, 1], over_b(l_im), MUL))
            own.step(v.tensor_tensor(zf[:], zf[:], u1[:], ADD))
            v.tensor_tensor(zf[:], zf[:], G[:, 0, :, CP:], ADD).then_inc(S["scanned"], 1)
            read_turns(final_state_turns())
            for c in range(KA):
                dve.wait_ge(S["ytk_turned"], c + 1)
                if c >= 2:
                    dve.wait_ge(S["y_gelu"], c - 1)
                v.scalar_tensor_tensor(out=ypre[c % 2][:], in0=projT[:, c, :], scalar=cw[:, 3 * 2 * JF + c:3 * 2 * JF + c + 1],
                                       in1=bank[4 + c % 4][:, 0:T], op0=MUL, op1=ADD).then_inc(S["y_pre"], 1)
                if c >= 1:
                    dve.wait_ge(S["y_gelu"], c)
                    own.step(v.tensor_copy(ygH[:, c - 1, :], ygl[(c - 1) % 2][:]))
                    v.tensor_tensor(ygL[:, c - 1, :], ygl[(c - 1) % 2][:], ygH[:, c - 1, :].bitcast(F32), SUB).then_inc(S["y_ready"], 1)
            c = KA
            dve.wait_ge(S["y_gelu"], c)
            own.step(v.tensor_copy(ygH[:, c - 1, :], ygl[(c - 1) % 2][:]))
            v.tensor_tensor(ygL[:, c - 1, :], ygl[(c - 1) % 2][:], ygH[:, c - 1, :].bitcast(F32), SUB).then_inc(S["y_ready"], 1)

            start_stream(GLU, ks_of["glu"])
            for m in range(KA):
                i, cc = m // 4, m % 4
                dve.wait_ge(S["y_ready"], KA)
                dve.wait_ge(acc_free[cc % 2], nth_pair(GLU + m) + 2)
                dve.wait_ge(S["s_ready"], m)
                own.step(v.tensor_tensor(part[0][:], ygH[:, m, :].bitcast(F32), ygL[:, m, :].bitcast(F32), ADD))
                own.step(v.tensor_tensor(part[0][:], part[0][:], gate[cc % 2][:], MUL))
                own.step(v.tensor_copy(sH[:, m, :], part[0][:]))
                v.tensor_tensor(sL[:, m, :], part[0][:], sH[:, m, :].bitcast(F32), SUB).then_inc(S["s_ready"], 1)
                split_ahead(i, GLU, cc, ks_of["glu"] if i == 0 else None, ks_of["glu"])

            def low_piece(i, x):
                i, x = i + x // 6, x % 6
                cc, k0, more = pieces_of_merge[x]
                high, low = piece_buffers(x)
                dve.wait_ge(S["half_hi" if more else "hi_done"], i * 2 + (cc // 2 + 1) if more else i * 4 + (MERGE + cc + 1))
                v.tensor_tensor(low, ring[cc][:, k0:k0 + KA, :], high.bitcast(F32), SUB).then_inc(S["half_split" if more else "split_done"], 1)

            for x in range(3):
                low_piece(0, x)

            def merge_pass(i, more):
                for x, (cc, _, _) in enumerate(pieces_of_merge):
                    if cc % 2:
                        h = cc // 2
                        dve.wait_ge(acc_free[0], i * 2 + (nth_pair(MERGE) + h + 2))
                        dve.wait_ge(S["chunk_done"], i * 4 + (MERGE + cc + 3))
                        v.tensor_tensor(part[h][:], bank[1][:, 0:T], gate[h][:], MUL).then_inc(acc_free[1], 1)
                    if cc == 3:
                        dve.wait_ge(acc_free[1], i * 2 + (nth_pair(MERGE) + 3))
                        v.tensor_tensor(merged[:, ds(i, 1), :].rearrange("p o t -> p (o t)"), part[0][:], part[1][:], ADD).then_inc(S["merged_ready"], 1)
                    if x < 3 or more:
                        low_piece(i, x + 3)
                    elif x > 3:
                        split_low(OUT + x - 4, x - 4, KD)

            with dve.Fori(0, KD - 1) as i:
                merge_pass(i, True)
            merge_pass(KD - 1, False)
            dve.wait_ge(S["merged_ready"], KD)
            dve.wait_ge(S["chunk_done"], OUT + 2)
            for k in range(KD):
                own.step(v.tensor_copy(mH[:, k, :], merged[:, k, :]))
                v.tensor_tensor(mL[:, k, :], merged[:, k, :], mH[:, k, :].bitcast(F32), SUB).then_inc(S["m_ready"], 1)

            def residual(src, m, gain, ready, free=None, r=res[0]):
                col = mod[:, ds(m + gain, 1), :].rearrange("p o c -> p (o c)")
                own.mark(v.tensor_scalar(r[:, 0:NP], src[:, 0:NP], col[:, 0:1], None, MUL))
                ins = v.tensor_tensor(samples(r[:]), samples(src), per_sample(col[:, 1:NC]), MUL)
                if free:
                    ins.then_inc(free[0], 1)
                    own.settle()
                    dve.wait_ge(free[0], free[1])
                else:
                    own.step(ins)
                x = xT[:, ds(m, 1), :].rearrange("p o t -> p (o t)")
                v.scalar_tensor_tensor(out=x, in0=x, scalar=ALPHA, in1=r[:], op0=MUL, op1=ADD).then_inc(ready, 1)

            def out_pass(i, next_ks):
                for cc in range(4):
                    dve.wait_ge(S["chunk_done"], i * 4 + (OUT + cc + 3))
                    dve.wait_ge(S["x_pre"], i * 4 + (cc + 1))
                    residual(bank[cc % 2][:, 0:T], i * 4 + cc, G1, S["x_pre"], (acc_free[cc % 2], i * 2 + (nth_pair(OUT) + cc // 2 + 2)))
                    split_ahead(i, OUT, cc, next_ks, ks_of["out"])

            passes(dve, "out", own, 4, out_pass)

            def layer_norm(nth):
                dve.wait_ge(S["mean_done"], nth + 1)
                own.step(v.tensor_copy(mu[:], bank[2][:, 0:T]))
                for k in range(KD):
                    v.tensor_tensor(xT[:, k, :], xT[:, k, :], mu[:], SUB).then_inc(S["centred"], 1)
                dve.wait_ge(S["var_done"], nth + 1)
                v.tensor_scalar(var[:], bank[3][:, 0:T], EPS, None, ADD).then_inc(S["var_ready"], 1)
                dve.wait_ge(S["sd_ready"], nth + 1)
                own.step(v.reciprocal(rstd[:], sd[:]))
                own.step(v.tensor_tensor(newton[:], rstd[:], rstd[:], MUL))
                own.step(v.tensor_tensor(newton[:], newton[:], var[:], MUL))
                own.step(v.tensor_scalar(newton[:], newton[:], -0.5, 1.5, MUL, ADD))
                v.tensor_tensor(rstd[:], rstd[:], newton[:], MUL).then_inc(S["rstd_ready"], 1)

            dve.wait_ge(S["state_stored"], 64)
            read_turns(conv_state_turns())
            layer_norm(0)
            for k in range(KD + 1):
                if k < KD:
                    dve.wait_ge(S["gained"], k + 1)
                    tmp = res[k % 2]
                    own.mark(v.tensor_scalar(tmp[:, 0:NP], xT[:, k, 0:NP], mod[:, SC2 + k, 0:1], mod[:, SH2 + k, 0:1], MUL, ADD))
                    own.step(v.tensor_tensor(samples(tmp), samples(xT[:, k, :]), per_sample(mod[:, SC2 + k, 1:NC]), MUL))
                    v.tensor_tensor(samples(tmp), samples(tmp), per_sample(mod[:, SH2 + k, 1:NC]), ADD).then_inc(S["modulated"], 1)
                if k >= 1:
                    dve.wait_ge(S["h2_hi"], k)
                    v.tensor_tensor(hL[:, k - 1, :], res[(k - 1) % 2][:], hH[:, k - 1, :].bitcast(F32), SUB).then_inc(S["h2_ready"], 1)
                    dve.wait_ge(S["h2_ready"], k)

            done, pairs = 0, 0
            j0 = 0
            for q, nj in enumerate(QUARTERS):
                n0 = first_of[f"up{q}"]

                def up_pass(i, next_ks):
                    for cc in range(4):
                        split_ahead(i, n0, cc, next_ks, ks_of["up0"])
                        n = i * 4 + (done + cc)
                        ch = i * 2 + (j0 + cc // 2 + (cc % 2) * JF)
                        dst = cvG if cc % 2 else cvV
                        dve.wait_ge(S["halo"], n + 1)
                        dve.wait_ge(S["conv_ev"], n + 1)
                        dve.wait_ge(acc_free[cc % 2], i * 2 + (nth_pair(n0) + cc // 2 + 2))
                        e = ext[cc]
                        own.step(v.tensor_scalar(dst[:, 0:EXT - 2], e[:, 0:EXT - 2], cw[:, ds(ch, 1)], par[:, ds(ch + P, 1)], MUL, ADD))
                        own.step(v.scalar_tensor_tensor(out=dst[:, 0:EXT - 2], in0=e[:, 1:EXT - 1], scalar=cw[:, ds(ch + 2 * JF, 1)], in1=dst[:, 0:EXT - 2], op0=MUL, op1=ADD))
                        v.scalar_tensor_tensor(out=dst[:, 0:EXT - 2], in0=e[:, 2:EXT], scalar=cw[:, ds(ch + 4 * JF, 1)],
                                               in1=dst[:, 0:EXT - 2], op0=MUL, op1=ADD).then_inc(S["ext_read"], 1)
                        dve.wait_ge(S["ext_read"], n + 5)
                        if cc % 2:
                            j = i * 2 + cc // 2
                            dve.wait_ge(S["gelu_done"], i * 2 + (pairs + cc // 2 + 1))
                            dve.wait_ge(S["f_ready"], i * 2 + (pairs + cc // 2 + 1))
                            own.mark(v.tensor_tensor(prod[:, 0:NP], cvV[:, 0:NP], cvG[:, 0:NP], MUL))
                            own.step(v.tensor_tensor(samples(prod[:]), late(cvV), late(cvG), MUL))
                            own.step(v.tensor_copy(fH[:, ds(j, 1), :], prod[:].unsqueeze(1)))
                            v.tensor_tensor(fL[:, ds(j, 1), :], prod[:].unsqueeze(1), fH[:, ds(j, 1), :].bitcast(F32), SUB).then_inc(S["f_ready"], 1)

                passes(dve, f"up{q}", own, 14, up_pass)
                done += 2 * nj
                pairs += nj
                n0 = first_of[f"down{q}"]

                def down_pass(i, next_ks):
                    for cc in range(4):
                        dve.wait_ge(S["chunk_done"], i * 4 + (n0 + cc + 3))
                        y = yacc[:, ds(i * 4 + cc, 1), :].rearrange("p o t -> p (o t)")
                        acc = bank[cc % 2][:, 0:T]
                        ins = v.tensor_tensor(y, y, acc, ADD) if q else v.tensor_copy(y, acc)
                        ins.then_inc(acc_free[cc % 2], 1)
                        split_ahead(i, n0, cc, next_ks, ks_of[f"down{q}"])
                        if q == len(QUARTERS) - 1:
                            dve.wait_ge(acc_free[cc % 2], i * 2 + (nth_pair(n0) + cc // 2 + 2))
                            residual(y, i * 4 + cc, G2, S["x_pre"], r=res[1])
                            dve.wait_ge(S["x_pre"], i * 4 + (KD + cc + 2))

                passes(dve, f"down{q}", own, 8 if q == len(QUARTERS) - 1 else 0, down_pass)
                j0 += nj
            read_turns(rows_out_turns())
            layer_norm(1)
            read_turns(y_turns())


_INS = ["x_prompt", "x_sample", "cache_k", "cache_v", "state_ssm_re", "state_ssm_im", "state_conv", "page_table",
        "c_prompt", "c_sample", "w_ada", "b_ada", "w_in", "w_att_br", "w_ssm_br", "w_out", "sb_bias",
        "ssm_a_re", "ssm_a_im", "ssm_log_dt", "ssm_b_re", "ssm_b_im", "ssm_c_re", "ssm_c_im", "ssm_d",
        "w_glu", "b_glu", "ln1_g", "ln1_b", "w_up", "conv_w", "conv_b", "w_down", "ln2_g", "ln2_b"]
_OUTS = [(1, NP, D), (SB, ST, D), (1, 1, NP, HEADS, HD), (1, 1, NP, HEADS, HD), (1, 1, GROUPS, GS), (1, 1, GROUPS, GS),
         (1, 1, 2, 2 * FF), (1, SB, ST, HEADS, HD), (1, SB, ST, HEADS, HD), (1, SB, GROUPS, GS), (1, SB, GROUPS, GS),
         (1, SB, 2, 2 * FF)]


def kernel(**inputs):
    import numpy as np
    import concourse.bacc as bacc
    from concourse.bass_utils import run_bass_kernel_spmd

    nc = bacc.Bacc("TRN2", target_bir_lowering=False, num_devices=1)
    arrays, args = {}, []
    for name in _INS:
        a = np.ascontiguousarray(inputs[name])
        arrays[f"in_{name}"] = a
        args.append(nc.dram_tensor(f"in_{name}", a.shape, mybir.dt.from_np(a.dtype), kind="ExternalInput").ap())
    for i, shape in enumerate(_OUTS):
        args.append(nc.dram_tensor(f"out_{i}", shape, F32, kind="ExternalOutput").ap())
    hybrid_step(nc, *args)
    r = run_bass_kernel_spmd(nc, [arrays], core_ids=[0])
    return tuple(r.results[0][f"out_{i}"] for i in range(len(_OUTS)))
```
